# Optimizing a Trainium2 kernel written in Bass

```python
import math
import jax, jax.numpy as jnp
from jax import lax
import numpy as np

D_MODEL = 1024
BATCH = 1
SEQ = 256
DEPTH = 1

D_MIX = D_MODEL
D_MLSTM = D_MIX // 2
D_DIFF = D_MIX - D_MLSTM
ML_HEADS = 4
ML_HD = D_MLSTM // ML_HEADS
CONV_W = 4
CHUNK = 128
DA_HEADS = 4
DA_VD = D_DIFF // DA_HEADS
DA_QD = DA_VD // 2
Q_BLOCK = 128
REL_BUCKETS = 32
REL_MAX_DIST = 128
N_GROUPS = 4
EXP_PER_GROUP = 8
N_EXPERTS = N_GROUPS * EXP_PER_GROUP
TOP_K_FINE = 2
D_FF_EXP = 512
EPS = 1e-6
SUBLN_EPS = 1e-5
IN_COLS = 3 * D_MLSTM + 3 * D_DIFF


def rmsnorm(x, g, eps=EPS):
    xf = x.astype(jnp.float32)
    y = xf * lax.rsqrt(jnp.mean(xf * xf, axis=-1, keepdims=True) + eps)
    return (y * g.astype(jnp.float32)).astype(x.dtype)

def head_layernorm(h, g):
    mu = jnp.mean(h, axis=-1, keepdims=True)
    var = jnp.mean(jnp.square(h - mu), axis=-1, keepdims=True)
    return (h - mu) * lax.rsqrt(var + EPS) * g.astype(jnp.float32)

def causal_conv(x, w, b):
    c = x.shape[-1]
    y = lax.conv_general_dilated(x, w[:, None, :].astype(x.dtype), window_strides=(1,),
                                 padding=[(CONV_W - 1, 0)],
                                 dimension_numbers=('NWC', 'WIO', 'NWC'),
                                 feature_group_count=c)
    return y + b.astype(x.dtype)

def mlstm_chunkwise(q, k, v, i_pre, logf):
    bsz, s, nh, d = q.shape
    nc = s // CHUNK
    def chunks(t):
        return t.reshape(bsz, nc, CHUNK, nh, d).transpose(1, 0, 3, 2, 4)
    def gchunks(t):
        return t.reshape(bsz, nc, CHUNK, nh).transpose(1, 0, 3, 2)
    tril = jnp.tril(jnp.ones((CHUNK, CHUNK), dtype=bool))

    def step(carry, xs):
        cmat, nvec, m = carry
        qc, kc, vc, ic, fc = xs
        b = jnp.cumsum(fc, axis=-1)
        inter = b + m[..., None]
        dmat = jnp.where(tril, b[..., :, None] - b[..., None, :] + ic[..., None, :], -jnp.inf)
        m_t = jnp.maximum(inter, jnp.max(dmat, axis=-1))
        w = jnp.exp(dmat - m_t[..., None]) * jnp.einsum('bhtd,bhsd->bhts', qc, kc)
        sp = jnp.exp(inter - m_t)
        num = sp[..., None] * jnp.einsum('bhtk,bhvk->bhtv', qc, cmat) + jnp.einsum('bhts,bhsv->bhtv', w, vc)
        den = sp * jnp.einsum('bhtk,bhk->bht', qc, nvec) + jnp.sum(w, axis=-1)
        h = num / jnp.maximum(jnp.abs(den), jnp.exp(-m_t))[..., None]
        b_end = b[..., -1]
        g = b_end[..., None] - b + ic
        m_new = jnp.maximum(b_end + m, jnp.max(g, axis=-1))
        wk = jnp.exp(g - m_new[..., None])
        decay = jnp.exp(b_end + m - m_new)
        c_new = decay[..., None, None] * cmat + jnp.einsum('bhs,bhsv,bhsk->bhvk', wk, vc, kc)
        n_new = decay[..., None] * nvec + jnp.einsum('bhs,bhsk->bhk', wk, kc)
        return (c_new, n_new, m_new), h

    init = (jnp.zeros((bsz, nh, d, d), jnp.float32), jnp.zeros((bsz, nh, d), jnp.float32),
            jnp.zeros((bsz, nh), jnp.float32))
    _, hs = lax.scan(step, init, (chunks(q), chunks(k), chunks(v), gchunks(i_pre), gchunks(logf)))
    return hs.transpose(1, 0, 3, 2, 4).reshape(bsz, s, nh, d)

def mlstm_group(c, v, z, conv_w, conv_b, w_mq, w_mk, w_mgate, b_mgate, m_norm_g, m_skip):
    bsz, s, _ = c.shape
    c_act = jax.nn.silu(causal_conv(c, conv_w, conv_b))
    ch = c_act.reshape(bsz, s, ML_HEADS, ML_HD)
    q = jnp.einsum('bshd,hde->bshe', ch, w_mq)
    k = jnp.einsum('bshd,hde->bshe', ch, w_mk)
    vh = v.reshape(bsz, s, ML_HEADS, ML_HD)
    gin = jnp.concatenate([q.reshape(bsz, s, -1), k.reshape(bsz, s, -1), v], axis=-1)
    gates = (gin @ w_mgate).astype(jnp.float32) + b_mgate.astype(jnp.float32)
    i_pre = gates[..., :ML_HEADS]
    logf = jax.nn.log_sigmoid(gates[..., ML_HEADS:])
    h = mlstm_chunkwise(q.astype(jnp.float32), (k * (ML_HD ** -0.5)).astype(jnp.float32),
                        vh.astype(jnp.float32), i_pre, logf)
    h = head_layernorm(h, m_norm_g.reshape(ML_HEADS, ML_HD)).reshape(bsz, s, D_MLSTM)
    h = h + m_skip.astype(jnp.float32) * c_act.astype(jnp.float32)
    o = jax.nn.sigmoid(z.astype(jnp.float32))
    return (o * h).astype(c.dtype)

def rel_bucket(qpos, kpos):
    n = jnp.maximum(qpos[:, None] - kpos[None, :], 0)
    max_exact = REL_BUCKETS // 2
    large = max_exact + (jnp.log(jnp.maximum(n, 1).astype(jnp.float32) / max_exact)
                         / math.log(REL_MAX_DIST / max_exact) * (REL_BUCKETS - max_exact)).astype(jnp.int32)
    large = jnp.minimum(large, REL_BUCKETS - 1)
    return jnp.where(n < max_exact, n, large)

def diff_attention(q, k, v, lam, rel_bias):
    bsz, s = q.shape[0], q.shape[1]
    nb = s // Q_BLOCK
    scale = DA_QD ** -0.5
    qb = jnp.moveaxis(q.reshape(bsz, nb, Q_BLOCK, DA_HEADS, 2, DA_QD), 1, 0)
    kpos = jnp.arange(s)

    def block(args):
        q_blk, bi = args
        qpos = bi * Q_BLOCK + jnp.arange(Q_BLOCK)
        bias = rel_bias[rel_bucket(qpos, kpos)].transpose(2, 0, 1).astype(jnp.float32)
        mask = kpos[None, :] <= qpos[:, None]
        logits = jnp.einsum('bqhcd,bkhcd->bchqk', q_blk, k).astype(jnp.float32) * scale + bias[None, None]
        p = jax.nn.softmax(jnp.where(mask, logits, -jnp.inf), axis=-1)
        a = p[:, 0] - lam * p[:, 1]
        return jnp.einsum('bhqk,bkhd->bqhd', a.astype(v.dtype), v)

    out = lax.map(block, (qb, jnp.arange(nb)))
    return jnp.moveaxis(out, 0, 1).reshape(bsz, s, DA_HEADS, DA_VD)

def hier_moe(h, w_rg, b_rg, w_re, b_re, w_eg, w_eu, w_ed):
    bsz, s, d = h.shape
    t = h.reshape(-1, d)
    lg = (t @ w_rg).astype(jnp.float32) + b_rg.astype(jnp.float32)
    pg = jax.nn.softmax(lg, axis=-1)
    _, g_idx = lax.top_k(lg, 1)
    pg_sel = jnp.take_along_axis(pg, g_idx, axis=-1)
    le = jnp.einsum('nd,dge->nge', t, w_re).astype(jnp.float32) + b_re.astype(jnp.float32)
    le_sel = jnp.take_along_axis(le, g_idx[:, :, None], axis=1)[:, 0]
    top_v, top_i = lax.top_k(le_sel, TOP_K_FINE)
    pw = jax.nn.softmax(top_v, axis=-1)
    eid = g_idx * EXP_PER_GROUP + top_i
    gates = jnp.sum(jax.nn.one_hot(eid, N_EXPERTS, dtype=jnp.float32) * (pg_sel * pw)[..., None], axis=1)
    gates = gates.astype(t.dtype)
    out = jnp.zeros_like(t)
    for e in range(N_EXPERTS):
        hid = jax.nn.silu(t @ w_eg[e]) * (t @ w_eu[e])
        out = out + gates[:, e:e + 1] * (hid @ w_ed[e])
    return out.reshape(bsz, s, d)

def first_inputs(seed: int = 0) -> dict:
    key = jax.random.key(seed)
    ks = jax.random.split(key, 32)
    f32 = jnp.float32
    def nrm(k, shape, sc):
        return jax.random.normal(k, shape, f32) * sc
    L = DEPTH
    b_i = nrm(ks[7], (L, ML_HEADS), 0.1)
    b_f = jnp.linspace(3.0, 6.0, ML_HEADS, dtype=f32)[None, :] + nrm(ks[8], (L, ML_HEADS), 0.01)
    return {
        'x': nrm(ks[0], (BATCH, SEQ, D_MODEL), 1.0),
        'w_in': nrm(ks[1], (L, D_MODEL, IN_COLS), D_MODEL ** -0.5),
        'conv_w': nrm(ks[2], (L, CONV_W, D_MLSTM), CONV_W ** -0.5),
        'conv_b': nrm(ks[3], (L, D_MLSTM), 0.01),
        'w_mq': nrm(ks[4], (L, ML_HEADS, ML_HD, ML_HD), ML_HD ** -0.5),
        'w_mk': nrm(ks[5], (L, ML_HEADS, ML_HD, ML_HD), ML_HD ** -0.5),
        'w_mgate': nrm(ks[6], (L, 3 * D_MLSTM, 2 * ML_HEADS), 0.1 * (3 * D_MLSTM) ** -0.5),
        'b_mgate': jnp.concatenate([b_i, b_f], axis=-1),
        'm_norm_g': 1.0 + nrm(ks[9], (L, D_MLSTM), 0.02),
        'm_skip': 1.0 + nrm(ks[10], (L, D_MLSTM), 0.02),
        'lambda_qk': nrm(ks[11], (L, 4, DA_QD), 0.1),
        'da_norm_g': 1.0 + nrm(ks[12], (L, DA_VD), 0.02),
        'rel_bias': nrm(ks[13], (REL_BUCKETS, DA_HEADS), 0.2),
        'w_out': nrm(ks[14], (L, D_MIX, D_MODEL), D_MIX ** -0.5),
        'norm1_g': 1.0 + nrm(ks[15], (L, D_MODEL), 0.02),
        'norm2_g': 1.0 + nrm(ks[16], (L, D_MODEL), 0.02),
        'w_rg': nrm(ks[17], (L, D_MODEL, N_GROUPS), D_MODEL ** -0.5),
        'b_rg': nrm(ks[18], (L, N_GROUPS), 0.01),
        'w_re': nrm(ks[19], (L, D_MODEL, N_GROUPS, EXP_PER_GROUP), D_MODEL ** -0.5),
        'b_re': nrm(ks[20], (L, N_GROUPS, EXP_PER_GROUP), 0.01),
        'w_eg': nrm(ks[21], (L, N_EXPERTS, D_MODEL, D_FF_EXP), D_MODEL ** -0.5),
        'w_eu': nrm(ks[22], (L, N_EXPERTS, D_MODEL, D_FF_EXP), D_MODEL ** -0.5),
        'w_ed': nrm(ks[23], (L, N_EXPERTS, D_FF_EXP, D_MODEL), D_FF_EXP ** -0.5),
        'normf_g': 1.0 + nrm(ks[24], (D_MODEL,), 0.02),
    }

def first_block(x, w_in, conv_w, conv_b, w_mq, w_mk, w_mgate, b_mgate, m_norm_g, m_skip,
              lambda_qk, da_norm_g, rel_bias, w_out, norm1_g, norm2_g, w_rg, b_rg, w_re, b_re,
              w_eg, w_eu, w_ed, normf_g):
    bsz, s, _ = x.shape
    splits = [D_MLSTM, 2 * D_MLSTM, 3 * D_MLSTM, 3 * D_MLSTM + D_DIFF, 3 * D_MLSTM + 2 * D_DIFF]
    for l in range(DEPTH):
        lam_init = 0.8 - 0.6 * math.exp(-0.3 * l)
        h = rmsnorm(x, norm1_g[l])
        proj = h @ w_in[l]
        c, vm, z, qd, kd, vd = jnp.split(proj, splits, axis=-1)
        y_m = mlstm_group(c, vm, z, conv_w[l], conv_b[l], w_mq[l], w_mk[l], w_mgate[l], b_mgate[l],
                          m_norm_g[l], m_skip[l])
        lq = lambda_qk[l].astype(jnp.float32)
        lam = jnp.exp(jnp.dot(lq[0], lq[1])) - jnp.exp(jnp.dot(lq[2], lq[3])) + lam_init
        y_d = diff_attention(qd.reshape(bsz, s, DA_HEADS, 2, DA_QD), kd.reshape(bsz, s, DA_HEADS, 2, DA_QD),
                             vd.reshape(bsz, s, DA_HEADS, DA_VD), lam, rel_bias)
        y_d = (rmsnorm(y_d, da_norm_g[l], SUBLN_EPS) * (1.0 - lam_init)).reshape(bsz, s, D_DIFF)
        x = x + jnp.concatenate([y_m, y_d.astype(x.dtype)], axis=-1) @ w_out[l]
        h2 = rmsnorm(x, norm2_g[l])
        x = x + hier_moe(h2, w_rg[l], b_rg[l], w_re[l], b_re[l], w_eg[l], w_eu[l], w_ed[l])
    return rmsnorm(x, normf_g)


DEPTH_2 = 2

SSD_D_INNER = D_MODEL
SSD_HEADDIM = 64
SSD_HEADS = SSD_D_INNER // SSD_HEADDIM
SSD_GROUPS = 2
SSD_HPG = SSD_HEADS // SSD_GROUPS
SSD_STATE = 128
SSD_CONV = 4
SSD_CHUNK = 128
SSD_CONV_DIM = SSD_D_INNER + 2 * SSD_GROUPS * SSD_STATE
RET_HEADS = 4
RET_QK_DIM = 128
RET_HEAD_V = D_MODEL // RET_HEADS
RET_CHUNK = 128
ROPE_BASE = 10000.0
ATT_Q_HEADS = 16
ATT_KV_HEADS = 2
ATT_GROUP = ATT_Q_HEADS // ATT_KV_HEADS
ATT_HEAD_DIM = D_MODEL // ATT_Q_HEADS
WINDOW = 128
ATT_BLOCK = 128
REL_MAX_EXACT = REL_BUCKETS // 2
N_BRANCH = 3
BRANCH_WIDTH = D_MODEL
D_FF = 2816
NEG = -1e30

IN_SPLIT_SIZES = (
    SSD_D_INNER,
    SSD_CONV_DIM,
    SSD_HEADS,
    RET_HEADS * RET_QK_DIM,
    RET_HEADS * RET_QK_DIM,
    RET_HEADS * RET_HEAD_V,
    RET_HEADS * RET_HEAD_V,
    ATT_Q_HEADS * ATT_HEAD_DIM,
    ATT_KV_HEADS * ATT_HEAD_DIM,
    ATT_KV_HEADS * ATT_HEAD_DIM,
    N_BRANCH * D_MODEL,
)
IN_WIDTH = sum(IN_SPLIT_SIZES)


def rmsnorm_2(x, g):
    xf = x.astype(jnp.float32)
    y = xf * lax.rsqrt(jnp.mean(xf * xf, axis=-1, keepdims=True) + EPS)
    return (y * g.astype(jnp.float32)).astype(x.dtype)

def swiglu(x, w_in, w_out):
    a, b = jnp.split(x @ w_in, 2, axis=-1)
    return (jax.nn.silu(a) * b) @ w_out

def causal_dwconv(x, w, b):
    c = x.shape[-1]
    y = lax.conv_general_dilated(x, w[:, None, :].astype(x.dtype), (1,), [(SSD_CONV - 1, 0)],
                                 dimension_numbers=('NWC', 'WIO', 'NWC'), feature_group_count=c)
    return y + b

def ssd_mixer(z, xbc, dt_raw, conv_w, conv_b, dt_bias, a_log, d_skip, norm_g):
    bsz, L, _ = z.shape
    nc = L // SSD_CHUNK
    xbc = jax.nn.silu(causal_dwconv(xbc, conv_w, conv_b))
    xs, bm, cm = jnp.split(xbc, [SSD_D_INNER, SSD_D_INNER + SSD_GROUPS * SSD_STATE], axis=-1)
    xs = xs.reshape(bsz, nc, SSD_CHUNK, SSD_GROUPS, SSD_HPG, SSD_HEADDIM)
    bm = bm.reshape(bsz, nc, SSD_CHUNK, SSD_GROUPS, SSD_STATE)
    cm = cm.reshape(bsz, nc, SSD_CHUNK, SSD_GROUPS, SSD_STATE)
    dt = jax.nn.softplus(dt_raw.astype(jnp.float32) + dt_bias.astype(jnp.float32))
    dt = dt.reshape(bsz, nc, SSD_CHUNK, SSD_GROUPS, SSD_HPG)
    a = -jnp.exp(a_log.astype(jnp.float32)).reshape(SSD_GROUPS, SSD_HPG)
    da = jnp.moveaxis(dt * a, 2, -1)
    a_cs = jnp.cumsum(da, axis=-1)
    causal = jnp.tril(jnp.ones((SSD_CHUNK, SSD_CHUNK), dtype=bool))
    seg = a_cs[..., :, None] - a_cs[..., None, :]
    lmat = jnp.exp(jnp.where(causal, seg, -jnp.inf))
    xdt = xs * dt[..., None]
    cb = jnp.einsum('bclgn,bcsgn->bcgls', cm, bm)
    y_diag = jnp.einsum('bcgjls,bcsgjp->bclgjp', cb[:, :, :, None] * lmat, xdt)
    decay_st = jnp.moveaxis(jnp.exp(a_cs[..., -1:] - a_cs), -1, 2)
    states = jnp.einsum('bclgn,bclgjp->bcgjpn', bm, xdt * decay_st[..., None])
    chunk_decay = jnp.exp(a_cs[..., -1])

    def step(h, inp):
        s, dcy = inp
        return (h * dcy[..., None, None] + s).astype(h.dtype), h

    h0 = jnp.zeros_like(states[:, 0])
    _, prev = lax.scan(step, h0, (jnp.moveaxis(states, 1, 0), jnp.moveaxis(chunk_decay, 1, 0)))
    prev = jnp.moveaxis(prev, 0, 1)
    decay_out = jnp.moveaxis(jnp.exp(a_cs), -1, 2)
    y_off = jnp.einsum('bclgn,bcgjpn->bclgjp', cm, prev) * decay_out[..., None]
    y = y_diag + y_off + xs * d_skip.reshape(SSD_GROUPS, SSD_HPG, 1)
    y = y.reshape(bsz, L, SSD_D_INNER).astype(z.dtype)
    return rmsnorm_2(y * jax.nn.silu(z), norm_g)

def rope(x, cos, sin):
    x1, x2 = jnp.split(x, 2, axis=-1)
    c = cos[:, None, :]
    s = sin[:, None, :]
    return jnp.concatenate([x1 * c - x2 * s, x2 * c + x1 * s], axis=-1)

def retention_mixer(q, k, v, g, gn_g, cos, sin):
    bsz, L, _ = q.shape
    nc = L // RET_CHUNK
    q = rope(q.reshape(bsz, L, RET_HEADS, RET_QK_DIM), cos, sin)
    k = rope(k.reshape(bsz, L, RET_HEADS, RET_QK_DIM), cos, sin) * (RET_QK_DIM ** -0.5)
    v = v.reshape(bsz, L, RET_HEADS, RET_HEAD_V)
    log_g = jnp.log(1.0 - jnp.exp2(-5.0 - jnp.arange(RET_HEADS, dtype=jnp.float32)))
    idx = jnp.arange(RET_CHUNK, dtype=jnp.float32)
    diff = idx[:, None] - idx[None, :]
    dmat = jnp.where(diff >= 0, jnp.exp(jnp.maximum(diff, 0.0)[None] * log_g[:, None, None]), 0.0)
    qc = q.reshape(bsz, nc, RET_CHUNK, RET_HEADS, RET_QK_DIM)
    kc = k.reshape(bsz, nc, RET_CHUNK, RET_HEADS, RET_QK_DIM)
    vc = v.reshape(bsz, nc, RET_CHUNK, RET_HEADS, RET_HEAD_V)
    inner = jnp.einsum('bnhij,bnjhe->bnihe', jnp.einsum('bnihd,bnjhd->bnhij', qc, kc) * dmat, vc)
    zeta = jnp.exp((RET_CHUNK - 1.0 - idx)[:, None] * log_g[None, :])
    chunk_kv = jnp.einsum('bnjhd,bnjhe->bnhde', kc * zeta[..., None], vc)
    chunk_decay = jnp.exp(RET_CHUNK * log_g)

    def step(r, s):
        return (r * chunk_decay[:, None, None] + s).astype(r.dtype), r

    r0 = jnp.zeros_like(chunk_kv[:, 0])
    _, prev = lax.scan(step, r0, jnp.moveaxis(chunk_kv, 1, 0))
    prev = jnp.moveaxis(prev, 0, 1)
    xi = jnp.exp((idx + 1.0)[:, None] * log_g[None, :])
    cross = jnp.einsum('bnihd,bnhde->bnihe', qc, prev) * xi[..., None]
    o = (inner + cross).reshape(bsz, L, RET_HEADS, RET_HEAD_V).astype(jnp.float32)
    mu = jnp.mean(o, axis=-1, keepdims=True)
    var = jnp.mean(jnp.square(o - mu), axis=-1, keepdims=True)
    o = ((o - mu) * lax.rsqrt(var + EPS)).reshape(bsz, L, RET_HEADS * RET_HEAD_V)
    o = (o * gn_g.astype(jnp.float32)).astype(g.dtype)
    return o * jax.nn.silu(g)

def t5_bucket(dist):
    is_small = dist < REL_MAX_EXACT
    d = jnp.maximum(dist, 1).astype(jnp.float32)
    large = REL_MAX_EXACT + (jnp.log(d / REL_MAX_EXACT) / math.log(REL_MAX_DIST / REL_MAX_EXACT)
                             * (REL_BUCKETS - REL_MAX_EXACT)).astype(jnp.int32)
    large = jnp.minimum(large, REL_BUCKETS - 1)
    return jnp.where(is_small, dist, large)

def swa_sink_attention(q, k, v, sinks, band_bias, band_mask):
    bsz, L, _ = q.shape
    nb = L // ATT_BLOCK
    q = q.reshape(bsz, nb, ATT_BLOCK, ATT_KV_HEADS, ATT_GROUP, ATT_HEAD_DIM)
    k = k.reshape(bsz, L, ATT_KV_HEADS, ATT_HEAD_DIM)
    v = v.reshape(bsz, L, ATT_KV_HEADS, ATT_HEAD_DIM)

    def band(t):
        tp = jnp.pad(t, ((0, 0), (ATT_BLOCK, 0), (0, 0), (0, 0)))
        tp = tp.reshape(bsz, nb + 1, ATT_BLOCK, ATT_KV_HEADS, ATT_HEAD_DIM)
        return jnp.concatenate([tp[:, :-1], tp[:, 1:]], axis=2)

    kb, vb = band(k), band(v)
    s = jnp.einsum('bnqkgd,bnskd->bnkgqs', q, kb).astype(jnp.float32) * (ATT_HEAD_DIM ** -0.5)
    s = jnp.where(band_mask[None, :, None, None], s + band_bias, NEG)
    sink = sinks.astype(jnp.float32).reshape(ATT_KV_HEADS, ATT_GROUP, 1, 1)
    m = jnp.maximum(jnp.max(s, axis=-1, keepdims=True), sink)
    e = jnp.exp(s - m)
    p = e / (jnp.sum(e, axis=-1, keepdims=True) + jnp.exp(sink - m))
    o = jnp.einsum('bnkgqs,bnskd->bnqkgd', p.astype(v.dtype), vb)
    return o.reshape(bsz, L, ATT_Q_HEADS * ATT_HEAD_DIM)

def second_inputs(seed: int = 0) -> dict:
    key = jax.random.key(seed)
    ks = iter(jax.random.split(key, 32))
    f32 = jnp.float32

    def nrm(shape, fan_in):
        return jax.random.normal(next(ks), shape, f32) * (fan_in ** -0.5)

    def gain(shape):
        return 1.0 + 0.1 * jax.random.normal(next(ks), shape, f32)

    x = jax.random.normal(next(ks), (BATCH, SEQ, D_MODEL), f32)
    ffn1_pre_g = gain((DEPTH_2, D_MODEL))
    ffn1_post_g = gain((DEPTH_2, D_MODEL))
    w_ffn1_in = nrm((DEPTH_2, D_MODEL, 2 * D_FF), D_MODEL)
    w_ffn1_out = nrm((DEPTH_2, D_FF, D_MODEL), D_FF)
    mix_pre_g = gain((DEPTH_2, D_MODEL))
    mix_post_g = gain((DEPTH_2, D_MODEL))
    w_in = nrm((DEPTH_2, D_MODEL, IN_WIDTH), D_MODEL)
    conv_w = nrm((DEPTH_2, SSD_CONV, SSD_CONV_DIM), SSD_CONV)
    conv_b = 0.1 * jax.random.normal(next(ks), (DEPTH_2, SSD_CONV_DIM), f32)
    dt0 = jnp.exp(jax.random.uniform(next(ks), (DEPTH_2, SSD_HEADS), f32,
                                     math.log(1e-3), math.log(1e-1)))
    dt_bias = dt0 + jnp.log(-jnp.expm1(-dt0))
    a_log = jnp.log(jax.random.uniform(next(ks), (DEPTH_2, SSD_HEADS), f32, 1.0, 16.0))
    d_skip = gain((DEPTH_2, SSD_HEADS))
    ssd_norm_g = gain((DEPTH_2, SSD_D_INNER))
    ret_gn_g = gain((DEPTH_2, RET_HEADS * RET_HEAD_V))
    attn_sinks = 0.5 * jax.random.normal(next(ks), (DEPTH_2, ATT_Q_HEADS), f32)
    rel_bias = 0.5 * jax.random.normal(next(ks), (REL_BUCKETS, ATT_Q_HEADS), f32)
    b_gate = 0.1 * jax.random.normal(next(ks), (DEPTH_2, N_BRANCH * D_MODEL), f32)
    w_branch = nrm((DEPTH_2, N_BRANCH, BRANCH_WIDTH, D_MODEL), BRANCH_WIDTH)
    w_out = nrm((DEPTH_2, D_MODEL, D_MODEL), D_MODEL)
    ffn2_pre_g = gain((DEPTH_2, D_MODEL))
    ffn2_post_g = gain((DEPTH_2, D_MODEL))
    w_ffn2_in = nrm((DEPTH_2, D_MODEL, 2 * D_FF), D_MODEL)
    w_ffn2_out = nrm((DEPTH_2, D_FF, D_MODEL), D_FF)
    return {"x": x, "ffn1_pre_g": ffn1_pre_g, "ffn1_post_g": ffn1_post_g,
            "w_ffn1_in": w_ffn1_in, "w_ffn1_out": w_ffn1_out,
            "mix_pre_g": mix_pre_g, "mix_post_g": mix_post_g, "w_in": w_in,
            "conv_w": conv_w, "conv_b": conv_b, "dt_bias": dt_bias, "a_log": a_log,
            "d_skip": d_skip, "ssd_norm_g": ssd_norm_g, "ret_gn_g": ret_gn_g,
            "attn_sinks": attn_sinks, "rel_bias": rel_bias, "b_gate": b_gate,
            "w_branch": w_branch, "w_out": w_out,
            "ffn2_pre_g": ffn2_pre_g, "ffn2_post_g": ffn2_post_g,
            "w_ffn2_in": w_ffn2_in, "w_ffn2_out": w_ffn2_out}

def second_block(x, ffn1_pre_g, ffn1_post_g, w_ffn1_in, w_ffn1_out, mix_pre_g, mix_post_g, w_in,
              conv_w, conv_b, dt_bias, a_log, d_skip, ssd_norm_g, ret_gn_g, attn_sinks, rel_bias,
              b_gate, w_branch, w_out, ffn2_pre_g, ffn2_post_g, w_ffn2_in, w_ffn2_out):
    bsz, L, _ = x.shape
    offsets = np.cumsum(IN_SPLIT_SIZES)[:-1].tolist()
    pos = jnp.arange(L, dtype=jnp.float32)
    inv = 1.0 / (ROPE_BASE ** (jnp.arange(0, RET_QK_DIM, 2, dtype=jnp.float32) / RET_QK_DIM))
    ang = pos[:, None] * inv[None, :]
    cos, sin = jnp.cos(ang), jnp.sin(ang)
    nb = L // ATT_BLOCK
    qi = jnp.arange(ATT_BLOCK)[:, None]
    sj = jnp.arange(2 * ATT_BLOCK)[None, :]
    dist = qi + ATT_BLOCK - sj
    blk = jnp.arange(nb)[:, None, None]
    band_mask = (dist >= 0) & (dist < WINDOW) & ((blk > 0) | (sj >= ATT_BLOCK))
    band_bias = jnp.transpose(rel_bias[t5_bucket(jnp.maximum(dist, 0))], (2, 0, 1))
    band_bias = band_bias.astype(jnp.float32).reshape(ATT_KV_HEADS, ATT_GROUP, ATT_BLOCK, 2 * ATT_BLOCK)

    for l in range(DEPTH_2):
        x = x + 0.5 * rmsnorm_2(swiglu(rmsnorm_2(x, ffn1_pre_g[l]), w_ffn1_in[l], w_ffn1_out[l]), ffn1_post_g[l])
        h = rmsnorm_2(x, mix_pre_g[l])
        (z, xbc, dt_raw, rq, rk, rv, rg, aq, ak, av, gate) = jnp.split(h @ w_in[l], offsets, axis=-1)
        y_ssd = ssd_mixer(z, xbc, dt_raw, conv_w[l], conv_b[l], dt_bias[l], a_log[l], d_skip[l], ssd_norm_g[l])
        y_ret = retention_mixer(rq, rk, rv, rg, ret_gn_g[l], cos, sin)
        y_att = swa_sink_attention(aq, ak, av, attn_sinks[l], band_bias, band_mask)
        ys = jnp.stack([y_ssd.astype(x.dtype), y_ret.astype(x.dtype), y_att.astype(x.dtype)], axis=2)
        branch = jnp.einsum('blmc,mcd->blmd', ys, w_branch[l])
        gates = jax.nn.sigmoid((gate + b_gate[l]).reshape(bsz, L, N_BRANCH, D_MODEL))
        y = jnp.sum(gates * branch, axis=2) @ w_out[l]
        x = x + rmsnorm_2(y, mix_post_g[l])
        x = x + 0.5 * rmsnorm_2(swiglu(rmsnorm_2(x, ffn2_pre_g[l]), w_ffn2_in[l], w_ffn2_out[l]), ffn2_post_g[l])
    return x


def setup_inputs(seed=0):
    out = dict(first_inputs(seed))
    for name, value in second_inputs(seed + 1).items():
        if name != "x":
            out[name + "_2"] = value
    return out


def reference(
    x, w_in, conv_w, conv_b, w_mq, w_mk, w_mgate, b_mgate, m_norm_g, m_skip, lambda_qk,
    da_norm_g, rel_bias, w_out, norm1_g, norm2_g, w_rg, b_rg, w_re, b_re, w_eg, w_eu, w_ed,
    normf_g, ffn1_pre_g_2, ffn1_post_g_2, w_ffn1_in_2, w_ffn1_out_2, mix_pre_g_2, mix_post_g_2,
    w_in_2, conv_w_2, conv_b_2, dt_bias_2, a_log_2, d_skip_2, ssd_norm_g_2, ret_gn_g_2,
    attn_sinks_2, rel_bias_2, b_gate_2, w_branch_2, w_out_2, ffn2_pre_g_2, ffn2_post_g_2,
    w_ffn2_in_2, w_ffn2_out_2,
):
    x = first_block(
        x, w_in, conv_w, conv_b, w_mq, w_mk, w_mgate, b_mgate, m_norm_g, m_skip, lambda_qk,
        da_norm_g, rel_bias, w_out, norm1_g, norm2_g, w_rg, b_rg, w_re, b_re, w_eg, w_eu, w_ed,
        normf_g,
    )
    return second_block(
        x, ffn1_pre_g_2, ffn1_post_g_2, w_ffn1_in_2, w_ffn1_out_2, mix_pre_g_2, mix_post_g_2,
        w_in_2, conv_w_2, conv_b_2, dt_bias_2, a_log_2, d_skip_2, ssd_norm_g_2, ret_gn_g_2,
        attn_sinks_2, rel_bias_2, b_gate_2, w_branch_2, w_out_2, ffn2_pre_g_2, ffn2_post_g_2,
        w_ffn2_in_2, w_ffn2_out_2,
    )


_drawn_inputs = setup_inputs


def setup_inputs(seed=0):
    import zlib

    import numpy as np

    out = dict(_drawn_inputs(seed))
    spreads = {}
    factors = {'b_rg': 2.87, 'attn_sinks_2': 6.082}
    for name, (base, spread) in spreads.items():
        noise = np.random.default_rng([zlib.crc32(name.encode()), seed]).standard_normal(out[name].shape)
        drawn = base * np.exp(spread * noise) if base else spread * noise
        out[name] = __import__('jax').numpy.asarray(drawn.astype(out[name].dtype))
    for name, factor in factors.items():
        out[name] = (out[name] * factor).astype(out[name].dtype)
    return out
```

```python
from contextlib import ExitStack, contextmanager
import math

import concourse.bass as bass
import numpy as np
from concourse import mybir

P = 128
T = 256
TT = T // P
D = 1024
KT = D // P
UNIT = 2048
SLOTS = 6
BANKS = 8
NEG = -1e30

H1 = 4
EXPERTS = 32
GROUPS = 4
PER_GROUP = 8
FE = 512
CAP = 64
PASSES = T // CAP
PAIRS = EXPERTS // 2
LAM_INIT = 0.8 - 0.6 * math.exp(-0.3 * 0)
EPS = 1e-6
SUBLN_EPS = 1e-5

LAYERS = 2
FF = 2816
FT = FF // P
SSD_H = 16
SSD_G = 2
CONV_T = 12
RET_H = 4
ATT_H = 16
ATT_D = 64

ALU = mybir.AluOpType
ACT = mybir.ActivationFunctionType
AX = mybir.AxisListType
F32 = mybir.dt.float32
F32R = mybir.dt.float32r
I32 = mybir.dt.int32
AHEAD_UNITS = 2
HI_BUFFERS = AHEAD_UNITS + 1

CONST = [("ident", P), ("mask", P), ("ones", T), ("before", P), ("slot", 2 * CAP), ("prior4", 4), ("prior8", 8), ("eps", 8)]
FIRST = [("g1", KT), ("g2", KT), ("convw", 16), ("convb", 4), ("mnorm", 4), ("mskip", 4), ("wgate", 96),
         ("bi", 1), ("bf", 1), ("lam", 256), ("danorm", 1), ("wroute", KT * 36), ("broute", 36),
         ("wmq", 512), ("wmk", 512), ("bias", 4 * (P + T))]
SECOND = [("decay", RET_H * 3 * P), ("cos", TT * 64), ("sin", TT * 64), ("bias", ATT_H * 2 * P)]
LAYER = [("gpre1", KT), ("gmix", KT), ("gpre2", KT), ("convw", CONV_T * 4), ("convb", CONV_T), ("wdt", KT * 16),
         ("gssd", KT), ("gret", KT), ("bgate", 3 * KT), ("dtbias", 1), ("alog", 1), ("dskip", KT), ("sinks", ATT_H)]


def offsets(table):
    out, at = {}, 0
    for name, n in table:
        out[name] = (at, n)
        at += n
    return out, at


def place(jobs, banks):
    where, uses = {}, [0] * banks
    for i, name in enumerate(jobs):
        b = i % banks
        assert name not in where, name
        where[name] = (b, uses[b])
        uses[b] += 1
    return where, uses


FIRST_JOBS = ([f"n1.{i}" for i in range(4)]
              + [f"{s}.{i}" for s in ("c", "v", "qd", "kd", "vd", "z") for i in range(2)]
              + [f"vtok.{t}" for t in range(2)] + [f"vdtok.{t}" for t in range(2)]
              + [f"ds0.{c}" for c in range(2)] + [f"ds1.{hp}.{c}" for hp in range(2) for c in range(2)]
              + [f"mq.{i}" for i in range(2)] + [f"mk.{i}" for i in range(2)]
              + ["gates"] + [f"ms.{h}" for h in range(4)]
              + ["gcol", "bc.0", "bc.1"] + ["daT.0", "daT.1", "daT.2"]
              + ["num.0", "num.1", "den"] + ["dout.0", "dout.1"]
              + ["hT.0", "hT.1"] + ["ydT.0", "ydT.1"]
              + [f"out.{n}.{t}" for n in range(2) for t in range(2)]
              + [f"n2.{i}" for i in range(4)] + ["route", "rank"])
FIRST_UNITS = [(f"{s}.{i}", f"{s}.{i}") for s in ("c", "v", "qd", "kd", "vd", "z") for i in range(2)] + \
              [(f"out.{n}.{i}", (None, f"out.{n}.1")[i]) for n in range(2) for i in range(2)]

LAYER_JOBS = ([f"f1.n.{i}" for i in range(4)] + [f"f1.in.{i}" for i in range(FT)]
              + [f"f1.out.{n}.{t}" for n in range(2) for t in range(2)]
              + [f"mx.n.{i}" for i in range(4)]
              + [f"rq.{t}" for t in range(2)] + [f"rk.{t}" for t in range(2)]
              + [f"rv.{n}.{t}" for n in range(2) for t in range(2)]
              + [f"rg.{n}.{t}" for n in range(2) for t in range(2)]
              + [f"xbc.{i}" for i in range(6)]
              + [f"rqT.{i}" for i in range(2)] + [f"rkT.{i}" for i in range(2)]
              + ["dt"] + [f"z.{i}" for i in range(4)] + [f"rs.{h}" for h in range(4)]
              + ["dtcol", "cb.0", "cb.1"] + [f"xst.{i}" for i in range(4)]
              + [f"ro.{t}.{i}" for t in range(2) for i in range(2)]
              + [f"sbc.{i}" for i in range(4)] + [f"aq.{i}" for i in range(4)] + ["sy.0", "sy.1"]
              + [f"sbc.{i}" for i in range(4, 8)] + ["akv"] + [f"rT.{i}" for i in range(4)] + ["sy.2", "sy.3", "ssum"]
              + [f"as.0.{kv}.{i}" for kv in range(2) for i in range(2)]
              + [f"as.1.{kv}.{i}" for kv in range(2) for i in range(4)]
              + [f"g.0.{i}" for i in range(4)] + [f"b.0.{i}" for i in range(4)]
              + [f"ap.0.{kv}.{j}" for kv in range(2) for j in range(2)] + ["ao.0.0", "ao.0.1"]
              + [f"ap.1.{kv}.{j}.{s}" for kv in range(2) for j in range(2) for s in range(2)] + ["ao.1.0", "ao.1.1"]
              + [f"{a}.{m}.{i}" for m in (1, 2) for a in ("g", "b") for i in range(4)]
              + [f"mx.out.{n}.{t}" for n in range(2) for t in range(2)]
              + [f"f2.n.{i}" for i in range(4)] + [f"f2.in.{i}" for i in range(FT)]
              + [f"f2.out.{n}.{t}" for n in range(2) for t in range(2)])


def row_units(name, jobs):
    return [(f"{name}.0", None), (f"{name}.1", jobs)]


def ffn_units(f):
    return ([(f"{f}.in.{i}", f"{f}.in.{i}") for i in range(FT)]
            + [(f"{f}.out.{i}", None if i < FT // 2 - 1 else f"{f}.out.1.1") for i in range(FT // 2)])


LAYER_UNITS = (ffn_units("f1") + row_units("rq", "rq.1") + row_units("rk", "rk.1")
               + [u for r in ("rv", "rg") for n in range(2) for u in row_units(f"{r}.{n}", f"{r}.{n}.1")]
               + [(f"xbc.{i}", f"xbc.{i}") for i in range(6)] + [(f"z.{i}", f"z.{i}") for i in range(4)]
               + [(f"aq.{i}", f"aq.{i}") for i in range(4)] + [("akv", "akv")]
               + [(f"{a}.{m}.{i}", f"{a}.{m}.{i}") for m in range(3) for a in ("g", "b") for i in range(4)]
               + [u for n in range(2) for u in row_units(f"mx.out.{n}", f"mx.out.{n}.1")]
               + ffn_units("f2"))


class Banks:

    def __init__(self, full_sems, free_sems, jobs, base, l=None):
        self.full_sems, self.free_sems, self.base, self.l = full_sems, free_sems, base, l
        self.where, self.uses = place(jobs, BANKS)

    def bank(self, job):
        return self.where[job][0]

    def count(self, job, extra):
        b, use = self.where[job]
        n = self.base[b] + use + extra
        return n if self.l is None else self.l * self.uses[b] + n

    def full(self, job):
        return self.full_sems[self.bank(job)]

    def free(self, job):
        return self.free_sems[self.bank(job)]

    def filled(self, job):
        return self.full(job), self.count(job, 1)

    def drained(self, job):
        return self.free(job), self.count(job, 1)

    def claim(self, pe, job):
        b, use = self.where[job]
        if self.base[b] + use:
            pe.wait_ge(self.free(job), self.count(job, 0))

    def after(self):
        return [x + y for x, y in zip(self.base, self.uses)]


class Units:

    def __init__(self, landed_sems, parts_sem, units, base, parts_base, B, l=None):
        self.landed_sems, self.parts_sem, self.base, self.B, self.l = landed_sems, parts_sem, base, B, l
        self.parts_base = parts_base
        self.names = [n for n, _ in units]
        self.ends = dict(units)
        self.index = {n: i for i, n in enumerate(self.names)}
        self.per = [len(range(s, len(units), SLOTS)) for s in range(SLOTS)]
        parts = [n for n in self.names if self.ends[n] is None]
        self.part = {n: i for i, n in enumerate(parts)}

    def slot(self, name):
        return self.index[name] % SLOTS

    def landed(self, name):
        i = self.index[name]
        n = self.base[i % SLOTS] + i // SLOTS + 1
        n = n if self.l is None else self.l * self.per[i % SLOTS] + n
        return self.landed_sems[self.slot(name)], n * 16

    def given_back(self, name):
        if self.ends[name] is not None:
            return self.B.filled(self.ends[name])
        n = self.parts_base + self.part[name] + 1
        return self.parts_sem, (n if self.l is None else self.l * len(self.part) + n)

    def after(self):
        return [x + y for x, y in zip(self.base, self.per)], self.parts_base + len(self.part)


class Flags:

    def __init__(self, make, prefix, per, l=None, before={}):
        self.make, self.prefix, self.per, self.l, self.before = make, prefix, per, l, before
        self.sems, self.raised, self.asked = {}, {}, {}

    def sem(self, name):
        if name not in self.sems:
            self.sems[name] = self.make(f"{self.prefix}{name}")
        return self.sems[name]

    def __getitem__(self, name):
        self.raised[name] = self.raised.get(name, 0) + 1
        return self.sem(name)

    def at(self, name, k=1):
        self.asked[name] = max(k, self.asked.get(name, 0))
        n = k + self.before.get(name, 0)
        assert n > 0, name
        return self.sem(name), (n if self.l is None else self.l * self.per.get(name, 1) + n)

    def settle(self):
        for name, n in self.raised.items():
            assert self.l is None or n == self.per.get(name, 1), (self.prefix, name, n)
        for name, k in self.asked.items():
            assert k <= self.raised.get(name, 0), (self.prefix, name, k)


class Chain:

    def __init__(self, engine, sem, base=0, per=0, l=None):
        self.engine, self.sem, self.base, self.per, self.l, self.n = engine, sem, base, per, l, 0

    def __call__(self, ins):
        self.n += 1
        n = self.base + self.n
        ins.then_inc(self.sem, 1)
        self.engine.wait_ge(self.sem, n if self.l is None else self.l * self.per + n)


def bc(ap, shape):
    while len(ap.shape) < len(shape):
        ap = ap.unsqueeze(len(ap.shape))
    return ap.to_broadcast(shape)


def split(ap, n):
    return ap.rearrange("p (n b) -> p n b", n=n)


class Memory:

    def __init__(self, area):
        self.area, self.at, self.high = area, 0, 0

    def take(self, n):
        ap = self.area[:, self.at:self.at + n]
        self.at += n
        self.high = max(self.high, self.at)
        return ap



def square_sums(act, x, scratch, sums, flag):
    for t in range(TT):
        act.activation(scratch[:, t, :], x[:, t, :], ACT.Square, scale=D ** -0.5, accum_out=sums[:, t:t + 1]).then_inc(flag(), 1)


def root_of_mean(pool, step, out, eps, minus_half, flag):
    step(pool.tensor_tensor(out, out, eps, ALU.add))
    pool.tensor_tensor(out, out, minus_half, ALU.pow).then_inc(flag, 1)


def inverse_root(pool, step, out, sums, minus_half, width, eps, flag):
    step(pool.tensor_scalar(out, sums, 1.0 / width, eps, ALU.mult, ALU.add))
    pool.tensor_tensor(out, out, minus_half, ALU.pow).then_inc(flag, 1)


def turn_rows(pe, B, names, ps, src, ident, F, f):
    for job in names:
        B.claim(pe, job)
    for t in range(TT):
        pe.wait_ge(*F.at(f"{f}.xn", t + 1))
        for i, job in enumerate(names):
            for k in range(2):
                mm = pe.transpose(ps[B.bank(job)][:, k * T + t * P:k * T + t * P + P],
                                  src[:, t, (2 * i + k) * P:(2 * i + k + 1) * P], ident)
            if t == TT - 1:
                mm.then_inc(B.full(job), 1)


def take_columns(eng, B, names, ps, dst, gain, odd):
    for i, job in enumerate(names):
        if i % 2 != odd:
            continue
        eng.wait_ge(*B.filled(job))
        bank = split(ps[B.bank(job)][:], 2)
        if not odd:
            eng.tensor_tensor(dst[:, 2 * i:2 * i + 2, :], bank, bc(gain[:, 2 * i:2 * i + 2], [P, 2, T]),
                              ALU.mult).then_inc(B.free(job), 1)
        else:
            for k in range(2):
                ins = eng.activation(dst[:, 2 * i + k, :], bank[:, k, :], ACT.Copy,
                                     scale=gain[:, 2 * i + k:2 * i + k + 1])
            ins.then_inc(B.free(job), 1)


def wait_columns(pe, B, names):
    for job in names:
        pe.wait_ge(*B.drained(job))


def project_columns(pe, B, U, ps, ring, job, unit, moving):
    B.claim(pe, job)
    pe.wait_ge(*U.landed(unit))
    w = ring[U.slot(unit)].rearrange("p (k n) -> p k n", k=KT)
    for c in range(2):
        for k in range(KT):
            mm = pe.matmul(ps[B.bank(job)][:, c * T:(c + 1) * T], w[:, k, c * P:(c + 1) * P], moving[:, k, :],
                           start=k == 0, stop=k == KT - 1)
    mm.then_inc(B.full(job), 1)


def project_rows(pe, B, U, ps, ring, jobs, units, held):
    for u, unit in enumerate(units):
        pe.wait_ge(*U.landed(unit))
        w = ring[U.slot(unit)].rearrange("p (k n) -> p k n", k=KT // 2)
        for t in range(TT):
            if u == 0:
                B.claim(pe, jobs[t])
            for k in range(KT // 2):
                kk = u * (KT // 2) + k
                mm = pe.matmul(ps[B.bank(jobs[t])][:], held[:, kk, t * P:(t + 1) * P], w[:, k, :],
                               start=kk == 0, stop=kk == KT - 1)
            if u == 1:
                mm.then_inc(B.full(jobs[t]), 1)
            elif t == TT - 1:
                mm.then_inc(U.parts_sem, 1)


def load_units(sp, U, ring, source, landed=None, last_turn=None):
    for i, name in enumerate(U.names):
        if i >= SLOTS:
            sp.wait_ge(*U.given_back(U.names[i - SLOTS]))
        elif i == 0 and last_turn is not None:
            sp.wait_ge(*last_turn)
        sp.dma_start(ring[i % SLOTS], source(i)).then_inc(U.landed_sems[i % SLOTS], 16)



def first_scalar(act, step, m, ps, B, F):
    act.wait_ge(F.sem("x_in"), 16)
    square_sums(act, m.x, m.xn, m.ss, lambda: F["n1.ss"])
    act.wait_ge(F.sem("params"), 32)
    take_columns(act, B, [f"n1.{i}" for i in range(4)], ps, m.hT, m.p["g1"], 1)
    for name in ("v", "qd", "kd", "vd"):
        for i in range(2):
            job = f"{name}.{i}"
            act.wait_ge(*B.filled(job))
            act.activation(m.cols[name][:, 2 * i:2 * i + 2, :], split(ps[B.bank(job)][:], 2),
                           ACT.Copy).then_inc(B.free(job), 1)
    for i in range(2):
        act.wait_ge(*B.filled(f"z.{i}"))
        act.activation(m.ez[:, 2 * i:2 * i + 2, :], split(ps[B.bank(f"z.{i}")][:], 2), ACT.Exp,
                       scale=-1.0).then_inc(B.free(f"z.{i}"), 1)
    act.wait_ge(*F.at("conv", 4))
    act.activation(m.ec, m.cv, ACT.Exp, scale=-1.0).then_inc(F["conv_exp"], 1)
    act.wait_ge(*F.at("lam_dots", 2))
    act.activation(m.lam[:, 2:4], m.lam[:, 0:2], ACT.Exp).then_inc(F["lam_exp"], 1)
    for t in range(TT):
        for h in range(H1):
            for c in range(2):
                n = (t * 2 + c) * H1 + h
                act.wait_ge(*F.at("ds_max", 2 if t == 0 else 2 + 2 * (h // 2) + c + 1))
                s = m.dp[t][:, c, h, :]
                act.activation(s, s, ACT.Exp, bias=m.dmax[:, n:n + 1],
                               accum_out=m.dsum[:, n:n + 1]).then_inc(F["ds_exp"], 1)
    for name, dst in (("mq", m.mq), ("mk", m.mk)):
        for i in range(2):
            job = f"{name}.{i}"
            act.wait_ge(*B.filled(job))
            act.activation(dst[:, 2 * i:2 * i + 2, :], split(ps[B.bank(job)][:], 2),
                           ACT.Copy).then_inc(B.free(job), 1)
    act.wait_ge(*F.at("absf"))
    step(act.activation(m.frow[1][0:4, :], m.frow[1][0:4, :], ACT.Exp, scale=-1.0))
    act.activation(m.frow[1][0:4, :], m.frow[1][0:4, :], ACT.Ln, bias=1.0).then_inc(F["softplus"], 1)
    act.wait_ge(*B.drained("gcol"))
    act.activation(m.em, m.gcol[:, 8:16], ACT.Exp, scale=-1.0).then_inc(F["em"], 1)
    for h in range(H1):
        act.wait_ge(*B.drained(f"bc.{h // 2}"))
        for st, lo, hi in ((0, 0, T), (1, T, T + P)):
            e = m.me[:, h, lo:hi]
            act.activation(e, e, ACT.Exp, bias=m.gcol[:, st * 4 + h:st * 4 + h + 1]).then_inc(F["me"], 1)
    act.wait_ge(*F.at("h_centred"))
    act.activation(m.hsq, m.hm, ACT.Square).then_inc(F["h_sq"], 1)
    for t in range(TT):
        act.wait_ge(*B.filled(f"dout.{t}"))
        act.activation(m.yd[:, t, :], ps[B.bank(f"dout.{t}")][:], ACT.Copy).then_inc(B.free(f"dout.{t}"), 1)
    act.wait_ge(*B.drained("dout.1"))
    act.wait_ge(*F.at("h_var"))
    act.activation(m.hsq, m.yd, ACT.Square).then_inc(F["d_sq"], 1)
    for n in range(2):
        for t in range(TT):
            act.wait_ge(*B.drained(f"out.{n}.{t}"))
    square_sums(act, m.x, m.xn, m.ss, lambda: F["n2.ss"])
    take_columns(act, B, [f"n2.{i}" for i in range(4)], ps, m.hT, m.p["g2"], 1)
    act.wait_ge(*F.at("lg_max"))
    for t in range(TT):
        act.activation(m.r.eg[:, t, :], m.r.lg[:, t, 0:4], ACT.Exp, bias=m.r.nmg[:, t:t + 1],
                       accum_out=m.r.sg[:, t:t + 1]).then_inc(F["lg_exp"], 1)
    act.wait_ge(*F.at("le_diff"))
    act.activation(m.r.e2, m.r.e2, ACT.Exp).then_inc(F["le_exp"], 1)


def first_pool(pool, step, m, B, F):
    pool.memset(m.half, -0.5).then_inc(F["half"], 1)
    pool.wait_ge(*F.at("half"))
    pool.wait_ge(F.sem("params"), 32)
    pool.wait_ge(*F.at("n1.ss", 2))
    root_of_mean(pool, step, m.ss, m.c["eps"][:, 0:2], m.half[:, 0:2], F["n1.rstd"])
    pool.wait_ge(*F.at("h_var"))
    inverse_root(pool, step, m.hv, m.hv, m.half[:, 0:8], P, EPS, F["h_rstd"])
    pool.wait_ge(*F.at("d_var"))
    inverse_root(pool, step, m.dv, m.dv, m.half[:, 0:8], P, SUBLN_EPS, F["d_rstd"])
    pool.wait_ge(*F.at("n2.ss", 2))
    root_of_mean(pool, step, m.ss, m.c["eps"][:, 0:2], m.half[:, 0:2], F["n2.rstd"])


def first_vector(dve, step, m, ps, B, F):
    p = m.p
    dve.memset(m.cpad[:, :, 0:3], 0.0).then_inc(F["pad"], 1)
    dve.wait_ge(F.sem("params"), 32)
    for i in range(2):
        dve.tensor_tensor_reduce(m.lamj[:, i * 64:(i + 1) * 64], p["lam"][:, i * 128:i * 128 + 64],
                                 p["lam"][:, i * 128 + 64:i * 128 + 128], 1.0, 0.0, ALU.mult, ALU.add,
                                 m.lam[:, i:i + 1]).then_inc(F["lam_dots"], 1)
    dve.wait_ge(*F.at("n1.rstd"))
    dve.wait_ge(F.sem("x_in"), 16)
    for t in range(TT):
        dve.tensor_scalar(m.xn[:, t, :], m.x[:, t, :], m.ss[:, t:t + 1], None, ALU.mult).then_inc(F["n1.xn"], 1)
    take_columns(dve, B, [f"n1.{i}" for i in range(4)], ps, m.hT, p["g1"], 0)
    for i in range(2):
        dve.wait_ge(*B.filled(f"c.{i}"))
        dve.tensor_copy(m.cpad[:, 2 * i:2 * i + 2, 3:], split(ps[B.bank(f"c.{i}")][:], 2)).then_inc(B.free(f"c.{i}"), 1)
    dve.wait_ge(*B.drained("c.1"))
    dve.wait_ge(*F.at("pad"))
    for i in range(4):
        causal_conv(dve, step, m.cv[:, i, :], m.cpad[:, i, :], p["convw"][:, 4 * i:4 * i + 4],
                    p["convb"][:, i:i + 1], F["conv"])
    dve.wait_ge(*F.at("conv_exp"))
    silu_tail(dve, step, m.ec, m.cv, m.cv, F["cact"])
    for i in range(2):
        dve.wait_ge(*B.drained(f"z.{i}"))
    step(dve.tensor_scalar(m.ez, m.ez, 1.0, None, ALU.add))
    dve.reciprocal(m.ez, m.ez).then_inc(F["sig_z"], 1)
    for name, dst in (("vtok", m.vtok), ("vdtok", m.vdtok)):
        for t in range(TT):
            job = f"{name}.{t}"
            dve.wait_ge(*B.filled(job))
            dve.tensor_copy(dst[:, t, :], ps[B.bank(job)][:]).then_inc(B.free(job), 1)
    scale = 64 ** -0.5
    bias0 = p["bias"][:, 0:H1 * P].rearrange("p (h k) -> p h k", h=H1)
    bias1 = p["bias"][:, H1 * P:].rearrange("p (h k) -> p h k", h=H1)
    for c in range(2):
        job = f"ds0.{c}"
        dve.wait_ge(*B.filled(job))
        dve.scalar_tensor_tensor(out=m.dp[0][:, c, :, :], in0=split(ps[B.bank(job)][:], 4), scalar=scale,
                                 in1=bias0, op0=ALU.mult, op1=ALU.add).then_inc(B.free(job), 1)
        dve.wait_ge(*B.drained(job))
        dve.tensor_reduce(m.dmax[:, c * 4:c * 4 + 4], m.dp[0][:, c, :, :], AX.X, ALU.max,
                          negate=True).then_inc(F["ds_max"], 1)
    for hp in range(2):
        for c in range(2):
            job = f"ds1.{hp}.{c}"
            dve.wait_ge(*B.filled(job))
            dst = m.dp[1][:, c, 2 * hp:2 * hp + 2, :]
            dve.scalar_tensor_tensor(out=dst, in0=split(ps[B.bank(job)][:], 2), scalar=scale,
                                     in1=bias1[:, 2 * hp:2 * hp + 2, :], op0=ALU.mult,
                                     op1=ALU.add).then_inc(B.free(job), 1)
            dve.wait_ge(*B.drained(job))
            n = 8 + c * 4 + 2 * hp
            dve.tensor_reduce(m.dmax[:, n:n + 2], dst, AX.X, ALU.max, negate=True).then_inc(F["ds_max"], 1)
    dve.wait_ge(*B.filled("gates"))
    gate = ps[B.bank("gates")]
    irow, row1, row2, frow, neg_m, bm = m.frow
    dve.tensor_scalar(irow[0:4, :], gate[0:4, 0:T], p["bi"][0:4, :], None, ALU.add).then_inc(F["irow"], 1)
    dve.tensor_scalar(frow[0:4, :], gate[0:4, T:2 * T], p["bf"][0:4, :], None, ALU.add).then_inc(B.free("gates"), 1)
    dve.wait_ge(*B.drained("gates"))
    magnitude(dve, row1[0:4, :], frow[0:4, :]).then_inc(F["absf"], 1)
    dve.tensor_scalar(row2[0:4, :], frow[0:4, :], 0.0, None, ALU.min).then_inc(F["minf"], 1)
    dve.wait_ge(*F.at("softplus"))
    dve.wait_ge(*F.at("minf"))
    step(dve.tensor_tensor(frow[0:4, :], row2[0:4, :], row1[0:4, :], ALU.subtract))
    step(dve.tensor_tensor_scan(row2[0:4, :], m.c["ones"][0:4, :], frow[0:4, :], 0.0, ALU.mult, ALU.add))
    dve.wait_ge(*F.at("irow"))
    step(dve.tensor_tensor(irow[0:4, :], irow[0:4, :], row2[0:4, :], ALU.subtract))
    step(dve.tensor_tensor_scan(row1[0:4, :], irow[0:4, :], irow[0:4, :], 0.0, ALU.max, ALU.max))
    dve.tensor_scalar(neg_m[0:4, :], row1[0:4, :], -1.0, None, ALU.mult).then_inc(F["rows"], 1)
    dve.tensor_tensor(bm[0:4, :], row1[0:4, :], row2[0:4, :], ALU.add).then_inc(F["rows"], 1)
    dve.wait_ge(*B.filled("gcol"))
    dve.tensor_copy(m.gcol, ps[B.bank("gcol")][:, 0:16]).then_inc(B.free("gcol"), 1)
    for i in range(2):
        job = f"bc.{i}"
        dve.wait_ge(*B.filled(job))
        spread_and_mask(dve, split(ps[B.bank(job)][:], 2), m.me[:, 2 * i:2 * i + 2, :], m.c["mask"], B.free(job))
    dve.wait_ge(*F.at("lam_exp"))
    step(dve.tensor_tensor(m.lam[:, 4:5], m.lam[:, 3:4], m.lam[:, 2:3], ALU.subtract))
    step(dve.tensor_scalar(m.lam[:, 4:5], m.lam[:, 4:5], -LAM_INIT, None, ALU.add))
    dve.wait_ge(*F.at("ds_exp", 16))
    step(dve.reciprocal(m.dsum, m.dsum))
    for t in range(TT):
        o = t * 8 + 4
        step(dve.tensor_scalar(m.dsum[:, o:o + 4], m.dsum[:, o:o + 4], m.lam[:, 4:5], None, ALU.mult))
    for t in range(TT):
        for c in range(2):
            r = m.dsum[:, t * 8 + c * 4:t * 8 + c * 4 + 4]
            step(dve.tensor_tensor(m.dp[t][:, c, :, :], m.dp[t][:, c, :, :], bc(r, [P, H1, (t + 1) * P]), ALU.mult))
        dve.tensor_tensor(m.dp[t][:, 0, :, :], m.dp[t][:, 0, :, :], m.dp[t][:, 1, :, :], ALU.add).then_inc(F["da"], 1)
    for h in range(H1):
        dve.wait_ge(*F.at("me", 2 * h + 2))
        dve.wait_ge(*B.filled(f"ms.{h}"))
        dve.scalar_tensor_tensor(out=m.me[:, h, :], in0=ps[B.bank(f"ms.{h}")][:, 0:3 * P], scalar=P ** -0.5,
                                 in1=m.me[:, h, :], op0=ALU.mult, op1=ALU.mult).then_inc(B.free(f"ms.{h}"), 1)
    for i in range(3):
        job = f"daT.{i}"
        dve.wait_ge(*B.filled(job))
        dve.tensor_copy(m.daT[:, i, :], ps[B.bank(job)][:]).then_inc(B.free(job), 1)
    dve.wait_ge(*F.at("em"))
    dve.wait_ge(*B.filled("den"))
    dve.tensor_copy(m.den, ps[B.bank("den")][:, 0:8]).then_inc(B.free("den"), 1)
    dve.wait_ge(*B.drained("den"))
    step(magnitude(dve, m.den, m.den))
    step(dve.tensor_tensor(m.den, m.den, m.em, ALU.max))
    step(dve.reciprocal(m.den, m.den))
    for t in range(TT):
        job = f"num.{t}"
        dve.wait_ge(*B.filled(job))
        dve.tensor_tensor(m.hm[:, 4 * t:4 * t + 4, :], split(ps[B.bank(job)][:], 4),
                          bc(m.den[:, 4 * t:4 * t + 4], [P, 4, P]), ALU.mult).then_inc(B.free(job), 1)
        dve.wait_ge(*B.drained(job))
    centre(dve, step, m.hm, m.hv, P, F["h_centred"])
    dve.wait_ge(*F.at("h_sq"))
    dve.tensor_reduce(m.hv, m.hsq, AX.X, ALU.add).then_inc(F["h_var"], 1)
    dve.wait_ge(*F.at("h_rstd"))
    dve.tensor_tensor(m.hm, m.hm, bc(m.hv, [P, 8, P]), ALU.mult).then_inc(F["hn"], 1)
    for h in range(H1):
        step(dve.tensor_scalar(m.cv[:, h, :], m.cv[:, h, :], p["mskip"][:, h:h + 1], None, ALU.mult))
    for i in range(2):
        job = f"hT.{i}"
        dve.wait_ge(*B.filled(job))
        for k in range(2):
            h = 2 * i + k
            ins = dve.scalar_tensor_tensor(out=m.yT[:, h, :], in0=ps[B.bank(job)][:, k * T:(k + 1) * T],
                                           scalar=p["mnorm"][:, h:h + 1], in1=m.cv[:, h, :], op0=ALU.mult,
                                           op1=ALU.add)
        ins.then_inc(B.free(job), 1)
        dve.wait_ge(*B.drained(job))
    dve.wait_ge(*F.at("sig_z"))
    dve.tensor_tensor(m.yT[:, 0:4, :], m.yT[:, 0:4, :], m.ez, ALU.mult).then_inc(F["ym"], 1)
    dve.wait_ge(*F.at("d_sq"))
    dve.tensor_reduce(m.dv, m.hsq, AX.X, ALU.add).then_inc(F["d_var"], 1)
    dve.wait_ge(*F.at("d_rstd"))
    dve.tensor_tensor(m.ydh, m.ydh, bc(m.dv, [P, 8, P]), ALU.mult).then_inc(F["dn"], 1)
    for i in range(2):
        job = f"ydT.{i}"
        dve.wait_ge(*B.filled(job))
        dve.tensor_scalar(m.yT[:, 4 + 2 * i:6 + 2 * i, :], split(ps[B.bank(job)][:], 2), p["danorm"], 1.0 - LAM_INIT,
                          ALU.mult, ALU.mult).then_inc(B.free(job), 1)
    for n in range(2):
        for t in range(TT):
            job = f"out.{n}.{t}"
            dve.wait_ge(*B.filled(job))
            xs = m.x[:, t, n * 512:(n + 1) * 512]
            dve.tensor_tensor(xs, xs, ps[B.bank(job)][:], ALU.add).then_inc(B.free(job), 1)
    dve.wait_ge(*F.at("n2.rstd"))
    for t in range(TT):
        dve.tensor_scalar(m.xn[:, t, :], m.x[:, t, :], m.ss[:, t:t + 1], None, ALU.mult).then_inc(F["n2.xn"], 1)
    take_columns(dve, B, [f"n2.{i}" for i in range(4)], ps, m.hT, p["g2"], 0)
    route_vector(dve, step, m, ps, B, F)


def magnitude(dve, out, x):
    return dve.scalar_tensor_tensor(out=out, in0=x, scalar=-1.0, in1=x, op0=ALU.mult, op1=ALU.max)


def causal_conv(dve, step, out, padded, w, b, flag):
    step(dve.tensor_scalar(out, padded[:, 0:T], w[:, 0:1], b, ALU.mult, ALU.add))
    for j in range(1, 4):
        ins = dve.scalar_tensor_tensor(out=out, in0=padded[:, j:j + T], scalar=w[:, j:j + 1], in1=out,
                                       op0=ALU.mult, op1=ALU.add)
        if j < 3:
            step(ins)
    ins.then_inc(flag, 1)


def silu_tail(dve, step, e, x, out, flag):
    step(dve.tensor_scalar(e, e, 1.0, None, ALU.add))
    step(dve.reciprocal(e, e))
    dve.tensor_tensor(out, x, e, ALU.mult).then_inc(flag, 1)


def spread_and_mask(dve, bank, out, mask, flag):
    both = mask.unsqueeze(1).to_broadcast([P, 2, P])
    dve.tensor_tensor(out[:, :, 0:P], bank[:, :, 0:P], both, ALU.add)
    dve.tensor_copy(out[:, :, P:T], bank[:, :, P:T])
    dve.tensor_tensor(out[:, :, T:T + P], bank[:, :, P:T], both, ALU.add).then_inc(flag, 1)


def centre(dve, step, x, stat, width, flag):
    step(dve.tensor_reduce(stat, x, AX.X, ALU.add, negate=True))
    step(dve.tensor_scalar(stat, stat, 1.0 / width, None, ALU.mult))
    dve.tensor_tensor(x, x, bc(stat, list(x.shape)), ALU.add).then_inc(flag, 1)


def first_tensor(pe, m, ps, B, U, F):
    ident = m.c["ident"]
    ring = m.ring
    pe.wait_ge(F.sem("params"), 32)
    turn_rows(pe, B, [f"n1.{i}" for i in range(4)], ps, m.xn, ident, F, "n1")
    wait_columns(pe, B, [f"n1.{i}" for i in range(4)])
    for name in ("c", "v", "qd", "kd", "vd", "z"):
        for i in range(2):
            project_columns(pe, B, U, ps, ring, f"{name}.{i}", f"{name}.{i}", m.hT)
    for name, src in (("vtok", "v"), ("vdtok", "vd")):
        for i in range(2):
            pe.wait_ge(*B.drained(f"{src}.{i}"))
        for t in range(TT):
            job = f"{name}.{t}"
            B.claim(pe, job)
            for h in range(H1):
                mm = pe.transpose(ps[B.bank(job)][:, h * P:(h + 1) * P], m.cols[src][:, h, t * P:(t + 1) * P], ident)
            mm.then_inc(B.full(job), 1)
    for i in range(2):
        pe.wait_ge(*B.drained(f"kd.{i}"))
    qd, kd = m.cols["qd"], m.cols["kd"]
    for c in range(2):
        job = f"ds0.{c}"
        B.claim(pe, job)
        for h in range(H1):
            mm = pe.matmul(ps[B.bank(job)][:, h * P:(h + 1) * P], qd[c * 64:c * 64 + 64, h, 0:P],
                           kd[c * 64:c * 64 + 64, h, 0:P], start=True, stop=True)
        mm.then_inc(B.full(job), 1)
    for hp in range(2):
        for c in range(2):
            job = f"ds1.{hp}.{c}"
            B.claim(pe, job)
            for k in range(2):
                h = 2 * hp + k
                mm = pe.matmul(ps[B.bank(job)][:, k * T:(k + 1) * T], qd[c * 64:c * 64 + 64, h, P:T],
                               kd[c * 64:c * 64 + 64, h, :], start=True, stop=True)
            mm.then_inc(B.full(job), 1)
    pe.wait_ge(*F.at("cact"))
    for name, w in (("mq", m.p["wmq"]), ("mk", m.p["wmk"])):
        for i in range(2):
            job = f"{name}.{i}"
            B.claim(pe, job)
            for k in range(2):
                h = 2 * i + k
                mm = pe.matmul(ps[B.bank(job)][:, k * T:(k + 1) * T], w[:, h * P:(h + 1) * P], m.cv[:, h, :],
                               start=True, stop=True)
            mm.then_inc(B.full(job), 1)
    for i in range(2):
        pe.wait_ge(*B.drained(f"mq.{i}"))
        pe.wait_ge(*B.drained(f"mk.{i}"))
    B.claim(pe, "gates")
    wgate = m.p["wgate"].rearrange("p (k n) -> p k n", k=12)
    for half in range(2):
        for k in range(12):
            src = (m.mq, m.mk, m.cols["v"])[k // 4]
            mm = pe.matmul(ps[B.bank("gates")][0:4, half * T:(half + 1) * T], wgate[:, k, half * 4:half * 4 + 4],
                           src[:, k % 4, :], start=k == 0, stop=k == 11)
    mm.then_inc(B.full("gates"), 1)
    for h in range(H1):
        causal_scores(pe, B, ps, f"ms.{h}", m.mk[:, h, :], m.mq[:, h, :])
    pe.wait_ge(*F.at("rows", 2))
    B.claim(pe, "gcol")
    for half, row in enumerate((m.frow[0], m.frow[5])):
        for t in range(TT):
            o = half * 8 + t * 4
            mm = pe.transpose(ps[B.bank("gcol")][:, o:o + 4], row[0:4, t * P:(t + 1) * P], ident[0:4, 0:4])
    mm.then_inc(B.full("gcol"), 1)
    for i in range(2):
        spread_rows(pe, B, ps, f"bc.{i}", m.frow[4], ident, 4, 2 * i)
    for i in range(3):
        job = f"daT.{i}"
        B.claim(pe, job)
        pe.wait_ge(*F.at("da", 1 if i == 0 else 2))
        for k in range(4):
            src = m.dp[0][:, 0, k, :] if i == 0 else m.dp[1][:, 0, 2 * (i - 1) + k // 2, (k % 2) * P:(k % 2 + 1) * P]
            mm = pe.transpose(ps[B.bank(job)][:, k * P:(k + 1) * P], src, ident)
        mm.then_inc(B.full(job), 1)
    for h in range(H1):
        pe.wait_ge(*B.drained(f"ms.{h}"))
    for t in range(TT):
        pe.wait_ge(*B.drained(f"vtok.{t}"))
    for t in range(TT):
        job = f"num.{t}"
        B.claim(pe, job)
        for h in range(H1):
            for s in range(t + 1):
                w = m.me[:, h, (t + s) * P:(t + s + 1) * P]
                mm = pe.matmul(ps[B.bank(job)][:, h * P:(h + 1) * P], w, m.vtok[:, s, h * P:(h + 1) * P],
                               start=s == 0, stop=s == t)
        mm.then_inc(B.full(job), 1)
    B.claim(pe, "den")
    for t in range(TT):
        for h in range(H1):
            for s in range(t + 1):
                w = m.me[:, h, (t + s) * P:(t + s + 1) * P]
                mm = pe.matmul(ps[B.bank("den")][:, t * 4 + h:t * 4 + h + 1], w, m.c["ones"][:, 0:1],
                               start=s == 0, stop=s == t)
    mm.then_inc(B.full("den"), 1)
    for i in range(3):
        pe.wait_ge(*B.drained(f"daT.{i}"))
    for t in range(TT):
        pe.wait_ge(*B.drained(f"vdtok.{t}"))
    for t in range(TT):
        job = f"dout.{t}"
        B.claim(pe, job)
        for h in range(H1):
            for s in range(t + 1):
                w = m.daT[:, 0, h * P:(h + 1) * P] if t == 0 else \
                    m.daT[:, 1 + h // 2, ((h % 2) * 2 + s) * P:((h % 2) * 2 + s + 1) * P]
                mm = pe.matmul(ps[B.bank(job)][:, h * P:(h + 1) * P], w, m.vdtok[:, s, h * P:(h + 1) * P],
                               start=s == 0, stop=s == t)
        mm.then_inc(B.full(job), 1)
    for name, src, ready in (("hT", m.hm, "hn"), ("ydT", m.ydh, "dn")):
        pe.wait_ge(*F.at(ready))
        for i in range(2):
            job = f"{name}.{i}"
            B.claim(pe, job)
            for k in range(2):
                for t in range(TT):
                    mm = pe.transpose(ps[B.bank(job)][:, k * T + t * P:k * T + t * P + P],
                                      src[:, t * 4 + 2 * i + k, :], ident)
            mm.then_inc(B.full(job), 1)
    pe.wait_ge(*F.at("ym"))
    for i in range(2):
        pe.wait_ge(*B.drained(f"ydT.{i}"))
    for n in range(2):
        project_rows(pe, B, U, ps, ring, [f"out.{n}.{t}" for t in range(TT)], [f"out.{n}.{i}" for i in range(2)], m.yT)
    turn_rows(pe, B, [f"n2.{i}" for i in range(4)], ps, m.xn, ident, F, "n2")
    wait_columns(pe, B, [f"n2.{i}" for i in range(4)])
    route_tensor(pe, m, ps, B, F)


def causal_scores(pe, B, ps, job, keys, queries):
    B.claim(pe, job)
    bank = ps[B.bank(job)]
    pe.matmul(bank[:, 0:T], keys[:, 0:P], queries, start=True, stop=True)
    pe.matmul(bank[:, T:T + P], keys[:, P:T], queries[:, P:T], start=True, stop=True).then_inc(B.full(job), 1)


def spread_rows(pe, B, ps, job, rows, ident, n, first):
    B.claim(pe, job)
    for k in range(2):
        mm = pe.matmul(ps[B.bank(job)][:, k * T:(k + 1) * T], ident[0:n, first + k:first + k + 1].to_broadcast([n, P]),
                       rows[0:n, :], start=True, stop=True)
    mm.then_inc(B.full(job), 1)



def route_tensor(pe, m, ps, B, F):
    wroute = m.p["wroute"].rearrange("p (k n) -> p k n", k=KT)
    B.claim(pe, "route")
    for t in range(TT):
        for k in range(KT):
            mm = pe.matmul(ps[B.bank("route")][:, t * 36:(t + 1) * 36], m.hT[:, k, t * P:(t + 1) * P], wroute[:, k, :],
                           start=k == 0, stop=k == KT - 1)
    mm.then_inc(B.full("route"), 1)
    pe.wait_ge(*F.at("chosen"))
    B.claim(pe, "rank")
    bank, chosen, before, ones = ps[B.bank("rank")], m.r.chosen, m.c["before"], m.c["ones"][:, 0:P]
    pe.matmul(bank[:, 0:32], before, chosen[:, 0, :], start=True, stop=True)
    pe.matmul(bank[:, 32:64], ones, chosen[:, 0, :], start=True, stop=False)
    pe.matmul(bank[:, 32:64], before, chosen[:, 1, :], start=False, stop=True)
    pe.matmul(bank[:, 64:96], ones, chosen[:, 0, :], start=True, stop=False)
    pe.matmul(bank[:, 64:96], ones, chosen[:, 1, :], start=False, stop=True).then_inc(B.full("rank"), 1)


def first_of(dve, step, values, best, prior, out):
    n = values.shape[2]
    step(dve.tensor_tensor(out, values, bc(best, [P, TT, n]), ALU.is_equal))
    step(dve.tensor_tensor(out, out, prior.unsqueeze(1).to_broadcast([P, TT, n]), ALU.mult))
    step(dve.tensor_reduce(best, out, AX.X, ALU.max))
    step(dve.tensor_tensor(out, out, bc(best, [P, TT, n]), ALU.is_equal))


def route_vector(dve, step, m, ps, B, F):
    r = m.r
    dve.wait_ge(*B.filled("route"))
    bank = ps[B.bank("route")][:, 0:72].rearrange("p (t n) -> p t n", t=TT)
    dve.tensor_tensor(r.lg, bank, m.p["broute"].unsqueeze(1).to_broadcast([P, TT, 36]),
                      ALU.add).then_inc(B.free("route"), 1)
    dve.wait_ge(*B.drained("route"))
    step(dve.tensor_reduce(r.best, r.lg[:, :, 0:4], AX.X, ALU.max))
    dve.tensor_scalar(r.nmg, r.best, -1.0, None, ALU.mult).then_inc(F["lg_max"], 1)
    first_of(dve, step, r.lg[:, :, 0:4], r.best, m.c["prior4"], r.group)
    for t in range(TT):
        step(dve.tensor_tensor(r.by_group[:, t], r.lg[:, t, 4:36].rearrange("p (g j) -> p g j", g=GROUPS),
                               bc(r.group[:, t, :], [P, GROUPS, PER_GROUP]), ALU.mult))
        step(dve.tensor_reduce(r.le[:, t, :], r.by_group[:, t].rearrange("p g j -> p j g"), AX.X, ALU.add))
    step(dve.tensor_reduce(r.best, r.le, AX.X, ALU.max))
    step(dve.tensor_scalar(r.e2, r.best, -1.0, None, ALU.mult))
    first_of(dve, step, r.le, r.best, m.c["prior8"], r.hot1)
    step(dve.scalar_tensor_tensor(out=r.le, in0=r.hot1, scalar=NEG, in1=r.le, op0=ALU.mult, op1=ALU.add))
    step(dve.tensor_reduce(r.best, r.le, AX.X, ALU.max))
    dve.tensor_tensor(r.e2, r.e2, r.best, ALU.add).then_inc(F["le_diff"], 1)
    first_of(dve, step, r.le, r.best, m.c["prior8"], r.hot2)
    step(dve.tensor_tensor(r.le, r.hot1, r.hot2, ALU.add))
    for t in range(TT):
        ins = dve.tensor_tensor(r.chosen[:, t, :].rearrange("p (g j) -> p g j", g=GROUPS),
                                bc(r.group[:, t, :], [P, GROUPS, PER_GROUP]),
                                r.le[:, t, :].unsqueeze(1).to_broadcast([P, GROUPS, PER_GROUP]), ALU.mult)
    ins.then_inc(F["chosen"], 1)
    dve.wait_ge(*F.at("lg_exp", 2))
    dve.wait_ge(*F.at("le_exp"))
    step(dve.tensor_scalar(r.w1, r.e2, 1.0, None, ALU.add))
    step(dve.tensor_tensor(r.sg, r.sg, r.w1, ALU.mult))
    step(dve.reciprocal(r.w1, r.sg))
    step(dve.tensor_tensor(r.w2, r.e2, r.w1, ALU.mult))
    step(dve.tensor_tensor(r.hot1, r.hot1, bc(r.w1, [P, TT, PER_GROUP]), ALU.mult))
    step(dve.tensor_tensor(r.hot2, r.hot2, bc(r.w2, [P, TT, PER_GROUP]), ALU.mult))
    step(dve.tensor_tensor(r.hot1, r.hot1, r.hot2, ALU.add))
    step(dve.memset(r.gates[:, :, PASSES * EXPERTS:], 0.0))
    step(dve.memset(r.ranks[:, :, PASSES * EXPERTS:], -1.0))
    for t in range(TT):
        for q in range(PASSES):
            dve.tensor_tensor(r.gates[:, t, q * EXPERTS:(q + 1) * EXPERTS].rearrange("p (g j) -> p g j", g=GROUPS),
                              bc(r.group[:, t, :], [P, GROUPS, PER_GROUP]),
                              r.hot1[:, t, :].unsqueeze(1).to_broadcast([P, GROUPS, PER_GROUP]), ALU.mult)
    dve.wait_ge(*B.filled("rank"))
    bank = ps[B.bank("rank")]
    step(dve.scalar_tensor_tensor(out=r.rank, in0=bank[:, 0:64].rearrange("p (t e) -> p t e", t=TT), scalar=1.0,
                                  in1=r.chosen, op0=ALU.add, op1=ALU.mult))
    dve.tensor_reduce(r.most, bank[:, 64:96], AX.X, ALU.max).then_inc(B.free("rank"), 1)
    dve.wait_ge(*B.drained("rank"))
    for q in range(PASSES):
        step(dve.tensor_scalar(r.ranks[:, :, q * EXPERTS:(q + 1) * EXPERTS], r.rank, -1.0 - q * CAP, None, ALU.add))
    step(dve.tensor_scalar(r.passes[:, 0:1], r.most, float(CAP), 1.0, ALU.is_gt, ALU.add))
    for q in range(2, PASSES):
        step(dve.tensor_scalar(r.passes[:, 1:2], r.most, float(q * CAP), None, ALU.is_gt))
        step(dve.tensor_tensor(r.passes[:, 0:1], r.passes[:, 0:1], r.passes[:, 1:2], ALU.add))
    step(dve.tensor_copy(r.turns_i[:, 0:1], r.passes[:, 0:1]))
    step(dve.tensor_scalar(r.passes[:, 1:2], r.passes[:, 0:1], float(PAIRS), None, ALU.mult))
    dve.tensor_copy(r.turns_i[:, 1:2], r.passes[:, 1:2]).then_inc(F["passes"], 1)


GATE, UP, GATHER, TURN, SUM, DOWN = 0, 1, 2, 4, 5, 6
EXPERT_UNITS = [(e, w, h) for w in range(3) for h in range(2) for e in range(2)]
LOADS = len(EXPERT_UNITS)
GROUPS_USED = LOADS // 2


def moe_select(dve, m, out, turn):
    cols = m.r.ranks[:, :, bass.ds(turn * 2, 2)]
    o = out.rearrange("p t (e s) -> p t e s", e=2)
    for t in range(TT):
        ins = dve.tensor_tensor(o[:, t], m.c["slot"].rearrange("p (e s) -> p e s", e=2),
                                bc(cols[:, t, :], [P, 2, CAP]), ALU.is_equal)
    return ins


AHEAD = {"vector": ("hidden", "added"), "scalar": ("rows",), "tensor": ("turned", "hid_turned", "summed")}


def since(n):
    return n + 1


def raise_ahead(engine, M, name):
    for n in AHEAD[name]:
        engine.sem_inc(M[n], 1)


def moe_vector(dve, m, ps, M):
    r = m.r
    raise_ahead(dve, M, "vector")
    turns = dve.value_load(r.turns_i[0:1, 1:2], min_val=PAIRS, max_val=PAIRS * PASSES)
    moe_select(dve, m, m.sel, 0).then_inc(M["sel"], 1)
    for g in range(2):
        dve.wait_ge(M["gathered"], g + 1)
        gather_columns(dve, m, ps, g).then_inc(M["columns"], 1)
    with dve.Fori(0, turns) as i:
        dve.wait_ge(M["gathered"], i * 2 + 2)
        moe_select(dve, m, m.sel, i + 1).then_inc(M["sel"], 1)
        dve.wait_ge(M["turned"], since(i))
        moe_select(dve, m, m.selg, i).then_inc(M["selg1"], 1)
        dve.wait_ge(M["selg1"], i + 1)
        for t in range(TT):
            o = m.selg[:, t].rearrange("p (e s) -> p e s", e=2)
            ins = dve.tensor_tensor(o, o, bc(r.gates[:, t, bass.ds(i * 2, 2)], [P, 2, CAP]), ALU.mult)
        ins.then_inc(M["selg"], 1)
        dve.wait_ge(M["gate_exp"], i + 1)
        dve.tensor_scalar(m.eg, m.eg, 1.0, None, ALU.add).then_inc(M["silu"], 1)
        dve.wait_ge(M["silu"], i * 3 + 1)
        dve.reciprocal(m.eg, m.eg).then_inc(M["silu"], 1)
        dve.wait_ge(M["silu"], i * 3 + 2)
        dve.tensor_tensor(m.eg, m.eg, ps[GATE][:], ALU.mult).then_inc(M["silu"], 1)
        dve.wait_ge(M["silu"], i * 3 + 3)
        dve.wait_ge(M["used"], (i + 1) * GROUPS_USED + 4)
        dve.wait_ge(M["hid_turned"], since(i))
        dve.tensor_tensor(m.hid, m.eg, ps[UP][:], ALU.mult).then_inc(M["hidden"], 1)
        for g in range(2):
            dve.wait_ge(M["gathered"], i * 2 + 3 + g)
            gather_columns(dve, m, ps, g).then_inc(M["columns"], 1)
        for q in range(4):
            t, n = q // 2, q % 2
            dve.wait_ge(M["summed"], since(i * 4 + q + 1))
            xs = m.x[:, t, n * 512:(n + 1) * 512]
            dve.tensor_tensor(xs, xs, ps[(SUM, TURN)[q % 2]][:], ALU.add).then_inc(M["added"], 1)


def gather_columns(dve, m, ps, g):
    return dve.tensor_tensor(m.hc[:, 4 * g:4 * g + 4, :], split(ps[GATHER + g][:], 4),
                             bc(m.gcols[:, 4 * g:4 * g + 4], [P, 4, P]), ALU.mult)


def moe_scalar(act, m, ps, M):
    raise_ahead(act, M, "scalar")
    turns = act.value_load(m.r.turns_i[0:1, 1:2], min_val=PAIRS, max_val=PAIRS * PASSES)
    with act.Fori(0, turns) as i:
        act.wait_ge(M["used"], (i + 1) * GROUPS_USED + 2)
        act.wait_ge(M["hidden"], since(i))
        act.activation(m.eg, ps[GATE][:], ACT.Exp, scale=-1.0).then_inc(M["gate_exp"], 1)
        act.wait_ge(M["turned"], since(i + 1))
        act.wait_ge(M["summed"], since(i * 4))
        act.activation(m.selgT, ps[TURN][:, 0:T], ACT.Copy).then_inc(M["selgT"], 1)
        act.wait_ge(M["hid_turned"], since(i + 1))
        act.activation(m.hidT, ps[TURN][:], ACT.Copy).then_inc(M["hidT"], 1)
        act.wait_ge(M["used"], (i + 1) * GROUPS_USED + 6)
        for n in range(2):
            act.activation(m.ym[:, n * 512:(n + 1) * 512], ps[DOWN + n][:], ACT.Copy).then_inc(M["rows"], 1)


def moe_gather(pe, m, ps, M):
    for g in range(2):
        for k in range(4):
            kk = 4 * g + k
            for t in range(TT):
                mm = pe.matmul(ps[GATHER + g][:, k * P:(k + 1) * P], m.xn[:, t, kk * P:(kk + 1) * P], m.sel[:, t, :],
                               start=t == 0, stop=t == TT - 1)
        mm.then_inc(M["gathered"], 1)


def moe_tensor(pe, m, ps, M, landed, base):
    ident = m.c["ident"]
    raise_ahead(pe, M, "tensor")
    turns = pe.value_load(m.r.turns_i[0:1, 1:2], min_val=PAIRS, max_val=PAIRS * PASSES)
    pe.wait_ge(M["sel"], 1)
    moe_gather(pe, m, ps, M)

    def unit(i, u):
        s = u % SLOTS
        pe.wait_ge(landed[s], (i * 2 + (base[s] + u // SLOTS + 1)) * 16)
        return m.ring[s]

    with pe.Fori(0, turns) as i:
        pe.wait_ge(M["columns"], i * 2 + 2)
        pe.wait_ge(M["hidden"], since(i))
        for w, bank in ((0, GATE), (1, UP)):
            for h in range(2):
                both = [unit(i, w * 4 + h * 2 + e).rearrange("p (k n) -> p k n", k=4) for e in range(2)]
                for k in range(4):
                    for e in range(2):
                        mm = pe.matmul(ps[bank][e * 64:e * 64 + 64, :], m.hc[:, h * 4 + k, e * 64:e * 64 + 64],
                                       both[e][:, k, :], start=h + k == 0, stop=h * 4 + k == 7)
                mm.then_inc(M["used"], 1)
        pe.wait_ge(M["selg"], i + 1)
        pe.wait_ge(M["added"], since(i * 4))
        for t in range(TT):
            mm = pe.transpose(ps[TURN][:, t * P:(t + 1) * P], m.selg[:, t, :], ident)
        mm.then_inc(M["turned"], 1)
        pe.wait_ge(M["sel"], i + 2)
        moe_gather(pe, m, ps, M)
        pe.wait_ge(M["hidden"], since(i + 1))
        pe.wait_ge(M["selgT"], i + 1)
        for f in range(4):
            mm = pe.transpose(ps[TURN][:, f * P:(f + 1) * P], m.hid[:, f * P:(f + 1) * P], ident)
        mm.then_inc(M["hid_turned"], 1)
        pe.wait_ge(M["hidT"], i + 1)
        pe.wait_ge(M["rows"], since(i * 2))
        for h in range(2):
            both = [unit(i, 8 + h * 2 + e).rearrange("p (f n) -> p f n", f=2) for e in range(2)]
            for f in range(2):
                ff = h * 2 + f
                for n in range(2):
                    for e in range(2):
                        mm = pe.matmul(ps[DOWN + n][e * 64:e * 64 + 64, :],
                                       m.hidT[:, ff * P + e * 64:ff * P + e * 64 + 64],
                                       both[e][:, f, n * 512:(n + 1) * 512], start=ff == 0, stop=ff == 3)
            mm.then_inc(M["used"], 1)
        pe.wait_ge(M["rows"], since(i * 2 + 2))
        for q in range(4):
            t, n = q // 2, q % 2
            if q >= 2:
                pe.wait_ge(M["added"], since(i * 4 + q - 1))
            pe.matmul(ps[(SUM, TURN)[q % 2]][:], m.selgT[:, t * P:(t + 1) * P], m.ym[:, n * 512:(n + 1) * 512],
                      start=True, stop=True).then_inc(M["summed"], 1)


def moe_loads(sp, m, M, landed, experts):
    sp.sem_inc(M["used"], GROUPS_USED)
    passes = sp.value_load(m.r.turns_i[0:1, 0:1], min_val=1, max_val=PASSES)
    with sp.Fori(0, passes) as q:
        with sp.Fori(0, PAIRS) as j:
            for u in range(LOADS):
                turn = q * PAIRS + j
                if u < SLOTS:
                    sp.wait_ge(M["used"], turn * GROUPS_USED + (u + SLOTS) // 2 + 1)
                else:
                    sp.wait_ge(M["used"], turn * GROUPS_USED + (GROUPS_USED + (u - SLOTS) // 2 + 1))
                sp.dma_start(m.ring[u % SLOTS], experts[bass.ds(j, 1), u]).then_inc(landed[u % SLOTS], 16)



BEFORE = {"f1": "f2", "mx": "f1", "f2": "mx"}



def passes_of(stationary, moving):
    return ((stationary[0], moving[0]), (stationary[0], moving[1]), (stationary[1], moving[0]))


def sofar(f, n):
    return n if f == "f2" else 0


def unit_hi(act, m, U, F, f, names, j):
    if j >= HI_BUFFERS:
        act.wait_ge(*U.given_back(names[j - HI_BUFFERS]))
    act.wait_ge(*U.landed(names[j]))
    act.activation(m.whi_r[j % HI_BUFFERS], m.ring[U.slot(names[j])], ACT.Copy).then_inc(F["ffn_hi"], 1)


def unit_lo(dve, m, U, F, f, names, j):
    slot = U.slot(names[j])
    dve.wait_ge(*F.at("ffn_hi", sofar(f, FT + FT // 2) + j + 1))
    dve.tensor_tensor(m.ring_r[slot], m.ring[slot], m.whi_r[j % HI_BUFFERS].bitcast(F32), ALU.subtract).then_inc(F["ffn_lo"], 1)


def ffn_unit_names(f):
    return [n for n, _ in ffn_units(f)]


def ffn_tensor(pe, m, ps, B, U, F, f):
    names = [f"{f}.n.{i}" for i in range(4)]
    units = ffn_unit_names(f)
    turn_rows(pe, B, names, ps, m.xn, m.c["ident"], F, f)
    wait_columns(pe, B, names)

    def parts(j, k):
        pe.wait_ge(*F.at("ffn_lo", sofar(f, FT + FT // 2) + j + 1))
        return [v.rearrange("p (k n) -> p k n", k=k) for v in (m.whi_r[j % HI_BUFFERS], m.ring_r[U.slot(units[j])])]

    for i in range(FT):
        job = f"{f}.in.{i}"
        B.claim(pe, job)
        hi, lo = parts(i, KT)
        for c in range(2):
            for k in range(KT):
                turns = passes_of([w[:, k, c * P:(c + 1) * P] for w in (hi, lo)], [x[:, k, :] for x in (m.hT_r, m.hTlo_r)])
                for n, (w, x) in enumerate(turns):
                    mm = pe.matmul(ps[B.bank(job)][:, c * T:(c + 1) * T], w, x, start=k + n == 0,
                                   stop=k == KT - 1 and n == 2)
        mm.then_inc(B.full(job), 1)
    for i in range(FT // 2):
        hi, lo = parts(FT + i, 2)
        for k in range(2):
            kk = 2 * i + k
            pe.wait_ge(*F.at("ffn_hid", sofar(f, FT) + kk + 1))
            for n in range(2):
                for t in range(TT):
                    job = f"{f}.out.{n}.{t}"
                    if kk == 0:
                        B.claim(pe, job)
                    turns = passes_of([x[:, kk, t * P:(t + 1) * P] for x in (m.hid_r, m.hidlo_r)],
                                      [w[:, k, n * 512:(n + 1) * 512] for w in (hi, lo)])
                    for q, (x, w) in enumerate(turns):
                        mm = pe.matmul(ps[B.bank(job)][:], x, w, start=kk + q == 0, stop=kk == FT - 1 and q == 2)
                    if kk == FT - 1:
                        mm.then_inc(B.full(job), 1)
        if i < FT // 2 - 1:
            mm.then_inc(U.parts_sem, 1)


def ffn_scalar(act, step, m, ps, B, U, F, f, gain):
    units = ffn_unit_names(f)
    for j in range(AHEAD_UNITS):
        unit_hi(act, m, U, F, f, units, j)
    row_squares(act, m, F, f)
    for i in range(4):
        job = f"{f}.n.{i}"
        act.wait_ge(*B.filled(job))
        for k in range(2):
            ins = act.activation(m.hT_r[:, 2 * i + k, :], ps[B.bank(job)][:, k * T:(k + 1) * T], ACT.Copy,
                                 scale=gain[:, 2 * i + k:2 * i + k + 1])
        ins.then_inc(F[f"{f}.cols"], 1)
    for i in range(FT):
        if i + AHEAD_UNITS < len(units):
            unit_hi(act, m, U, F, f, units, i + AHEAD_UNITS)
        job, e = f"{f}.in.{i}", m.fe[i % 2]
        act.wait_ge(*B.filled(job))
        if i >= 2:
            act.wait_ge(*F.at("ffn_hid", sofar(f, FT) + i - 1))
        step(act.activation(e, ps[B.bank(job)][:, 0:T], ACT.Exp, scale=-1.0))
        step(act.activation(e, e, ACT.Ln, bias=1.0))
        act.activation(e, e, ACT.Exp, scale=-1.0).then_inc(F["ffn_exp"], 1)
    for j in range(FT + AHEAD_UNITS, len(units)):
        unit_hi(act, m, U, F, f, units, j)
    post_scalar(act, m, ps, B, F, f)


def row_squares(act, m, F, f):
    for t in range(TT):
        act.wait_ge(*F.at(BEFORE[f] + ".x", t + 1 if f != "f1" else t - 1))
        act.activation(m.hrows[:, t, :], m.x[:, t, :], ACT.Square, scale=D ** -0.5,
                       accum_out=m.ss[:, t:t + 1]).then_inc(F[f"{f}.ss"], 1)


def post_scalar(act, m, ps, B, F, f):
    for n in range(2):
        for t in range(TT):
            job = f"{f}.out.{n}.{t}"
            act.wait_ge(*B.filled(job))
            act.activation(m.hrows[:, t, n * 512:(n + 1) * 512], ps[B.bank(job)][:], ACT.Square, scale=D ** -0.5,
                           accum_out=m.halves[:, n, t:t + 1]).then_inc(F[f"{f}.pss"], 1)
    if f == "f2":
        act.sem_inc(F["ring_free"], 1)


def ffn_vector(dve, step, m, ps, B, U, F, f, gain, post):
    units = ffn_unit_names(f)
    unit_lo(dve, m, U, F, f, units, 0)
    scale_rows(dve, m, F, f)
    for i in range(4):
        job = f"{f}.n.{i}"
        dve.wait_ge(*F.at(f"{f}.cols", i + 1))
        for k in range(2):
            kk = 2 * i + k
            ins = dve.scalar_tensor_tensor(out=m.hTlo_r[:, kk, :], in0=ps[B.bank(job)][:, k * T:(k + 1) * T],
                                           scalar=gain[:, kk:kk + 1], in1=m.hT_r[:, kk, :].bitcast(F32), op0=ALU.mult,
                                           op1=ALU.subtract)
        ins.then_inc(B.free(job), 1)
    unit_lo(dve, m, U, F, f, units, 1)
    for i in range(FT):
        unit_lo(dve, m, U, F, f, units, i + AHEAD_UNITS)
        job = f"{f}.in.{i}"
        bank, e = ps[B.bank(job)], m.fe[i % 2]
        dve.wait_ge(*F.at("ffn_exp", sofar(f, FT) + i + 1))
        step(dve.tensor_tensor(e, e, bank[:, 0:T], ALU.mult))
        dve.tensor_tensor(e, e, bank[:, T:2 * T], ALU.mult).then_inc(B.free(job), 1)
        dve.wait_ge(*B.drained(job))
        step(dve.tensor_copy(m.hid_r[:, i, :], e))
        dve.tensor_tensor(m.hidlo_r[:, i, :], e, m.hid_r[:, i, :].bitcast(F32), ALU.subtract).then_inc(F["ffn_hid"], 1)
    for j in range(FT + AHEAD_UNITS, len(units)):
        unit_lo(dve, m, U, F, f, units, j)
    post_vector(dve, m, ps, B, F, f, post, 0.5)


def scale_rows(dve, m, F, f):
    dve.wait_ge(*F.at(f"{f}.rstd"))
    for t in range(TT):
        dve.tensor_scalar(m.xn[:, t, :], m.x[:, t, :], m.ss[:, t:t + 1], None, ALU.mult).then_inc(F[f"{f}.xn"], 1)


def post_vector(dve, m, ps, B, F, f, post, weight):
    for n in range(2):
        for t in range(TT):
            job = f"{f}.out.{n}.{t}"
            c = slice(n * 512, (n + 1) * 512)
            dve.wait_ge(*F.at(f"{f}.pss", 2 * n + t + 1))
            dve.scalar_tensor_tensor(out=m.xn[:, t, c], in0=ps[B.bank(job)][:], scalar=weight, in1=post[:, c],
                                     op0=ALU.mult, op1=ALU.mult).then_inc(B.free(job), 1)
    for t in range(TT):
        for n in range(2):
            dve.wait_ge(*B.drained(f"{f}.out.{n}.{t}"))
    dve.wait_ge(*F.at(f"{f}.prstd"))
    for t in range(TT):
        dve.scalar_tensor_tensor(out=m.x[:, t, :], in0=m.xn[:, t, :], scalar=m.pr[:, t:t + 1], in1=m.x[:, t, :],
                                 op0=ALU.mult, op1=ALU.add).then_inc(F[f"{f}.x"], 1)
    dve.wait_ge(*F.at(f"{f}.x", 2))


def pre_pool(pool, step, m, F, f):
    pool.wait_ge(*F.at(f"{f}.ss", 2))
    root_of_mean(pool, step, m.ss, m.c["eps"][:, 0:2], m.half[:, 0:2], F[f"{f}.rstd"])


def post_pool(pool, step, m, F, f):
    pool.wait_ge(*F.at(f"{f}.pss", 4))
    step(pool.tensor_tensor(m.pr, m.halves[:, 0, :], m.halves[:, 1, :], ALU.add))
    root_of_mean(pool, step, m.pr, m.c["eps"][:, 0:2], m.half[:, 0:2], F[f"{f}.prstd"])


def layer_pool(pool, m, B, F, step):
    pre_pool(pool, step, m, F, "f1")
    post_pool(pool, step, m, F, "f1")
    pre_pool(pool, step, m, F, "mx")
    pool.wait_ge(*F.at("o_var"))
    root_of_mean(pool, step, m.ov, m.c["eps"], m.half[:, 0:8], F["o_rstd"])
    pool.wait_ge(*B.drained("ssum"))
    pool.tensor_tensor(m.srs, m.srs, m.half, ALU.pow).then_inc(F["ssd_rs"], 1)
    post_pool(pool, step, m, F, "mx")
    pre_pool(pool, step, m, F, "f2")
    post_pool(pool, step, m, F, "f2")


def mix_tensor(pe, m, ps, B, U, F):
    ident, ring = m.c["ident"], m.ring
    names = [f"mx.n.{i}" for i in range(4)]
    turn_rows(pe, B, names, ps, m.xn, ident, F, "mx")
    wait_columns(pe, B, names)
    for r in ("rq", "rk"):
        project_rows(pe, B, U, ps, ring, [f"{r}.{t}" for t in range(TT)], [f"{r}.{i}" for i in range(2)], m.hT)
    for r in ("rv", "rg"):
        for n in range(2):
            project_rows(pe, B, U, ps, ring, [f"{r}.{n}.{t}" for t in range(TT)], [f"{r}.{n}.{i}" for i in range(2)],
                         m.hT)
    for i in range(6):
        project_columns(pe, B, U, ps, ring, f"xbc.{i}", f"xbc.{i}", m.hT)
    pe.wait_ge(*F.at("rope", 4))
    for n, name in enumerate(("rqT", "rkT")):
        for i in range(2):
            job = f"{name}.{i}"
            B.claim(pe, job)
            for k in range(2):
                h = 2 * i + k
                for t in range(TT):
                    mm = pe.transpose(ps[B.bank(job)][:, k * T + t * P:k * T + t * P + P],
                                      m.rope[:, n, t, h * P:(h + 1) * P], ident)
            mm.then_inc(B.full(job), 1)
    B.claim(pe, "dt")
    wdt = m.lp["wdt"].rearrange("p (k n) -> p k n", k=KT)
    for k in range(KT):
        mm = pe.matmul(ps[B.bank("dt")][0:16, 0:T], wdt[:, k, :], m.hT[:, k, :], start=k == 0, stop=k == KT - 1)
    mm.then_inc(B.full("dt"), 1)
    for i in range(4):
        project_columns(pe, B, U, ps, ring, f"z.{i}", f"z.{i}", m.hT)
    for h in range(RET_H):
        if h % 2 == 0:
            pe.wait_ge(*B.drained(f"rqT.{h // 2}"))
            pe.wait_ge(*B.drained(f"rkT.{h // 2}"))
        causal_scores(pe, B, ps, f"rs.{h}", m.rT[:, 1, h, :], m.rT[:, 0, h, :])
    pe.wait_ge(*F.at("dt_rows", 2))
    B.claim(pe, "dtcol")
    for half, row in enumerate((m.drow[0], m.drow[1])):
        for t in range(TT):
            o = (half * 2 + t) * 16
            mm = pe.matmul(ps[B.bank("dtcol")][:, o:o + 16], row[0:16, t * P:(t + 1) * P], ident[0:16, 0:16],
                           start=True, stop=True)
    mm.then_inc(B.full("dtcol"), 1)
    pe.wait_ge(*F.at("xc", 3))
    for g in range(SSD_G):
        causal_scores(pe, B, ps, f"cb.{g}", m.xc[:, 8 + g, :], m.xc[:, 10 + g, :])
    for i in range(4):
        job = f"xst.{i}"
        B.claim(pe, job)
        for k in range(4):
            mm = pe.transpose(ps[B.bank(job)][:, k * P:(k + 1) * P],
                              m.xc[:, 4 * (i % 2) + k, (i // 2) * P:(i // 2 + 1) * P], ident)
        mm.then_inc(B.full(job), 1)
    for h in range(RET_H):
        pe.wait_ge(*B.drained(f"rs.{h}"))
    for n in range(2):
        for t in range(TT):
            pe.wait_ge(*B.drained(f"rv.{n}.{t}"))
    for t in range(TT):
        for i in range(2):
            job = f"ro.{t}.{i}"
            B.claim(pe, job)
            for k in range(2):
                h = 2 * i + k
                for s in range(t + 1):
                    mm = pe.matmul(ps[B.bank(job)][:, k * T:(k + 1) * T], m.rw[:, h, (t + s) * P:(t + s + 1) * P],
                                   m.rv[:, s, h * T:(h + 1) * T], start=s == 0, stop=s == t)
            mm.then_inc(B.full(job), 1)

    def spread(i):
        spread_rows(pe, B, ps, f"sbc.{i}", m.drow[1], ident, 16, 2 * i)

    def ssd_out(i):
        job = f"sy.{i}"
        B.claim(pe, job)
        pe.wait_ge(*F.at("sw", 2 * i + 2))
        for c in range(2):
            for s in range(2):
                for e in range(2):
                    h = 4 * i + 2 * c + e
                    lo, n = (0, T) if s == 0 else (P, P)
                    mm = pe.matmul(ps[B.bank(job)][e * 64:e * 64 + 64, c * T + lo:c * T + lo + n],
                                   m.xdt[:, s, h * 64:(h + 1) * 64],
                                   m.sw[:, h % 8, s * T:s * T + n], start=s == 0, stop=s == 1)
        mm.then_inc(B.full(job), 1)

    for i in range(4):
        spread(i)
    for i in range(4):
        project_columns(pe, B, U, ps, ring, f"aq.{i}", f"aq.{i}", m.hT)
    for i in range(4):
        pe.wait_ge(*B.drained(f"xst.{i}"))
    ssd_out(0)
    ssd_out(1)
    for i in range(4, 8):
        spread(i)
    B.claim(pe, "akv")
    pe.wait_ge(*U.landed("akv"))
    w = ring[U.slot("akv")].rearrange("p (k n) -> p k n", k=KT)
    for k in range(KT):
        pe.matmul(ps[B.bank("akv")][:, 0:T], w[:, k, 0:P], m.hT[:, k, :], start=k == 0, stop=k == KT - 1)
    for t in range(TT):
        for k in range(KT):
            mm = pe.matmul(ps[B.bank("akv")][:, T + t * P:T + (t + 1) * P], m.hT[:, k, t * P:(t + 1) * P], w[:, k, P:T],
                           start=k == 0, stop=k == KT - 1)
    mm.then_inc(B.full("akv"), 1)
    pe.wait_ge(*F.at("ret_y"))
    for i in range(4):
        job = f"rT.{i}"
        B.claim(pe, job)
        for k in range(2):
            for t in range(TT):
                mm = pe.transpose(ps[B.bank(job)][:, k * T + t * P:k * T + t * P + P],
                                  m.ro[:, t, (2 * i + k) * P:(2 * i + k + 1) * P], ident)
        mm.then_inc(B.full(job), 1)
    ssd_out(2)
    ssd_out(3)
    pe.wait_ge(*F.at("ssd_sq"))
    B.claim(pe, "ssum")
    for k in range(KT):
        mm = pe.matmul(ps[B.bank("ssum")][:, 0:T], m.c["ones"][:, 0:P], m.ysum[:, k, :], start=k == 0, stop=k == KT - 1)
    mm.then_inc(B.full("ssum"), 1)
    pe.wait_ge(*B.drained("akv"))
    for i in range(4):
        pe.wait_ge(*B.drained(f"aq.{i}"))
    for kv in range(2):
        for g in range(2):
            job = f"as.0.{kv}.{g}"
            B.claim(pe, job)
            for k in range(4):
                mm = pe.matmul(ps[B.bank(job)][:, k * P:(k + 1) * P], m.aq[kv * 64:kv * 64 + 64, 4 * g + k, 0:P],
                               m.akv[kv * 64:kv * 64 + 64, 0:P], start=True, stop=True)
            mm.then_inc(B.full(job), 1)
    for kv in range(2):
        for g in range(4):
            job = f"as.1.{kv}.{g}"
            B.claim(pe, job)
            for k in range(2):
                mm = pe.matmul(ps[B.bank(job)][:, k * T:(k + 1) * T], m.aq[kv * 64:kv * 64 + 64, 2 * g + k, P:T],
                               m.akv[kv * 64:kv * 64 + 64, 0:T], start=True, stop=True)
            mm.then_inc(B.full(job), 1)

    def branch(b):
        for i in range(4):
            project_columns(pe, B, U, ps, ring, f"g.{b}.{i}", f"g.{b}.{i}", m.hT)
        if b == 0:
            pe.wait_ge(*F.at("ssd_y", 8))
        elif b == 1:
            for i in range(4):
                pe.wait_ge(*B.drained(f"rT.{i}"))
        else:
            for t in range(TT):
                for j in range(2):
                    pe.wait_ge(*B.drained(f"ao.{t}.{j}"))
        for i in range(4):
            project_columns(pe, B, U, ps, ring, f"b.{b}.{i}", f"b.{b}.{i}", (m.zT, m.yret, m.yatt)[b])

    def attend(t):
        pe.wait_ge(*F.at("ap", t + 1))
        for kv in range(2):
            for j in range(2):
                for s in range(t + 1):
                    job = f"ap.0.{kv}.{j}" if t == 0 else f"ap.1.{kv}.{j}.{s}"
                    B.claim(pe, job)
                    for k in range(4):
                        mm = pe.transpose(ps[B.bank(job)][:, k * P:(k + 1) * P],
                                          m.al[t][:, kv * 8 + 4 * j + k, s * P:(s + 1) * P], ident)
                    mm.then_inc(B.full(job), 1)
        for j in range(2):
            job = f"ao.{t}.{j}"
            B.claim(pe, job)
            for s in range(t + 1):
                for kv in range(2):
                    pe.wait_ge(*B.drained(f"ap.0.{kv}.{j}" if t == 0 else f"ap.1.{kv}.{j}.{s}"))
                    mm = pe.matmul(ps[B.bank(job)][kv * 64:kv * 64 + 64, :],
                                   m.akv[:, T + s * P + kv * 64:T + s * P + kv * 64 + 64],
                                   m.pT[:, ((kv * 2 + j) * (t + 1) + s) * 512:((kv * 2 + j) * (t + 1) + s + 1) * 512],
                                   start=s == 0, stop=s == t)
            mm.then_inc(B.full(job), 1)

    branch(0)
    attend(0)
    attend(1)
    branch(1)
    branch(2)
    pe.wait_ge(*F.at("ysum", 8))
    for n in range(2):
        project_rows(pe, B, U, ps, ring, [f"mx.out.{n}.{t}" for t in range(TT)], [f"mx.out.{n}.{i}" for i in range(2)],
                     m.ysum)


def mix_scalar(act, step, m, ps, B, F):
    lp = m.lp
    row_squares(act, m, F, "mx")
    take_columns(act, B, [f"mx.n.{i}" for i in range(4)], ps, m.hT, lp["gmix"], 1)
    for n in range(2):
        for t in range(TT):
            job = f"rv.{n}.{t}"
            act.wait_ge(*B.filled(job))
            act.activation(m.rv[:, t, n * 512:(n + 1) * 512], ps[B.bank(job)][:], ACT.Copy).then_inc(B.free(job), 1)
    for n in range(2):
        for t in range(TT):
            job = f"rg.{n}.{t}"
            act.wait_ge(*B.filled(job))
            act.activation(m.rg[:, t, n * 512:(n + 1) * 512], ps[B.bank(job)][:], ACT.Exp,
                           scale=-1.0).then_inc(F["rg_exp"], 1)
    for i in range(6):
        job = f"xbc.{i}"
        act.wait_ge(*B.filled(job))
        act.activation(m.xpad[:, 2 * i:2 * i + 2, 3:], split(ps[B.bank(job)][:], 2), ACT.Copy).then_inc(B.free(job), 1)
    for name, n in (("rqT", 0), ("rkT", 1)):
        for i in range(2):
            job = f"{name}.{i}"
            act.wait_ge(*B.filled(job))
            act.activation(m.rT[:, n, 2 * i:2 * i + 2, :], split(ps[B.bank(job)][:], 2),
                           ACT.Copy).then_inc(B.free(job), 1)
    for i in range(3):
        act.wait_ge(*F.at("conv", 4 * i + 4))
        if i:
            act.wait_ge(*F.at("xc", i))
        act.activation(m.ce, m.xc[:, 4 * i:4 * i + 4, :], ACT.Exp, scale=-1.0).then_inc(F["conv_exp"], 1)
    for i in range(4):
        job = f"z.{i}"
        act.wait_ge(*B.filled(job))
        act.activation(m.zT[:, 2 * i:2 * i + 2, :], split(ps[B.bank(job)][:], 2), ACT.Exp,
                       scale=-1.0).then_inc(F["z_exp"], 1)
    act.activation(m.acol[0:16, 0:1], lp["alog"][0:16, :], ACT.Exp).then_inc(F["a"], 1)
    act.wait_ge(*F.at("abs_dt"))
    step(act.activation(m.drow[2][0:16, :], m.drow[2][0:16, :], ACT.Exp, scale=-1.0))
    act.activation(m.drow[2][0:16, :], m.drow[2][0:16, :], ACT.Ln, bias=1.0).then_inc(F["dt_ln"], 1)
    for g in range(SSD_G):
        job = f"cb.{g}"
        act.wait_ge(*B.filled(job))
        act.activation(m.cb[:, g, :], ps[B.bank(job)][:, 0:3 * P], ACT.Copy).then_inc(B.free(job), 1)
    for t in range(TT):
        for i in range(2):
            job = f"ro.{t}.{i}"
            act.wait_ge(*B.filled(job))
            act.activation(m.ro[:, t, i * 512:(i + 1) * 512], ps[B.bank(job)][:], ACT.Copy).then_inc(B.free(job), 1)
    act.wait_ge(*B.drained("dtcol"))

    def decay(i):
        act.wait_ge(*B.drained(f"sbc.{i}"))
        for k in range(2):
            h = 2 * i + k
            for s, lo, hi in ((0, 0, T), (1, T, T + P)):
                e = m.sw[:, h % 8, lo:hi]
                act.activation(e, e, ACT.Exp, bias=m.dcol[:, 32 + s * 16 + h:33 + s * 16 + h]).then_inc(F["decay"], 1)

    for i in range(4):
        decay(i)
    for i in range(4):
        job = f"aq.{i}"
        act.wait_ge(*B.filled(job))
        act.activation(m.aq[:, 2 * i:2 * i + 2, :], split(ps[B.bank(job)][:], 2), ACT.Copy).then_inc(B.free(job), 1)
    act.wait_ge(*F.at("o_centred"))
    act.activation(m.osq, m.ro, ACT.Square, scale=T ** -0.5).then_inc(F["o_sq"], 1)
    for i in range(4, 8):
        decay(i)
    act.wait_ge(*B.filled("akv"))
    act.activation(m.akv, ps[B.bank("akv")][:], ACT.Copy).then_inc(B.free("akv"), 1)
    act.wait_ge(*F.at("ssd_gated", 4))
    act.activation(m.ysum, m.zT, ACT.Square).then_inc(F["ssd_sq"], 1)
    for t in range(TT):
        act.wait_ge(*F.at("a_max", t + 1))
        for h in range(ATT_H):
            s = m.al[t][:, h, :]
            act.activation(s, s, ACT.Exp, bias=m.amax[:, t * 16 + h:t * 16 + h + 1],
                           accum_out=m.asum[:, t * 16 + h:t * 16 + h + 1]).then_inc(F["a_exp"], 1)
        act.wait_ge(*F.at("a_sink", t + 1))
        c = slice(t * 16, t * 16 + 16)
        act.activation(m.asink[:, c], m.asink[:, c], ACT.Exp).then_inc(F["a_sink_exp"], 1)

    def gate(b):
        for i in range(4):
            job = f"g.{b}.{i}"
            act.wait_ge(*B.filled(job))
            if b == 1:
                act.wait_ge(*B.drained(f"b.0.{i}"))
            elif b == 2:
                act.wait_ge(*F.at("ysum", i + 1))
            for k in range(2):
                n = b * KT + 2 * i + k
                ins = act.activation(m.sg[:, 2 * i + k, :], ps[B.bank(job)][:, k * T:(k + 1) * T], ACT.Exp,
                                     bias=m.nbg[:, n:n + 1], scale=-1.0)
            ins.then_inc(B.free(job), 1)

    gate(0)
    for t in range(TT):
        for kv in range(2):
            for j in range(2):
                for s in range(t + 1):
                    if (j + s) % 2:
                        turned_probs(act, m, ps, B, F, t, kv, j, s)
    gate(1)
    gate(2)
    post_scalar(act, m, ps, B, F, "mx")


def turned_probs(eng, m, ps, B, F, t, kv, j, s):
    job = f"ap.0.{kv}.{j}" if t == 0 else f"ap.1.{kv}.{j}.{s}"
    eng.wait_ge(*B.filled(job))
    if t:
        for k in range(2):
            eng.wait_ge(*B.filled(f"ao.0.{k}"))
    n = (kv * 2 + j) * (t + 1) + s
    dst = m.pT[:, n * 512:(n + 1) * 512]
    if (j + s) % 2:
        eng.activation(dst, ps[B.bank(job)][:], ACT.Copy).then_inc(B.free(job), 1)
    else:
        eng.tensor_copy(dst, ps[B.bank(job)][:]).then_inc(B.free(job), 1)


def mix_vector(dve, step, m, ps, B, F):
    lp = m.lp
    scale_rows(dve, m, F, "mx")
    take_columns(dve, B, [f"mx.n.{i}" for i in range(4)], ps, m.hT, lp["gmix"], 0)
    step(dve.tensor_scalar(m.nbg, lp["bgate"], -1.0, None, ALU.mult))
    for n, r in enumerate(("rq", "rk")):
        for t in range(TT):
            job = f"{r}.{t}"
            dve.wait_ge(*B.filled(job))
            x = ps[B.bank(job)][:].rearrange("p (h c d) -> p h c d", h=RET_H, c=2)
            o = m.rope[:, n, t, :].rearrange("p (h c d) -> p h c d", h=RET_H, c=2)
            cos = m.s["cos"][:, t * 64:(t + 1) * 64].unsqueeze(1).to_broadcast([P, RET_H, 64])
            sin = m.s["sin"][:, t * 64:(t + 1) * 64].unsqueeze(1).to_broadcast([P, RET_H, 64])
            t0, t1 = m.rtmp[0], m.rtmp[1]
            dve.tensor_tensor(o[:, :, 0, :], x[:, :, 0, :], cos, ALU.mult)
            dve.tensor_tensor(o[:, :, 1, :], x[:, :, 1, :], cos, ALU.mult)
            dve.tensor_tensor(t0, x[:, :, 1, :], sin, ALU.mult)
            dve.tensor_tensor(t1, x[:, :, 0, :], sin, ALU.mult).then_inc(B.free(job), 1)
            dve.wait_ge(*B.drained(job))
            dve.tensor_tensor(o[:, :, 0, :], o[:, :, 0, :], t0, ALU.subtract)
            dve.tensor_tensor(o[:, :, 1, :], o[:, :, 1, :], t1, ALU.add).then_inc(F["rope"], 1)
            dve.wait_ge(*F.at("rope", 2 * n + t + 1))
    for n in range(2):
        for t in range(TT):
            job = f"rg.{n}.{t}"
            e = m.rg[:, t, n * 512:(n + 1) * 512]
            dve.wait_ge(*F.at("rg_exp", 2 * n + t + 1))
            step(dve.tensor_scalar(e, e, 1.0, None, ALU.add))
            step(dve.reciprocal(e, e))
            dve.tensor_tensor(e, e, ps[B.bank(job)][:], ALU.mult).then_inc(B.free(job), 1)
    step(dve.memset(m.xpad[:, :, 0:3], 0.0))
    for i in range(CONV_T):
        if i % 2 == 0:
            dve.wait_ge(*B.drained(f"xbc.{i // 2}"))
        causal_conv(dve, step, m.xc[:, i, :], m.xpad[:, i, :], lp["convw"][:, 4 * i:4 * i + 4],
                    lp["convb"][:, i:i + 1], F["conv"])
    for i in range(3):
        dve.wait_ge(*F.at("conv_exp", i + 1))
        silu_tail(dve, step, m.ce, m.xc[:, 4 * i:4 * i + 4, :], m.xc[:, 4 * i:4 * i + 4, :], F["xc"])
    dt, cs, r2, r3 = m.drow
    dve.wait_ge(*B.filled("dt"))
    dve.tensor_scalar(r3[0:16, :], ps[B.bank("dt")][0:16, 0:T], lp["dtbias"][0:16, :], None,
                      ALU.add).then_inc(B.free("dt"), 1)
    dve.wait_ge(*B.drained("dt"))
    magnitude(dve, r2[0:16, :], r3[0:16, :]).then_inc(F["abs_dt"], 1)
    step(dve.tensor_scalar(r3[0:16, :], r3[0:16, :], 0.0, None, ALU.max))
    for i in range(4):
        job = f"z.{i}"
        e = m.zT[:, 2 * i:2 * i + 2, :]
        dve.wait_ge(*F.at("z_exp", i + 1))
        step(dve.tensor_scalar(e, e, 1.0, None, ALU.add))
        step(dve.reciprocal(e, e))
        dve.tensor_tensor(e, e, split(ps[B.bank(job)][:], 2), ALU.mult).then_inc(B.free(job), 1)
    dve.wait_ge(*F.at("dt_ln"))
    dve.tensor_tensor(dt[0:16, :], r3[0:16, :], r2[0:16, :], ALU.add).then_inc(F["dt_rows"], 1)
    dve.wait_ge(*F.at("dt_rows"))
    dve.wait_ge(*F.at("a"))
    step(dve.tensor_scalar(r3[0:16, :], dt[0:16, :], m.acol[0:16, 0:1], -1.0, ALU.mult, ALU.mult))
    dve.tensor_tensor_scan(cs[0:16, :], m.c["ones"][0:16, :], r3[0:16, :], 0.0, ALU.mult,
                           ALU.add).then_inc(F["dt_rows"], 1)
    for h in range(RET_H):
        job = f"rs.{h}"
        dve.wait_ge(*B.filled(job))
        dve.scalar_tensor_tensor(out=m.rw[:, h, :], in0=ps[B.bank(job)][:, 0:3 * P], scalar=P ** -0.5,
                                 in1=split(m.s["decay"], RET_H)[:, h, :], op0=ALU.mult,
                                 op1=ALU.mult).then_inc(B.free(job), 1)
    dve.wait_ge(*B.filled("dtcol"))
    dve.tensor_copy(m.dcol[:, 0:32], ps[B.bank("dtcol")][:, 0:32])
    dve.tensor_scalar(m.dcol[:, 32:64], ps[B.bank("dtcol")][:, 32:64], -1.0, None,
                      ALU.mult).then_inc(B.free("dtcol"), 1)
    dve.wait_ge(*B.drained("dtcol"))
    for i in range(4):
        job, t, g = f"xst.{i}", i // 2, i % 2
        dve.wait_ge(*B.filled(job))
        dve.tensor_tensor(m.xdt[:, t, g * 512:(g + 1) * 512].rearrange("p (h d) -> p h d", h=8),
                          split(ps[B.bank(job)][:], 8), bc(m.dcol[:, t * 16 + g * 8:t * 16 + g * 8 + 8], [P, 8, 64]),
                          ALU.mult).then_inc(B.free(job), 1)

    def spread(i):
        job = f"sbc.{i}"
        dve.wait_ge(*B.filled(job))
        if i >= 4:
            dve.wait_ge(*B.filled(f"sy.{(i - 4) // 2}"))
        spread_and_mask(dve, split(ps[B.bank(job)][:], 2), m.sw[:, 2 * i % 8:2 * i % 8 + 2, :], m.c["mask"],
                        B.free(job))

    def weights(i):
        dve.wait_ge(*F.at("decay", 4 * i + 4))
        w = m.sw[:, 2 * i % 8:2 * i % 8 + 2, :]
        dve.tensor_tensor(w, w, m.cb[:, i // 4, :].unsqueeze(1).to_broadcast([P, 2, 3 * P]),
                          ALU.mult).then_inc(F["sw"], 1)

    def gated(i):
        job = f"sy.{i}"
        dve.wait_ge(*B.filled(job))
        for c in range(2):
            k = 2 * i + c
            ins = dve.scalar_tensor_tensor(out=m.xc[:, k, :], in0=m.xc[:, k, :], scalar=lp["dskip"][:, k:k + 1],
                                           in1=ps[B.bank(job)][:, c * T:(c + 1) * T], op0=ALU.mult, op1=ALU.add)
        ins.then_inc(B.free(job), 1)
        dve.wait_ge(*B.drained(job))
        z = m.zT[:, 2 * i:2 * i + 2, :]
        dve.tensor_tensor(z, z, m.xc[:, 2 * i:2 * i + 2, :], ALU.mult).then_inc(F["ssd_gated"], 1)

    for i in range(4):
        spread(i)
    for g in range(SSD_G):
        dve.wait_ge(*B.drained(f"cb.{g}"))
    for i in range(4):
        weights(i)
    for t in range(TT):
        for i in range(2):
            dve.wait_ge(*B.drained(f"ro.{t}.{i}"))
    centre(dve, step, m.roh, m.ov, T, F["o_centred"])
    gated(0)
    gated(1)
    for i in range(4, 8):
        spread(i)
    dve.wait_ge(*F.at("o_sq"))
    dve.tensor_reduce(m.ov, m.osqh, AX.X, ALU.add).then_inc(F["o_var"], 1)
    for i in range(4, 8):
        weights(i)
    dve.wait_ge(*F.at("o_rstd"))
    step(dve.tensor_tensor(m.roh, m.roh, bc(m.ov, [P, 8, T]), ALU.mult))
    dve.tensor_tensor(m.ro, m.ro, m.rg, ALU.mult).then_inc(F["ret_y"], 1)
    for i in range(4):
        job = f"rT.{i}"
        dve.wait_ge(*B.filled(job))
        dve.tensor_tensor(m.yret[:, 2 * i:2 * i + 2, :], split(ps[B.bank(job)][:], 2),
                          bc(lp["gret"][:, 2 * i:2 * i + 2], [P, 2, T]), ALU.mult).then_inc(B.free(job), 1)
    gated(2)
    gated(3)
    dve.wait_ge(*F.at("ssd_gated", 4))
    dve.wait_ge(*B.filled("ssum"))
    dve.tensor_scalar(m.srs, ps[B.bank("ssum")][:, 0:T], 1.0 / D, EPS, ALU.mult, ALU.add).then_inc(B.free("ssum"), 1)
    abias = m.s["bias"].rearrange("p (h k) -> p h k", h=ATT_H)
    for t in range(TT):
        per = 4 if t == 0 else 2
        for kv in range(2):
            for g in range(8 // per):
                job = f"as.{t}.{kv}.{g}"
                h = kv * 8 + g * per
                dst = m.al[t][:, h:h + per, :]
                dve.wait_ge(*B.filled(job))
                dve.scalar_tensor_tensor(out=dst, in0=split(ps[B.bank(job)][:], per), scalar=ATT_D ** -0.5,
                                         in1=abias[:, h:h + per, (1 - t) * P:], op0=ALU.mult,
                                         op1=ALU.add).then_inc(B.free(job), 1)
                dve.wait_ge(*B.drained(job))
                step(dve.tensor_reduce(m.amax[:, t * 16 + h:t * 16 + h + per], dst, AX.X, ALU.max))
        c = slice(t * 16, t * 16 + 16)
        step(dve.tensor_tensor(m.amax[:, c], m.amax[:, c], lp["sinks"], ALU.max))
        dve.tensor_scalar(m.amax[:, c], m.amax[:, c], -1.0, None, ALU.mult).then_inc(F["a_max"], 1)
        dve.wait_ge(*F.at("a_max", t + 1))
        dve.tensor_tensor(m.asink[:, c], m.amax[:, c], lp["sinks"], ALU.add).then_inc(F["a_sink"], 1)
    dve.wait_ge(*F.at("ssd_rs"))
    for k in range(KT):
        dve.scalar_tensor_tensor(out=m.zT[:, k, :], in0=m.zT[:, k, :], scalar=lp["gssd"][:, k:k + 1], in1=m.srs,
                                 op0=ALU.mult, op1=ALU.mult).then_inc(F["ssd_y"], 1)

    def probabilities(t):
        c = slice(t * 16, t * 16 + 16)
        dve.wait_ge(*F.at("a_exp", 16 * (t + 1)))
        dve.wait_ge(*F.at("a_sink_exp", t + 1))
        step(dve.tensor_tensor(m.asum[:, c], m.asum[:, c], m.asink[:, c], ALU.add))
        step(dve.reciprocal(m.asum[:, c], m.asum[:, c]))
        dve.tensor_tensor(m.al[t], m.al[t], bc(m.asum[:, c], [P, ATT_H, (t + 1) * P]), ALU.mult).then_inc(F["ap"], 1)

    def gates(b):
        for i in range(4):
            dve.wait_ge(*B.drained(f"g.{b}.{i}"))
            s = m.sg[:, 2 * i:2 * i + 2, :]
            step(dve.tensor_scalar(s, s, 1.0, None, ALU.add))
            step(dve.reciprocal(s, s))

    def branch(b):
        for i in range(4):
            job = f"b.{b}.{i}"
            dve.wait_ge(*B.filled(job))
            s, y = m.sg[:, 2 * i:2 * i + 2, :], m.ysum[:, 2 * i:2 * i + 2, :]
            bank = split(ps[B.bank(job)][:], 2)
            if b == 0:
                dve.tensor_tensor(y, bank, s, ALU.mult).then_inc(B.free(job), 1)
                dve.wait_ge(*B.drained(job))
            else:
                dve.tensor_tensor(s, bank, s, ALU.mult).then_inc(B.free(job), 1)
                dve.wait_ge(*B.drained(job))
                dve.tensor_tensor(y, y, s, ALU.add).then_inc(F["ysum"], 1)

    gates(0)
    probabilities(0)
    probabilities(1)
    branch(0)
    for t in range(TT):
        for kv in range(2):
            for j in range(2):
                for s in range(t + 1):
                    if (j + s) % 2 == 0:
                        turned_probs(dve, m, ps, B, F, t, kv, j, s)
        for j in range(2):
            job = f"ao.{t}.{j}"
            dve.wait_ge(*B.filled(job))
            dve.tensor_copy(m.yatt[:, 4 * j:4 * j + 4, t * P:(t + 1) * P],
                            split(ps[B.bank(job)][:], 4)).then_inc(B.free(job), 1)
    for b in (1, 2):
        gates(b)
        branch(b)
    post_vector(dve, m, ps, B, F, "mx", m.post[:, D:2 * D], 1.0)



LAYER_PER = {"f1.ss": 2, "f1.xn": 2, "f1.pss": 4, "f1.x": 2, "f2.ss": 2, "f2.xn": 2, 
             "f2.pss": 4, "f2.x": 2, "mx.ss": 2, "mx.xn": 2, "mx.pss": 4, "mx.x": 2, "rope": 4, "rg_exp": 4,
             "conv": CONV_T, "conv_exp": 3, "xc": 3, "z_exp": 4, "dt_rows": 2, "decay": 32, "sw": 8, "ssd_gated": 4,
             "a_max": 2, "a_sink": 2, "a_sink_exp": 2, "a_exp": 32, "ap": 2, "ssd_y": 8, "ysum": 8}
LAYER_PER.update({"ffn_hi": 2 * (FT + FT // 2), "ffn_lo": 2 * (FT + FT // 2), "ffn_hid": 2 * FT, "ffn_exp": 2 * FT,
                  "f1.cols": 4, "f2.cols": 4})
LAYER_BEFORE = {"f2.pss": 2, "f2.prstd": 1, "f2.x": 2, "ring_free": 1}
DVE_STEPS, ACT_STEPS, POOL_STEPS = 195, 89, 10


def lay_out(sb, both):
    m = type("Views", (), {})()
    m.x = sb("x", [P, TT, D], F32)[:]
    m.xn = sb("rows", [P, TT, D], F32)[:]
    m.half = sb("minus_half", [P, T], F32)[:]
    m.ss = sb("sums", [P, TT], F32)[:]
    m.pr = sb("post_roots", [P, TT], F32)[:]
    m.halves = split(sb("half_sums", [P, 2 * TT], F32)[:], 2)
    at, n = offsets(CONST)
    m.const = sb("const", [P, n], F32)
    m.c = {k: m.const[:, o:o + w] for k, (o, w) in at.items()}

    second, n_second = offsets(SECOND)
    layer, n_layer = offsets(LAYER)
    kept = n_second + n_layer + 3 * D
    total = 33684
    m.turns = sb("turns", [P, 2], I32)[:]
    with both(F32) as sb_f32:
        hT, ring, area = sb_f32("columns", KT * T), sb_f32("ring", SLOTS * UNIT), sb_f32("work", total)
    with both(F32R) as sb_f32r:
        hT_r, ring_r, area_r = (sb_f32r("columns_parts", KT * T), sb_f32r("ring_parts", SLOTS * UNIT),
                                sb_f32r("work_parts", 2 * FT * T + KT * T + HI_BUFFERS * UNIT))
    m.hT, m.hrows, m.hT_r = split(hT, KT), split(hT, TT), split(hT_r, KT)
    m.ring, m.ring_r = ([v[:, s * UNIT:(s + 1) * UNIT] for s in range(SLOTS)] for v in (ring, ring_r))

    S = Memory(area)
    S.at = total - kept
    m.second_area = S.take(n_second)
    m.s = {k: m.second_area[:, o:o + w] for k, (o, w) in second.items()}
    m.layer_area = S.take(n_layer)
    m.lp = {k: m.layer_area[:, o:o + w] for k, (o, w) in layer.items()}
    m.post = S.take(3 * D)

    W = Memory(area)
    first, n_first = offsets(FIRST)
    m.first_area = W.take(n_first)
    m.p = {k: m.first_area[:, o:o + w] for k, (o, w) in first.items()}
    m.gcols = m.p["g2"]
    r = m.r = type("Routing", (), {})()

    def t2(n):
        return split(W.take(TT * n), TT)
    r.lg, r.eg, r.group, r.le, r.hot1, r.hot2 = t2(36), t2(4), t2(4), t2(8), t2(8), t2(8)
    r.by_group = W.take(TT * 32).rearrange("p (t g j) -> p t g j", t=TT, g=GROUPS)
    r.chosen, r.rank = t2(32), t2(32)
    r.gates, r.ranks = t2(PASSES * EXPERTS + 2), t2(PASSES * EXPERTS + 2)
    r.best, r.nmg, r.sg, r.e2, r.w1, r.w2, r.passes = [W.take(2) for _ in range(7)]
    r.most = W.take(1)
    r.turns_i = m.turns
    m.sel, m.selg, m.selgT = t2(2 * CAP), t2(2 * CAP), W.take(T)
    m.hc = split(W.take(KT * P), KT)
    m.eg, m.hid, m.hidT, m.ym = W.take(FE), W.take(FE), W.take(4 * P), W.take(D)
    m.cpad = split(W.take(4 * (T + 3)), 4)
    m.cv, m.ec, m.ez = [split(W.take(4 * T), 4) for _ in range(3)]
    m.cols = {n: split(W.take(4 * T), 4) for n in ("v", "qd", "kd", "vd")}
    m.vtok, m.vdtok = t2(4 * P), t2(4 * P)
    m.dp = [W.take(2 * H1 * (t + 1) * P).rearrange("p (c h k) -> p c h k", c=2, h=H1) for t in range(TT)]
    m.mq, m.mk = split(W.take(4 * T), 4), split(W.take(4 * T), 4)
    m.frow = [W.take(T) for _ in range(6)]
    m.me = split(W.take(H1 * 3 * P), H1)
    m.gcol, m.em = W.take(16), W.take(8)
    m.daT = split(W.take(3 * 4 * P), 3)
    m.hm = split(W.take(8 * P), 8)
    m.hsq = m.ec.rearrange("p a b -> p (a b)").rearrange("p (n d) -> p n d", n=8)
    yd = W.take(8 * P)
    m.yd, m.ydh = split(yd, TT), split(yd, 8)
    m.yT = split(W.take(KT * T), KT)
    m.dmax, m.dsum, m.den, m.hv, m.dv, m.lam, m.lamj = [W.take(n) for n in (16, 16, 8, 8, 8, 5, 128)]
    assert W.at <= total, W.at

    W = Memory(area)
    R = Memory(area_r)
    m.hid_r, m.hidlo_r, m.hTlo_r = split(R.take(FT * T), FT), split(R.take(FT * T), FT), split(R.take(KT * T), KT)
    m.whi_r = [R.take(UNIT) for _ in range(HI_BUFFERS)]
    W.at = R.at
    m.fe = [W.take(T) for _ in range(2)]
    W = Memory(area)
    al = W.take(ATT_H * 2 * P)
    m.rope = al[:, 0:2048].rearrange("p (n t c) -> p n t c", n=2, t=TT)
    m.ro = split(al[:, 0:2048], TT)
    m.roh = split(al[:, 0:2048], 8)
    m.rg = split(al[:, 2048:4096], TT)
    m.al = [m.xn.rearrange("p t d -> p (t d)").rearrange("p (h k) -> p h k", h=ATT_H), split(al, ATT_H)]
    m.osq = m.xn
    m.osqh = m.xn.rearrange("p t d -> p (t d)").rearrange("p (n d) -> p n d", n=8)
    rt = W.take(2 * RET_H * T)
    m.rT = rt.rearrange("p (n h t) -> p n h t", n=2, h=RET_H)
    m.yret = split(rt, KT)
    rv = W.take(TT * D)
    m.rv, m.aq = split(rv, TT), split(rv, KT)
    rw = W.take(RET_H * 3 * P)
    m.rw, m.akv = split(rw, RET_H), rw[:, 0:512]
    conv = W.take(CONV_T * (T + 3) + CONV_T * T)
    m.xpad = split(conv[:, 0:CONV_T * (T + 3)], CONV_T)
    m.sw = split(conv[:, 0:8 * 3 * P], 8)
    m.xc = split(conv[:, CONV_T * (T + 3):], CONV_T)
    m.pT = conv[:, 0:4096]
    m.sg = split(conv[:, 4096:4096 + 2048], KT)
    m.zT = split(W.take(KT * T), KT)
    xdt = W.take(KT * T)
    m.xdt, m.ysum = split(xdt, TT), split(xdt, KT)
    m.cb = split(W.take(2 * 3 * P), 2)
    m.drow = [W.take(T) for _ in range(4)]
    ya = W.take(KT * T)
    m.yatt = split(ya, KT)
    m.ce = split(ya[:, 0:4 * T], 4)
    m.rtmp = [split(ya[:, (4 + i) * T:(5 + i) * T], RET_H) for i in range(2)]
    m.dcol, m.acol, m.nbg, m.ov, m.srs = W.take(64), W.take(1), W.take(24), W.take(8), W.take(T)
    m.amax, m.asum, m.asink = W.take(32), W.take(32), W.take(32)
    assert W.at <= total - kept, (W.at, total - kept)
    return m


def build(nc, x, const, first, second, layer, post, normf, w_first, w_experts, w_layers, out):
    with ExitStack() as ctx:
        def sb(name, shape, dt):
            return ctx.enter_context(nc.sbuf_tensor(name, shape, dt))

        def sem(name):
            return ctx.enter_context(nc.semaphore(name))

        @contextmanager
        def both(dt):
            with ExitStack() as own:
                yield lambda name, n: own.enter_context(nc.sbuf_tensor(name, [P, n], dt))[:]

        m = lay_out(sb, both)
        ps = [ctx.enter_context(nc.psum_tensor(f"bank{b}", [P, 512], F32)) for b in range(BANKS)]
        full = [sem(f"bank{b}_full") for b in range(BANKS)]
        free = [sem(f"bank{b}_read") for b in range(BANKS)]
        landed = [sem(f"slot{s}_landed") for s in range(SLOTS)]
        parts = sem("unit_parts_read")
        turn_end = sem("last_turn")

        F = Flags(sem, "a_", {})
        B1 = Banks(full, free, FIRST_JOBS, [0] * BANKS)
        U1 = Units(landed, parts, FIRST_UNITS, [0] * SLOTS, 0, B1)
        M = {n: sem(f"moe_{n}") for n in ("sel", "selg1", "selg", "gathered", "columns", "used", "gate_exp", "silu", "hidden",
                                          "turned", "selgT", "hid_turned", "hidT", "rows", "summed", "added")}
        flags = {}
        N = Flags(sem, "n_", {})
        first_layer = Flags(lambda n: flags[n] if n in flags else flags.setdefault(n, sem(n)), "b_", {})
        steps = {n: sem(f"{n}_step") for n in ("pool", "act", "dve", "pool2", "act2", "dve2")}
        loads = sem("small_loads")
        layer_loads = sem("layer_loads")
        base2, _ = U1.after()
        landed2 = [sem(f"layer_slot{s}_landed") for s in range(SLOTS)]
        parts2 = sem("layer_parts_read")

        def layer_parts(l):
            B = Banks(full, free, LAYER_JOBS, B1.after(), l)
            U = Units(landed2, parts2, LAYER_UNITS, [0] * SLOTS, 0, B, l)
            G = Flags(lambda n: flags[n] if n in flags else flags.setdefault(n, sem(n)), "b_", LAYER_PER, l, LAYER_BEFORE)
            return B, U, G

        raised = {}

        def close(G):
            for n, k in G.raised.items():
                raised[n] = raised.get(n, 0) + k

        block = ctx.enter_context(nc.Block())

        @block.sync
        def _(sp):
            sp.dma_start(m.x, x.rearrange("b (t p) d -> p (b t) d", p=P)).then_inc(F.sem("x_in"), 16)
            sp.dma_start(m.const[:], const).then_inc(F.sem("params"), 16)
            sp.dma_start(m.first_area, first).then_inc(F.sem("params"), 16)
            load_units(sp, U1, m.ring, lambda i: w_first[i])
            sp.wait_ge(*U1.given_back("out.1.1"))
            sp.wait_ge(*F.at("passes"))
            moe_loads(sp, m, M, landed, w_experts)
            turns = sp.value_load(m.r.turns_i[0:1, 1:2], min_val=PAIRS, max_val=PAIRS * PASSES)
            sp.wait_ge(M["used"], (turns + 1) * GROUPS_USED)
            sp.sem_inc(first_layer["ring_free"], 1)
            with sp.Fori(0, LAYERS) as l:
                B, U, G = layer_parts(l)
                load_units(sp, U, m.ring, lambda i: w_layers[bass.ds(l, 1), i], landed2, G.at("ring_free", 0))
                close(G)
            G = layer_parts(LAYERS - 1)[2]
            sp.wait_ge(*G.at("f2.x", 2))
            sp.dma_start(out.rearrange("b (t p) d -> p (b t) d", p=P), m.x).then_inc(loads, 16)
            sp.wait_ge(loads, 16)

        @block.gpsimd
        def _(pool):
            first_pool(pool, Chain(pool, steps["pool"]), m, B1, F)
            pool.wait_ge(*F.at("passes"))
            pool.dma_start(m.second_area, second).then_inc(layer_loads, 16)
            pool.dma_start(m.post[:, 0:D], normf.to_broadcast([P, D])).then_inc(layer_loads, 16)
            pool.wait_ge(*first_layer.at("f2.pss", 2))
            root_of_mean(pool, Chain(pool, steps["pool"], 4), m.ss, m.c["eps"][:, 0:2], m.half[:, 0:2], first_layer["f2.prstd"])
            pool.wait_ge(layer_loads, 32)
            with pool.Fori(0, LAYERS) as l:
                B, U, G = layer_parts(l)
                pool.wait_ge(*G.at("f2.x", 0))
                pool.dma_start(m.layer_area, layer[bass.ds(l, 1)].squeeze(0)).then_inc(layer_loads, 16)
                pool.dma_start(m.post, post[bass.ds(l, 1)].squeeze(0).to_broadcast([P, 3 * D])).then_inc(layer_loads, 16)
                step = Chain(pool, steps["pool2"], 0, POOL_STEPS, l)
                layer_pool(pool, m, B, G, step)
                assert step.n == POOL_STEPS, step.n
                close(G)

        @block.scalar
        def _(act):
            first_scalar(act, Chain(act, steps["act"]), m, ps, B1, F)
            act.wait_ge(*F.at("passes"))
            moe_scalar(act, m, ps, M)
            act.wait_ge(*N.at("moe"))
            square_sums(act, m.x, m.xn, m.ss, lambda: first_layer["f2.pss"])
            with act.Fori(0, LAYERS) as l:
                B, U, G = layer_parts(l)
                step = Chain(act, steps["act2"], 0, ACT_STEPS, l)
                act.wait_ge(layer_loads, l * 32 + 64)
                ffn_scalar(act, step, m, ps, B, U, G, "f1", m.lp["gpre1"])
                mix_scalar(act, step, m, ps, B, G)
                ffn_scalar(act, step, m, ps, B, U, G, "f2", m.lp["gpre2"])
                assert step.n == ACT_STEPS, step.n
                close(G)

        @block.vector
        def _(dve):
            first_vector(dve, Chain(dve, steps["dve"]), m, ps, B1, F)
            dve.wait_ge(*F.at("passes"))
            moe_vector(dve, m, ps, M)
            end = dve.value_load(m.r.turns_i[0:1, 1:2], min_val=PAIRS, max_val=PAIRS * PASSES)
            dve.wait_ge(M["added"], since(end * 4))
            dve.memset(m.r.best, 0.0).then_inc(N["moe"], 1)
            dve.wait_ge(*first_layer.at("f2.prstd"))
            dve.wait_ge(layer_loads, 32)
            for t in range(TT):
                dve.scalar_tensor_tensor(out=m.x[:, t, :], in0=m.x[:, t, :], scalar=m.ss[:, t:t + 1],
                                         in1=m.post[:, 0:D], op0=ALU.mult, op1=ALU.mult).then_inc(first_layer["f2.x"], 1)
            with dve.Fori(0, LAYERS) as l:
                B, U, G = layer_parts(l)
                step = Chain(dve, steps["dve2"], 0, DVE_STEPS, l)
                dve.wait_ge(layer_loads, l * 32 + 64)
                ffn_vector(dve, step, m, ps, B, U, G, "f1", m.lp["gpre1"], m.post[:, 0:D])
                mix_vector(dve, step, m, ps, B, G)
                ffn_vector(dve, step, m, ps, B, U, G, "f2", m.lp["gpre2"], m.post[:, 2 * D:])
                assert step.n == DVE_STEPS, step.n
                close(G)

        @block.tensor
        def _(pe):
            first_tensor(pe, m, ps, B1, U1, F)
            pe.wait_ge(*F.at("passes"))
            moe_tensor(pe, m, ps, M, landed, base2)
            with pe.Fori(0, LAYERS) as l:
                B, U, G = layer_parts(l)
                pe.wait_ge(layer_loads, l * 32 + 64)
                ffn_tensor(pe, m, ps, B, U, G, "f1")
                mix_tensor(pe, m, ps, B, U, G)
                ffn_tensor(pe, m, ps, B, U, G, "f2")
                close(G)
        F.settle()
        N.settle()
        assert first_layer.raised == LAYER_BEFORE, first_layer.raised
        for n, k in raised.items():
            assert k == LAYER_PER.get(n, 1), (n, k)


def bucket(dist):
    exact, far = 16, 128
    d = np.maximum(dist, 1).astype(np.float32)
    large = exact + (np.log(d / np.float32(exact)) / np.float32(math.log(far / exact)) * 16).astype(np.int32)
    return np.where(dist < exact, dist, np.minimum(large, 31))


def cols(v):
    return np.ascontiguousarray(v).reshape(-1, P).T


def rows(v):
    return np.broadcast_to(np.ascontiguousarray(v).reshape(1, -1), (P, v.size))


def on_few(v):
    out = np.zeros((P, 1), v.dtype)
    out[:v.size, 0] = v.reshape(-1)
    return out


def pack(table, parts):
    for name, n in table:
        assert parts[name].shape == (P, n), (name, parts[name].shape)
    return np.concatenate([parts[name] for name, _ in table], axis=1)


def column_units(w, n=256):
    k = w.shape[0] // P
    return w.reshape(k, P, w.shape[1] // n, n).transpose(2, 1, 0, 3).reshape(-1, P, k * n)


def row_unit_pairs(w):
    return w.reshape(2, 4, P, w.shape[1] // 512, 512).transpose(3, 0, 2, 1, 4).reshape(-1, P, UNIT)


def deep_units(w):
    return w.reshape(-1, 2, P, D).transpose(0, 2, 1, 3).reshape(-1, P, UNIT)


def masked_bias(table, dist, keep):
    b = table[bucket(np.maximum(dist, 0))].transpose(0, 2, 1).copy()
    b[np.broadcast_to(~keep[:, None, :], b.shape)] = NEG
    return b.astype(np.float32)


def kernel(**inputs):
    import concourse.bacc as bacc
    from concourse.bass_utils import run_bass_kernel_spmd as run

    a = {k: np.asarray(v) for k, v in inputs.items()}
    q, k = np.arange(P), np.arange(T)
    arrays = {"x": a["x"]}

    ident = np.eye(P, dtype=np.float32)
    arrays["const"] = pack(CONST, {
        "ident": ident, "mask": np.where(q[:, None] <= q[None, :], 0, NEG).astype(np.float32),
        "ones": np.ones((P, T), np.float32), "before": (q[:, None] < q[None, :]).astype(np.float32),
        "slot": rows(np.tile(np.arange(CAP, dtype=np.float32), 2)),
        "eps": np.full((P, 8), EPS, np.float32),
        "prior4": rows(np.arange(4, 0, -1, dtype=np.float32)), "prior8": rows(np.arange(8, 0, -1, dtype=np.float32))})

    dist = k[:, None] - k[None, :]
    bias1 = masked_bias(a["rel_bias"], dist, dist >= 0)
    wr = np.concatenate([a["w_rg"][0], a["w_re"][0].reshape(D, EXPERTS)], axis=1)
    arrays["first"] = pack(FIRST, {
        "g1": cols(a["norm1_g"]), "g2": cols(a["norm2_g"]),
        "convw": a["conv_w"][0].reshape(4, 4, P).transpose(2, 1, 0).reshape(P, 16), "convb": cols(a["conv_b"]),
        "mnorm": cols(a["m_norm_g"]), "mskip": cols(a["m_skip"]),
        "wgate": a["w_mgate"][0].reshape(12, P, 8).transpose(1, 0, 2).reshape(P, 96),
        "bi": on_few(a["b_mgate"][0, :4]), "bf": on_few(a["b_mgate"][0, 4:]), "lam": rows(a["lambda_qk"]),
        "danorm": cols(a["da_norm_g"]), "wroute": wr.reshape(KT, P, 36).transpose(1, 0, 2).reshape(P, KT * 36),
        "broute": rows(np.concatenate([a["b_rg"].ravel(), a["b_re"].ravel()])),
        "wmq": a["w_mq"][0].transpose(1, 0, 2).reshape(P, 512), "wmk": a["w_mk"][0].transpose(1, 0, 2).reshape(P, 512),
        "bias": np.concatenate([bias1[:P, :, :P].reshape(P, -1), bias1[P:].reshape(P, -1)], axis=1)})

    log_g = np.log(1.0 - 2.0 ** (-5.0 - np.arange(RET_H)))
    lag = q[None, :] - q[:, None]
    blocks = [np.where(lag >= 0, np.exp(np.maximum(lag, 0) * g), 0) for g in log_g]
    decay = np.stack([np.concatenate([b, np.exp((lag + P) * g), b], axis=1) for b, g in zip(blocks, log_g)], axis=1)
    inv = (1.0 / (np.float32(10000.0) ** (np.arange(0, 128, 2, dtype=np.float32) / np.float32(128)))).astype(np.float32)
    ang = k.astype(np.float32)[:, None] * inv[None, :]
    band = q[:, None] + P - k[None, :]
    arrays["second"] = pack(SECOND, {
        "decay": decay.reshape(P, -1).astype(np.float32),
        "cos": np.cos(ang).reshape(TT, P, 64).transpose(1, 0, 2).reshape(P, -1).astype(np.float32),
        "sin": np.sin(ang).reshape(TT, P, 64).transpose(1, 0, 2).reshape(P, -1).astype(np.float32),
        "bias": masked_bias(a["rel_bias_2"], band, (band >= 0) & (band < P)).reshape(P, -1)})

    perm = np.arange(D).reshape(2, 8, ATT_D).transpose(1, 0, 2).ravel()
    layers, weights = [], []
    for l in range(LAYERS):
        layers.append(pack(LAYER, {
            "gpre1": cols(a["ffn1_pre_g_2"][l]), "gmix": cols(a["mix_pre_g_2"][l]), "gpre2": cols(a["ffn2_pre_g_2"][l]),
            "convw": a["conv_w_2"][l].reshape(4, CONV_T, P).transpose(2, 1, 0).reshape(P, -1),
            "convb": cols(a["conv_b_2"][l]),
            "wdt": a["w_in_2"][l][:, 2560:2576].reshape(KT, P, 16).transpose(1, 0, 2).reshape(P, -1),
            "gssd": cols(a["ssd_norm_g_2"][l]), "gret": cols(a["ret_gn_g_2"][l]), "bgate": cols(a["b_gate_2"][l]),
            "dtbias": on_few(a["dt_bias_2"][l]), "alog": on_few(a["a_log_2"][l]),
            "dskip": cols(np.repeat(a["d_skip_2"][l], 64)), "sinks": rows(a["attn_sinks_2"][l])}))
        w = a["w_in_2"][l]
        z, xbc, rq, rk, rv, rg, aq, akv, gate = (w[:, i:j] for i, j in (
            (0, 1024), (1024, 2560), (2576, 3088), (3088, 3600), (3600, 4624), (4624, 5648), (5648, 6672),
            (6672, 6928), (6928, 10000)))

        def gated(w_in):
            return column_units(w_in.reshape(D, 2, FT, P).transpose(0, 2, 1, 3).reshape(D, 2 * FF))

        branch = a["w_branch_2"][l]
        pairs = []
        for b in range(3):
            pairs += [column_units(gate[:, b * D:(b + 1) * D]), column_units(branch[b] if b < 2 else branch[b][perm])]
        weights.append(np.concatenate(
            [gated(a["w_ffn1_in_2"][l]), deep_units(a["w_ffn1_out_2"][l])]
            + [row_unit_pairs(v) for v in (rq, rk, rv, rg)]
            + [column_units(v) for v in (xbc, z, aq[:, perm], akv)] + pairs
            + [row_unit_pairs(a["w_out_2"][l]), gated(a["w_ffn2_in_2"][l]), deep_units(a["w_ffn2_out_2"][l])], axis=0))
    arrays["layer"] = np.stack(layers)
    arrays["w_layers"] = np.stack(weights)
    arrays["post"] = np.stack([a[f"{n}_post_g_2"] for n in ("ffn1", "mix", "ffn2")], axis=1).reshape(LAYERS, 1, 3 * D)
    arrays["normf"] = a["normf_g"].reshape(1, D)

    c, v, z, qd, kd, vd = (a["w_in"][0][:, i * 512:(i + 1) * 512] for i in range(6))
    arrays["w_first"] = np.concatenate([column_units(w) for w in (c, v, qd, kd, vd, z)]
                                       + [row_unit_pairs(a["w_out"][0])], axis=0)
    up = [a[n][0].reshape(PAIRS, 2, 2, 4, P, FE).transpose(0, 2, 1, 4, 3, 5).reshape(PAIRS, 4, P, UNIT)
          for n in ("w_eg", "w_eu")]
    down = a["w_ed"][0].reshape(PAIRS, 2, 2, 2, P, D).transpose(0, 2, 1, 4, 3, 5).reshape(PAIRS, 4, P, UNIT)
    arrays["w_experts"] = np.concatenate(up + [down], axis=1)

    nc = bacc.Bacc("TRN2", target_bir_lowering=False, num_devices=1)
    order = ("x", "const", "first", "second", "layer", "post", "normf", "w_first", "w_experts", "w_layers")
    feed, args = {}, []
    for name in order:
        v = np.ascontiguousarray(arrays[name])
        feed[f"in_{name}"] = v
        args.append(nc.dram_tensor(f"in_{name}", v.shape, mybir.dt.from_np(v.dtype), kind="ExternalInput").ap())
    args.append(nc.dram_tensor("out", (1, T, D), F32, kind="ExternalOutput").ap())
    build(nc, *args)
    return run(nc, [feed], core_ids=[0]).results[0]["out"]
```

```python
from contextlib import ExitStack, contextmanager
import math

import concourse.bass as bass
import numpy as np
from concourse import mybir

P = 128
T = 256
TT = T // P
D = 1024
KT = D // P
UNIT = 2048
SLOTS = 6
BANKS = 8
NEG = -1e30

H1 = 4
EXPERTS = 32
GROUPS = 4
PER_GROUP = 8
FE = 512
CAP = 64
PASSES = T // CAP
PAIRS = EXPERTS // 2
LAM_INIT = 0.8 - 0.6 * math.exp(-0.3 * 0)
EPS = 1e-6
SUBLN_EPS = 1e-5

LAYERS = 2
FF = 2816
FT = FF // P
SSD_H = 16
SSD_G = 2
CONV_T = 12
RET_H = 4
ATT_H = 16
ATT_D = 64

ALU = mybir.AluOpType
ACT = mybir.ActivationFunctionType
AX = mybir.AxisListType
F32 = mybir.dt.float32
F32R = mybir.dt.float32r
I32 = mybir.dt.int32
AHEAD_UNITS = 2
HI_BUFFERS = AHEAD_UNITS + 1

CONST = [("ident", P), ("mask", P), ("ones", T), ("before", P), ("slot", 2 * CAP), ("prior4", 4), ("prior8", 8), ("eps", 8)]
FIRST = [("g1", KT), ("g2", KT), ("convw", 16), ("convb", 4), ("mnorm", 4), ("mskip", 4), ("wgate", 96),
         ("bi", 1), ("bf", 1), ("lam", 256), ("danorm", 1), ("wroute", KT * 36), ("broute", 36),
         ("wmq", 512), ("wmk", 512), ("bias", 4 * (P + T))]
SECOND = [("decay", RET_H * 3 * P), ("cos", TT * 64), ("sin", TT * 64), ("bias", ATT_H * 2 * P)]
LAYER = [("gpre1", KT), ("gmix", KT), ("gpre2", KT), ("convw", CONV_T * 4), ("convb", CONV_T), ("wdt", KT * 16),
         ("gssd", KT), ("gret", KT), ("bgate", 3 * KT), ("dtbias", 1), ("alog", 1), ("dskip", KT), ("sinks", ATT_H)]


def offsets(table):
    out, at = {}, 0
    for name, n in table:
        out[name] = (at, n)
        at += n
    return out, at


def place(jobs, banks):
    where, uses = {}, [0] * banks
    for i, name in enumerate(jobs):
        b = i % banks
        assert name not in where, name
        where[name] = (b, uses[b])
        uses[b] += 1
    return where, uses


FIRST_JOBS = ([f"n1.{i}" for i in range(4)]
              + [f"{s}.{i}" for s in ("c", "v", "qd", "kd", "vd", "z") for i in range(2)]
              + [f"vtok.{t}" for t in range(2)] + [f"vdtok.{t}" for t in range(2)]
              + [f"ds0.{c}" for c in range(2)] + [f"ds1.{hp}.{c}" for hp in range(2) for c in range(2)]
              + [f"mq.{i}" for i in range(2)] + [f"mk.{i}" for i in range(2)]
              + ["gates"] + [f"ms.{h}" for h in range(4)]
              + ["gcol", "bc.0", "bc.1"] + ["daT.0", "daT.1", "daT.2"]
              + ["num.0", "num.1", "den"] + ["dout.0", "dout.1"]
              + ["hT.0", "hT.1"] + ["ydT.0", "ydT.1"]
              + [f"out.{n}.{t}" for n in range(2) for t in range(2)]
              + [f"n2.{i}" for i in range(4)] + ["route", "rank"])
FIRST_UNITS = [(f"{s}.{i}", f"{s}.{i}") for s in ("c", "v", "qd", "kd", "vd", "z") for i in range(2)] + \
              [(f"out.{n}.{i}", (None, f"out.{n}.1")[i]) for n in range(2) for i in range(2)]

LAYER_JOBS = ([f"f1.n.{i}" for i in range(4)] + [f"f1.in.{i}" for i in range(FT)]
              + [f"f1.out.{n}.{t}" for n in range(2) for t in range(2)]
              + [f"mx.n.{i}" for i in range(4)]
              + [f"rq.{t}" for t in range(2)] + [f"rk.{t}" for t in range(2)]
              + [f"rv.{n}.{t}" for n in range(2) for t in range(2)]
              + [f"rg.{n}.{t}" for n in range(2) for t in range(2)]
              + [f"xbc.{i}" for i in range(6)]
              + [f"rqT.{i}" for i in range(2)] + [f"rkT.{i}" for i in range(2)]
              + ["dt"] + [f"z.{i}" for i in range(4)] + [f"rs.{h}" for h in range(4)]
              + ["dtcol", "cb.0", "cb.1"] + [f"xst.{i}" for i in range(4)]
              + [f"ro.{t}.{i}" for t in range(2) for i in range(2)]
              + [f"sbc.{i}" for i in range(4)] + [f"aq.{i}" for i in range(3)] + ["sy.0", "sy.1"]
              + [f"sbc.{i}" for i in range(4, 8)] + ["akv", "aq.3"] + [f"rT.{i}" for i in range(4)] + ["sy.2", "sy.3", "ssum"]
              + [f"as.0.{kv}.{i}" for kv in range(2) for i in range(2)]
              + [f"as.1.{kv}.{i}" for kv in range(2) for i in range(4)]
              + [f"g.0.{i}" for i in range(4)] + [f"b.0.{i}" for i in range(4)]
              + [f"ap.0.{kv}.{j}" for kv in range(2) for j in range(2)] + ["ao.0.0", "ao.0.1"]
              + [f"ap.1.{kv}.{j}.{s}" for kv in range(2) for j in range(2) for s in range(2)] + ["ao.1.0", "ao.1.1"]
              + [f"{a}.{m}.{i}" for m in (1, 2) for a in ("g", "b") for i in range(4)]
              + [f"mx.out.{n}.{t}" for n in range(2) for t in range(2)]
              + [f"f2.n.{i}" for i in range(4)] + [f"f2.in.{i}" for i in range(FT)]
              + [f"f2.out.{n}.{t}" for n in range(2) for t in range(2)])


MIX_SPLIT = ([f"{r}.{i}" for r in ("rq", "rk") for i in range(2)]
             + [f"{r}.{n}.{i}" for r in ("rv", "rg") for n in range(2) for i in range(2)] + [f"xbc.{i}" for i in range(6)])
END_SPLIT = ([f"{a}.{b}.{i}" for b in (1, 2) for a in ("g", "b") for i in range(4)]
             + [f"mx.out.{n}.{i}" for n in range(2) for i in range(2)])
SPLIT_BEFORE = {"f1": 0, "mx": FT + FT // 2, "end": FT + FT // 2 + len(MIX_SPLIT),
                "f2": FT + FT // 2 + len(MIX_SPLIT) + len(END_SPLIT)}
SPLITS = SPLIT_BEFORE["f2"] + FT + FT // 2


def row_units(name, jobs):
    return [(f"{name}.0", None), (f"{name}.1", jobs)]


def ffn_units(f):
    return ([(f"{f}.in.{i}", f"{f}.in.{i}") for i in range(FT)]
            + [(f"{f}.out.{i}", None if i < FT // 2 - 1 else f"{f}.out.1.1") for i in range(FT // 2)])


LAYER_UNITS = (ffn_units("f1") + row_units("rq", "rq.1") + row_units("rk", "rk.1")
               + [u for r in ("rv", "rg") for n in range(2) for u in row_units(f"{r}.{n}", f"{r}.{n}.1")]
               + [(f"xbc.{i}", f"xbc.{i}") for i in range(6)] + [(f"z.{i}", f"z.{i}") for i in range(4)]
               + [(f"aq.{i}", f"aq.{i}") for i in range(3)] + [("akv", "akv"), ("aq.3", "aq.3")]
               + [(f"{a}.{m}.{i}", f"{a}.{m}.{i}") for m in range(3) for a in ("g", "b") for i in range(4)]
               + [u for n in range(2) for u in row_units(f"mx.out.{n}", f"mx.out.{n}.1")]
               + ffn_units("f2"))


class Banks:

    def __init__(self, full_sems, free_sems, jobs, base, l=None):
        self.full_sems, self.free_sems, self.base, self.l = full_sems, free_sems, base, l
        self.where, self.uses = place(jobs, BANKS)

    def bank(self, job):
        return self.where[job][0]

    def count(self, job, extra):
        b, use = self.where[job]
        n = self.base[b] + use + extra
        return n if self.l is None else self.l * self.uses[b] + n

    def full(self, job):
        return self.full_sems[self.bank(job)]

    def free(self, job):
        return self.free_sems[self.bank(job)]

    def filled(self, job):
        return self.full(job), self.count(job, 1)

    def drained(self, job):
        return self.free(job), self.count(job, 1)

    def claim(self, pe, job):
        b, use = self.where[job]
        if self.base[b] + use:
            pe.wait_ge(self.free(job), self.count(job, 0))

    def after(self):
        return [x + y for x, y in zip(self.base, self.uses)]


class Units:

    def __init__(self, landed_sems, parts_sem, units, base, parts_base, B, l=None):
        self.landed_sems, self.parts_sem, self.base, self.B, self.l = landed_sems, parts_sem, base, B, l
        self.parts_base = parts_base
        self.names = [n for n, _ in units]
        self.ends = dict(units)
        self.index = {n: i for i, n in enumerate(self.names)}
        self.per = [len(range(s, len(units), SLOTS)) for s in range(SLOTS)]
        parts = [n for n in self.names if self.ends[n] is None]
        self.part = {n: i for i, n in enumerate(parts)}

    def slot(self, name):
        return self.index[name] % SLOTS

    def landed(self, name):
        i = self.index[name]
        n = self.base[i % SLOTS] + i // SLOTS + 1
        n = n if self.l is None else self.l * self.per[i % SLOTS] + n
        return self.landed_sems[self.slot(name)], n * 16

    def given_back(self, name):
        if self.ends[name] is not None:
            return self.B.filled(self.ends[name])
        n = self.parts_base + self.part[name] + 1
        return self.parts_sem, (n if self.l is None else self.l * len(self.part) + n)

    def after(self):
        return [x + y for x, y in zip(self.base, self.per)], self.parts_base + len(self.part)


class Flags:

    def __init__(self, make, prefix, per, l=None, before={}):
        self.make, self.prefix, self.per, self.l, self.before = make, prefix, per, l, before
        self.sems, self.raised, self.asked = {}, {}, {}

    def sem(self, name):
        if name not in self.sems:
            self.sems[name] = self.make(f"{self.prefix}{name}")
        return self.sems[name]

    def __getitem__(self, name):
        self.raised[name] = self.raised.get(name, 0) + 1
        return self.sem(name)

    def at(self, name, k=1):
        self.asked[name] = max(k, self.asked.get(name, 0))
        n = k + self.before.get(name, 0)
        assert n > 0, name
        return self.sem(name), (n if self.l is None else self.l * self.per.get(name, 1) + n)

    def settle(self):
        for name, n in self.raised.items():
            assert self.l is None or n == self.per.get(name, 1), (self.prefix, name, n)
        for name, k in self.asked.items():
            assert k <= self.raised.get(name, 0), (self.prefix, name, k)


class Chain:

    def __init__(self, engine, sem, base=0, per=0, l=None):
        self.engine, self.sem, self.base, self.per, self.l, self.n = engine, sem, base, per, l, 0

    def __call__(self, ins):
        self.n += 1
        n = self.base + self.n
        ins.then_inc(self.sem, 1)
        self.engine.wait_ge(self.sem, n if self.l is None else self.l * self.per + n)


def bc(ap, shape):
    while len(ap.shape) < len(shape):
        ap = ap.unsqueeze(len(ap.shape))
    return ap.to_broadcast(shape)


def split(ap, n):
    return ap.rearrange("p (n b) -> p n b", n=n)


class Memory:

    def __init__(self, area):
        self.area, self.at, self.high = area, 0, 0

    def take(self, n):
        ap = self.area[:, self.at:self.at + n]
        self.at += n
        self.high = max(self.high, self.at)
        return ap



def square_sums(act, x, scratch, sums, flag):
    for t in range(TT):
        act.activation(scratch[:, t, :], x[:, t, :], ACT.Square, scale=D ** -0.5, accum_out=sums[:, t:t + 1]).then_inc(flag(), 1)


def root_of_mean(pool, step, out, eps, minus_half, flag):
    step(pool.tensor_tensor(out, out, eps, ALU.add))
    pool.tensor_tensor(out, out, minus_half, ALU.pow).then_inc(flag, 1)


def inverse_root(pool, step, out, sums, minus_half, width, eps, flag):
    step(pool.tensor_scalar(out, sums, 1.0 / width, eps, ALU.mult, ALU.add))
    pool.tensor_tensor(out, out, minus_half, ALU.pow).then_inc(flag, 1)


def turn_rows(pe, B, names, ps, src, ident, F, f):
    for job in names:
        B.claim(pe, job)
    for t in range(TT):
        pe.wait_ge(*F.at(f"{f}.xn", t + 1))
        for i, job in enumerate(names):
            for k in range(2):
                mm = pe.transpose(ps[B.bank(job)][:, k * T + t * P:k * T + t * P + P],
                                  src[:, t, (2 * i + k) * P:(2 * i + k + 1) * P], ident)
            if t == TT - 1:
                mm.then_inc(B.full(job), 1)


def take_columns(eng, B, names, ps, dst, gain, odd):
    for i, job in enumerate(names):
        if i % 2 != odd:
            continue
        eng.wait_ge(*B.filled(job))
        bank = split(ps[B.bank(job)][:], 2)
        if not odd:
            eng.tensor_tensor(dst[:, 2 * i:2 * i + 2, :], bank, bc(gain[:, 2 * i:2 * i + 2], [P, 2, T]),
                              ALU.mult).then_inc(B.free(job), 1)
        else:
            for k in range(2):
                ins = eng.activation(dst[:, 2 * i + k, :], bank[:, k, :], ACT.Copy,
                                     scale=gain[:, 2 * i + k:2 * i + k + 1])
            ins.then_inc(B.free(job), 1)


def wait_columns(pe, B, names):
    for job in names:
        pe.wait_ge(*B.drained(job))


def project_columns(pe, B, U, ps, ring, job, unit, moving):
    B.claim(pe, job)
    pe.wait_ge(*U.landed(unit))
    w = ring[U.slot(unit)].rearrange("p (k n) -> p k n", k=KT)
    for c in range(2):
        for k in range(KT):
            mm = pe.matmul(ps[B.bank(job)][:, c * T:(c + 1) * T], w[:, k, c * P:(c + 1) * P], moving[:, k, :],
                           start=k == 0, stop=k == KT - 1)
    mm.then_inc(B.full(job), 1)


def project_rows(pe, B, U, ps, ring, jobs, units, held):
    for u, unit in enumerate(units):
        pe.wait_ge(*U.landed(unit))
        w = ring[U.slot(unit)].rearrange("p (k n) -> p k n", k=KT // 2)
        for t in range(TT):
            if u == 0:
                B.claim(pe, jobs[t])
            for k in range(KT // 2):
                kk = u * (KT // 2) + k
                mm = pe.matmul(ps[B.bank(jobs[t])][:], held[:, kk, t * P:(t + 1) * P], w[:, k, :],
                               start=kk == 0, stop=kk == KT - 1)
            if u == 1:
                mm.then_inc(B.full(jobs[t]), 1)
            elif t == TT - 1:
                mm.then_inc(U.parts_sem, 1)


def load_units(sp, U, ring, source, last_turn=None):
    for i, name in enumerate(U.names):
        if i >= SLOTS:
            sp.wait_ge(*U.given_back(U.names[i - SLOTS]))
        elif i == 0 and last_turn is not None:
            sp.wait_ge(*last_turn)
        sp.dma_start(ring[i % SLOTS], source(i)).then_inc(U.landed_sems[i % SLOTS], 16)


def sigmoid_tail(act, step, e, flag):
    step(act.activation(e, e, ACT.Ln, bias=1.0))
    act.activation(e, e, ACT.Exp, scale=-1.0).then_inc(flag, 1)



def first_scalar(act, step, m, ps, B, F):
    act.wait_ge(F.sem("x_in"), 16)
    square_sums(act, m.x, m.xn, m.ss, lambda: F["n1.ss"])
    act.wait_ge(F.sem("params"), 32)
    take_columns(act, B, [f"n1.{i}" for i in range(4)], ps, m.hT, m.p["g1"], 1)
    for name in ("v", "qd", "kd", "vd"):
        if name == "kd":
            act.wait_ge(*F.at("conv", 4))
            step(act.activation(m.ec, m.cv, ACT.Exp, scale=-1.0))
            sigmoid_tail(act, step, m.ec, F["conv_sig"])
        for i in range(2):
            job = f"{name}.{i}"
            act.wait_ge(*B.filled(job))
            act.activation(m.cols[name][:, 2 * i:2 * i + 2, :], split(ps[B.bank(job)][:], 2),
                           ACT.Copy).then_inc(B.free(job), 1)
    for i in range(2):
        act.wait_ge(*B.filled(f"z.{i}"))
        act.activation(m.ez[:, 2 * i:2 * i + 2, :], split(ps[B.bank(f"z.{i}")][:], 2), ACT.Exp,
                       scale=-1.0).then_inc(B.free(f"z.{i}"), 1)
    act.wait_ge(*F.at("lam_dots", 2))
    act.activation(m.lam[:, 2:4], m.lam[:, 0:2], ACT.Exp).then_inc(F["lam_exp"], 1)
    for t in range(TT):
        for h in range(H1):
            for c in range(2):
                n = (t * 2 + c) * H1 + h
                act.wait_ge(*F.at("ds_max", 2 if t == 0 else 2 + 2 * (h // 2) + c + 1))
                s = m.dp[t][:, c, h, :]
                act.activation(s, s, ACT.Exp, bias=m.dmax[:, n:n + 1],
                               accum_out=m.dsum[:, n:n + 1]).then_inc(F["ds_exp"], 1)
    for name, dst in (("mq", m.mq), ("mk", m.mk)):
        for i in range(2):
            job = f"{name}.{i}"
            act.wait_ge(*B.filled(job))
            act.activation(dst[:, 2 * i:2 * i + 2, :], split(ps[B.bank(job)][:], 2),
                           ACT.Copy).then_inc(B.free(job), 1)
    for i in range(2):
        act.wait_ge(*B.drained(f"z.{i}"))
    sigmoid_tail(act, step, m.ez, F["sig_z"])
    act.wait_ge(*F.at("absf"))
    step(act.activation(m.frow[1][0:4, :], m.frow[1][0:4, :], ACT.Exp, scale=-1.0))
    act.activation(m.frow[1][0:4, :], m.frow[1][0:4, :], ACT.Ln, bias=1.0).then_inc(F["softplus"], 1)
    act.wait_ge(*B.drained("gcol"))
    act.activation(m.em, m.gcol[:, 8:16], ACT.Exp, scale=-1.0).then_inc(F["em"], 1)
    for h in range(H1):
        act.wait_ge(*B.drained(f"bc.{h // 2}"))
        for st, lo, hi in ((0, 0, T), (1, T, T + P)):
            e = m.me[:, h, lo:hi]
            act.activation(e, e, ACT.Exp, bias=m.gcol[:, st * 4 + h:st * 4 + h + 1]).then_inc(F["me"], 1)
    act.wait_ge(*F.at("h_centred"))
    act.activation(m.hsq, m.hm, ACT.Square).then_inc(F["h_sq"], 1)
    for t in range(TT):
        act.wait_ge(*B.filled(f"dout.{t}"))
        act.activation(m.yd[:, t, :], ps[B.bank(f"dout.{t}")][:], ACT.Copy).then_inc(B.free(f"dout.{t}"), 1)
    act.wait_ge(*B.drained("dout.1"))
    act.wait_ge(*F.at("h_var"))
    act.activation(m.hsq, m.yd, ACT.Square).then_inc(F["d_sq"], 1)
    for n in range(2):
        for t in range(TT):
            act.wait_ge(*B.drained(f"out.{n}.{t}"))
    square_sums(act, m.x, m.xn, m.ss, lambda: F["n2.ss"])
    take_columns(act, B, [f"n2.{i}" for i in range(4)], ps, m.hT, m.p["g2"], 1)
    act.wait_ge(*F.at("lg_max"))
    for t in range(TT):
        act.activation(m.r.eg[:, t, :], m.r.lg[:, t, 0:4], ACT.Exp, bias=m.r.nmg[:, t:t + 1],
                       accum_out=m.r.sg[:, t:t + 1]).then_inc(F["lg_exp"], 1)
    act.wait_ge(*F.at("le_diff"))
    act.activation(m.r.e2, m.r.e2, ACT.Exp).then_inc(F["le_exp"], 1)


def first_pool(pool, step, m, B, F):
    pool.memset(m.half, -0.5).then_inc(F["half"], 1)
    pool.wait_ge(*F.at("half"))
    pool.wait_ge(F.sem("params"), 32)
    pool.wait_ge(*F.at("n1.ss", 2))
    root_of_mean(pool, step, m.ss, m.c["eps"][:, 0:2], m.half[:, 0:2], F["n1.rstd"])
    pool.wait_ge(*F.at("h_var"))
    inverse_root(pool, step, m.hv, m.hv, m.half[:, 0:8], P, EPS, F["h_rstd"])
    pool.wait_ge(*F.at("d_var"))
    inverse_root(pool, step, m.dv, m.dv, m.half[:, 0:8], P, SUBLN_EPS, F["d_rstd"])
    pool.wait_ge(*F.at("n2.ss", 2))
    root_of_mean(pool, step, m.ss, m.c["eps"][:, 0:2], m.half[:, 0:2], F["n2.rstd"])


def first_vector(dve, step, m, ps, B, F):
    p = m.p
    dve.memset(m.cpad[:, :, 0:3], 0.0).then_inc(F["pad"], 1)
    dve.wait_ge(F.sem("params"), 32)
    for i in range(2):
        dve.tensor_tensor_reduce(m.lamj[:, i * 64:(i + 1) * 64], p["lam"][:, i * 128:i * 128 + 64],
                                 p["lam"][:, i * 128 + 64:i * 128 + 128], 1.0, 0.0, ALU.mult, ALU.add,
                                 m.lam[:, i:i + 1]).then_inc(F["lam_dots"], 1)
    dve.wait_ge(*F.at("n1.rstd"))
    dve.wait_ge(F.sem("x_in"), 16)
    for t in range(TT):
        dve.tensor_scalar(m.xn[:, t, :], m.x[:, t, :], m.ss[:, t:t + 1], None, ALU.mult).then_inc(F["n1.xn"], 1)
    take_columns(dve, B, [f"n1.{i}" for i in range(4)], ps, m.hT, p["g1"], 0)
    for i in range(2):
        dve.wait_ge(*B.filled(f"c.{i}"))
        dve.tensor_copy(m.cpad[:, 2 * i:2 * i + 2, 3:], split(ps[B.bank(f"c.{i}")][:], 2)).then_inc(B.free(f"c.{i}"), 1)
    dve.wait_ge(*B.drained("c.1"))
    dve.wait_ge(*F.at("pad"))
    for i in range(4):
        causal_conv(dve, step, m.cv[:, i, :], m.cpad[:, i, :], p["convw"][:, 4 * i:4 * i + 4],
                    p["convb"][:, i:i + 1], F["conv"])
    dve.wait_ge(*F.at("conv_sig"))
    dve.tensor_tensor(m.cv, m.cv, m.ec, ALU.mult).then_inc(F["cact"], 1)
    for name, dst in (("vtok", m.vtok), ("vdtok", m.vdtok)):
        for t in range(TT):
            job = f"{name}.{t}"
            dve.wait_ge(*B.filled(job))
            dve.tensor_copy(dst[:, t, :], ps[B.bank(job)][:]).then_inc(B.free(job), 1)
    scale = 64 ** -0.5
    bias0 = p["bias"][:, 0:H1 * P].rearrange("p (h k) -> p h k", h=H1)
    bias1 = p["bias"][:, H1 * P:].rearrange("p (h k) -> p h k", h=H1)
    for c in range(2):
        job = f"ds0.{c}"
        dve.wait_ge(*B.filled(job))
        dve.scalar_tensor_tensor(out=m.dp[0][:, c, :, :], in0=split(ps[B.bank(job)][:], 4), scalar=scale,
                                 in1=bias0, op0=ALU.mult, op1=ALU.add).then_inc(B.free(job), 1)
        dve.wait_ge(*B.drained(job))
        dve.tensor_reduce(m.dmax[:, c * 4:c * 4 + 4], m.dp[0][:, c, :, :], AX.X, ALU.max,
                          negate=True).then_inc(F["ds_max"], 1)
    for hp in range(2):
        for c in range(2):
            job = f"ds1.{hp}.{c}"
            dve.wait_ge(*B.filled(job))
            dst = m.dp[1][:, c, 2 * hp:2 * hp + 2, :]
            dve.scalar_tensor_tensor(out=dst, in0=split(ps[B.bank(job)][:], 2), scalar=scale,
                                     in1=bias1[:, 2 * hp:2 * hp + 2, :], op0=ALU.mult,
                                     op1=ALU.add).then_inc(B.free(job), 1)
            dve.wait_ge(*B.drained(job))
            n = 8 + c * 4 + 2 * hp
            dve.tensor_reduce(m.dmax[:, n:n + 2], dst, AX.X, ALU.max, negate=True).then_inc(F["ds_max"], 1)
    dve.wait_ge(*B.filled("gates"))
    gate = ps[B.bank("gates")]
    irow, row1, row2, frow, neg_m, bm = m.frow
    dve.tensor_scalar(irow[0:4, :], gate[0:4, 0:T], p["bi"][0:4, :], None, ALU.add).then_inc(F["irow"], 1)
    dve.tensor_scalar(frow[0:4, :], gate[0:4, T:2 * T], p["bf"][0:4, :], None, ALU.add).then_inc(B.free("gates"), 1)
    dve.wait_ge(*B.drained("gates"))
    magnitude(dve, row1[0:4, :], frow[0:4, :]).then_inc(F["absf"], 1)
    dve.tensor_scalar(row2[0:4, :], frow[0:4, :], 0.0, None, ALU.min).then_inc(F["minf"], 1)
    dve.wait_ge(*F.at("softplus"))
    dve.wait_ge(*F.at("minf"))
    step(dve.tensor_tensor(frow[0:4, :], row2[0:4, :], row1[0:4, :], ALU.subtract))
    step(dve.tensor_tensor_scan(row2[0:4, :], m.c["ones"][0:4, :], frow[0:4, :], 0.0, ALU.mult, ALU.add))
    dve.wait_ge(*F.at("irow"))
    step(dve.tensor_tensor(irow[0:4, :], irow[0:4, :], row2[0:4, :], ALU.subtract))
    step(dve.tensor_tensor_scan(row1[0:4, :], irow[0:4, :], irow[0:4, :], 0.0, ALU.max, ALU.max))
    dve.tensor_scalar(neg_m[0:4, :], row1[0:4, :], -1.0, None, ALU.mult).then_inc(F["rows"], 1)
    dve.tensor_tensor(bm[0:4, :], row1[0:4, :], row2[0:4, :], ALU.add).then_inc(F["rows"], 1)
    dve.wait_ge(*B.filled("gcol"))
    dve.tensor_copy(m.gcol, ps[B.bank("gcol")][:, 0:16]).then_inc(B.free("gcol"), 1)
    for i in range(2):
        job = f"bc.{i}"
        dve.wait_ge(*B.filled(job))
        spread_and_mask(dve, split(ps[B.bank(job)][:], 2), m.me[:, 2 * i:2 * i + 2, :], m.c["mask"], B.free(job))
    dve.wait_ge(*F.at("lam_exp"))
    step(dve.tensor_tensor(m.lam[:, 4:5], m.lam[:, 3:4], m.lam[:, 2:3], ALU.subtract))
    step(dve.tensor_scalar(m.lam[:, 4:5], m.lam[:, 4:5], -LAM_INIT, None, ALU.add))
    dve.wait_ge(*F.at("ds_exp", 16))
    step(dve.reciprocal(m.dsum, m.dsum))
    for t in range(TT):
        o = t * 8 + 4
        step(dve.tensor_scalar(m.dsum[:, o:o + 4], m.dsum[:, o:o + 4], m.lam[:, 4:5], None, ALU.mult))
    for t in range(TT):
        for c in range(2):
            r = m.dsum[:, t * 8 + c * 4:t * 8 + c * 4 + 4]
            step(dve.tensor_tensor(m.dp[t][:, c, :, :], m.dp[t][:, c, :, :], bc(r, [P, H1, (t + 1) * P]), ALU.mult))
        dve.tensor_tensor(m.dp[t][:, 0, :, :], m.dp[t][:, 0, :, :], m.dp[t][:, 1, :, :], ALU.add).then_inc(F["da"], 1)
    for h in range(H1):
        dve.wait_ge(*F.at("me", 2 * h + 2))
        dve.wait_ge(*B.filled(f"ms.{h}"))
        dve.scalar_tensor_tensor(out=m.me[:, h, :], in0=ps[B.bank(f"ms.{h}")][:, 0:3 * P], scalar=P ** -0.5,
                                 in1=m.me[:, h, :], op0=ALU.mult, op1=ALU.mult).then_inc(B.free(f"ms.{h}"), 1)
    for i in range(3):
        job = f"daT.{i}"
        dve.wait_ge(*B.filled(job))
        dve.tensor_copy(m.daT[:, i, :], ps[B.bank(job)][:]).then_inc(B.free(job), 1)
    dve.wait_ge(*F.at("em"))
    dve.wait_ge(*B.filled("den"))
    dve.tensor_copy(m.den, ps[B.bank("den")][:, 0:8]).then_inc(B.free("den"), 1)
    dve.wait_ge(*B.drained("den"))
    step(magnitude(dve, m.den, m.den))
    step(dve.tensor_tensor(m.den, m.den, m.em, ALU.max))
    step(dve.reciprocal(m.den, m.den))
    for t in range(TT):
        job = f"num.{t}"
        dve.wait_ge(*B.filled(job))
        dve.tensor_tensor(m.hm[:, 4 * t:4 * t + 4, :], split(ps[B.bank(job)][:], 4),
                          bc(m.den[:, 4 * t:4 * t + 4], [P, 4, P]), ALU.mult).then_inc(B.free(job), 1)
        dve.wait_ge(*B.drained(job))
    centre(dve, step, m.hm, m.hv, P, F["h_centred"])
    dve.wait_ge(*F.at("h_sq"))
    dve.tensor_reduce(m.hv, m.hsq, AX.X, ALU.add).then_inc(F["h_var"], 1)
    dve.wait_ge(*F.at("h_rstd"))
    dve.tensor_tensor(m.hm, m.hm, bc(m.hv, [P, 8, P]), ALU.mult).then_inc(F["hn"], 1)
    for h in range(H1):
        step(dve.tensor_scalar(m.cv[:, h, :], m.cv[:, h, :], p["mskip"][:, h:h + 1], None, ALU.mult))
    for i in range(2):
        job = f"hT.{i}"
        dve.wait_ge(*B.filled(job))
        for k in range(2):
            h = 2 * i + k
            ins = dve.scalar_tensor_tensor(out=m.yT[:, h, :], in0=ps[B.bank(job)][:, k * T:(k + 1) * T],
                                           scalar=p["mnorm"][:, h:h + 1], in1=m.cv[:, h, :], op0=ALU.mult,
                                           op1=ALU.add)
        ins.then_inc(B.free(job), 1)
        dve.wait_ge(*B.drained(job))
    dve.wait_ge(*F.at("sig_z"))
    dve.tensor_tensor(m.yT[:, 0:4, :], m.yT[:, 0:4, :], m.ez, ALU.mult).then_inc(F["ym"], 1)
    dve.wait_ge(*F.at("d_sq"))
    dve.tensor_reduce(m.dv, m.hsq, AX.X, ALU.add).then_inc(F["d_var"], 1)
    dve.wait_ge(*F.at("d_rstd"))
    dve.tensor_tensor(m.ydh, m.ydh, bc(m.dv, [P, 8, P]), ALU.mult).then_inc(F["dn"], 1)
    for i in range(2):
        job = f"ydT.{i}"
        dve.wait_ge(*B.filled(job))
        dve.tensor_scalar(m.yT[:, 4 + 2 * i:6 + 2 * i, :], split(ps[B.bank(job)][:], 2), p["danorm"], 1.0 - LAM_INIT,
                          ALU.mult, ALU.mult).then_inc(B.free(job), 1)
    for n in range(2):
        for t in range(TT):
            job = f"out.{n}.{t}"
            dve.wait_ge(*B.filled(job))
            xs = m.x[:, t, n * 512:(n + 1) * 512]
            dve.tensor_tensor(xs, xs, ps[B.bank(job)][:], ALU.add).then_inc(B.free(job), 1)
    dve.wait_ge(*F.at("n2.rstd"))
    for t in range(TT):
        dve.tensor_scalar(m.xn[:, t, :], m.x[:, t, :], m.ss[:, t:t + 1], None, ALU.mult).then_inc(F["n2.xn"], 1)
    take_columns(dve, B, [f"n2.{i}" for i in range(4)], ps, m.hT, p["g2"], 0)
    route_vector(dve, step, m, ps, B, F)


def magnitude(dve, out, x):
    return dve.scalar_tensor_tensor(out=out, in0=x, scalar=-1.0, in1=x, op0=ALU.mult, op1=ALU.max)


def causal_conv(dve, step, out, padded, w, b, flag):
    step(dve.tensor_scalar(out, padded[:, 0:T], w[:, 0:1], b, ALU.mult, ALU.add))
    for j in range(1, 4):
        ins = dve.scalar_tensor_tensor(out=out, in0=padded[:, j:j + T], scalar=w[:, j:j + 1], in1=out,
                                       op0=ALU.mult, op1=ALU.add)
        if j < 3:
            step(ins)
    ins.then_inc(flag, 1)


def spread_and_mask(dve, bank, out, mask, flag):
    both = mask.unsqueeze(1).to_broadcast([P, 2, P])
    dve.tensor_tensor(out[:, :, 0:P], bank[:, :, 0:P], both, ALU.add)
    dve.tensor_copy(out[:, :, P:T], bank[:, :, P:T])
    dve.tensor_tensor(out[:, :, T:T + P], bank[:, :, P:T], both, ALU.add).then_inc(flag, 1)


def centre(dve, step, x, stat, width, flag):
    step(dve.tensor_reduce(stat, x, AX.X, ALU.add, negate=True))
    step(dve.tensor_scalar(stat, stat, 1.0 / width, None, ALU.mult))
    dve.tensor_tensor(x, x, bc(stat, list(x.shape)), ALU.add).then_inc(flag, 1)


def first_tensor(pe, m, ps, B, U, F):
    ident = m.c["ident"]
    ring = m.ring
    pe.wait_ge(F.sem("params"), 32)
    turn_rows(pe, B, [f"n1.{i}" for i in range(4)], ps, m.xn, ident, F, "n1")
    wait_columns(pe, B, [f"n1.{i}" for i in range(4)])
    for name in ("c", "v", "qd", "kd", "vd", "z"):
        for i in range(2):
            project_columns(pe, B, U, ps, ring, f"{name}.{i}", f"{name}.{i}", m.hT)
    for name, src in (("vtok", "v"), ("vdtok", "vd")):
        for i in range(2):
            pe.wait_ge(*B.drained(f"{src}.{i}"))
        for t in range(TT):
            job = f"{name}.{t}"
            B.claim(pe, job)
            for h in range(H1):
                mm = pe.transpose(ps[B.bank(job)][:, h * P:(h + 1) * P], m.cols[src][:, h, t * P:(t + 1) * P], ident)
            mm.then_inc(B.full(job), 1)
    for i in range(2):
        pe.wait_ge(*B.drained(f"kd.{i}"))
    qd, kd = m.cols["qd"], m.cols["kd"]
    for c in range(2):
        job = f"ds0.{c}"
        B.claim(pe, job)
        for h in range(H1):
            mm = pe.matmul(ps[B.bank(job)][:, h * P:(h + 1) * P], qd[c * 64:c * 64 + 64, h, 0:P],
                           kd[c * 64:c * 64 + 64, h, 0:P], start=True, stop=True)
        mm.then_inc(B.full(job), 1)
    for hp in range(2):
        for c in range(2):
            job = f"ds1.{hp}.{c}"
            B.claim(pe, job)
            for k in range(2):
                h = 2 * hp + k
                mm = pe.matmul(ps[B.bank(job)][:, k * T:(k + 1) * T], qd[c * 64:c * 64 + 64, h, P:T],
                               kd[c * 64:c * 64 + 64, h, :], start=True, stop=True)
            mm.then_inc(B.full(job), 1)
    pe.wait_ge(*F.at("cact"))
    for name, w in (("mq", m.p["wmq"]), ("mk", m.p["wmk"])):
        for i in range(2):
            job = f"{name}.{i}"
            B.claim(pe, job)
            for k in range(2):
                h = 2 * i + k
                mm = pe.matmul(ps[B.bank(job)][:, k * T:(k + 1) * T], w[:, h * P:(h + 1) * P], m.cv[:, h, :],
                               start=True, stop=True)
            mm.then_inc(B.full(job), 1)
    for i in range(2):
        pe.wait_ge(*B.drained(f"mq.{i}"))
        pe.wait_ge(*B.drained(f"mk.{i}"))
    B.claim(pe, "gates")
    wgate = m.p["wgate"].rearrange("p (k n) -> p k n", k=12)
    for half in range(2):
        for k in range(12):
            src = (m.mq, m.mk, m.cols["v"])[k // 4]
            mm = pe.matmul(ps[B.bank("gates")][0:4, half * T:(half + 1) * T], wgate[:, k, half * 4:half * 4 + 4],
                           src[:, k % 4, :], start=k == 0, stop=k == 11)
    mm.then_inc(B.full("gates"), 1)
    for h in range(H1):
        causal_scores(pe, B, ps, f"ms.{h}", m.mk[:, h, :], m.mq[:, h, :])
    pe.wait_ge(*F.at("rows", 2))
    B.claim(pe, "gcol")
    for half, row in enumerate((m.frow[0], m.frow[5])):
        for t in range(TT):
            o = half * 8 + t * 4
            mm = pe.transpose(ps[B.bank("gcol")][:, o:o + 4], row[0:4, t * P:(t + 1) * P], ident[0:4, 0:4])
    mm.then_inc(B.full("gcol"), 1)
    for i in range(2):
        spread_rows(pe, B, ps, f"bc.{i}", m.frow[4], ident, 4, 2 * i)
    for i in range(3):
        job = f"daT.{i}"
        B.claim(pe, job)
        pe.wait_ge(*F.at("da", 1 if i == 0 else 2))
        for k in range(4):
            src = m.dp[0][:, 0, k, :] if i == 0 else m.dp[1][:, 0, 2 * (i - 1) + k // 2, (k % 2) * P:(k % 2 + 1) * P]
            mm = pe.transpose(ps[B.bank(job)][:, k * P:(k + 1) * P], src, ident)
        mm.then_inc(B.full(job), 1)
    for h in range(H1):
        pe.wait_ge(*B.drained(f"ms.{h}"))
    for t in range(TT):
        pe.wait_ge(*B.drained(f"vtok.{t}"))
    for t in range(TT):
        job = f"num.{t}"
        B.claim(pe, job)
        for h in range(H1):
            for s in range(t + 1):
                w = m.me[:, h, (t + s) * P:(t + s + 1) * P]
                mm = pe.matmul(ps[B.bank(job)][:, h * P:(h + 1) * P], w, m.vtok[:, s, h * P:(h + 1) * P],
                               start=s == 0, stop=s == t)
        mm.then_inc(B.full(job), 1)
    B.claim(pe, "den")
    for t in range(TT):
        for h in range(H1):
            for s in range(t + 1):
                w = m.me[:, h, (t + s) * P:(t + s + 1) * P]
                mm = pe.matmul(ps[B.bank("den")][:, t * 4 + h:t * 4 + h + 1], w, m.c["ones"][:, 0:1],
                               start=s == 0, stop=s == t)
    mm.then_inc(B.full("den"), 1)
    for i in range(3):
        pe.wait_ge(*B.drained(f"daT.{i}"))
    for t in range(TT):
        pe.wait_ge(*B.drained(f"vdtok.{t}"))
    for t in range(TT):
        job = f"dout.{t}"
        B.claim(pe, job)
        for h in range(H1):
            for s in range(t + 1):
                w = m.daT[:, 0, h * P:(h + 1) * P] if t == 0 else \
                    m.daT[:, 1 + h // 2, ((h % 2) * 2 + s) * P:((h % 2) * 2 + s + 1) * P]
                mm = pe.matmul(ps[B.bank(job)][:, h * P:(h + 1) * P], w, m.vdtok[:, s, h * P:(h + 1) * P],
                               start=s == 0, stop=s == t)
        mm.then_inc(B.full(job), 1)
    for name, src, ready in (("hT", m.hm, "hn"), ("ydT", m.ydh, "dn")):
        pe.wait_ge(*F.at(ready))
        for i in range(2):
            job = f"{name}.{i}"
            B.claim(pe, job)
            for k in range(2):
                for t in range(TT):
                    mm = pe.transpose(ps[B.bank(job)][:, k * T + t * P:k * T + t * P + P],
                                      src[:, t * 4 + 2 * i + k, :], ident)
            mm.then_inc(B.full(job), 1)
    pe.wait_ge(*F.at("ym"))
    for i in range(2):
        pe.wait_ge(*B.drained(f"ydT.{i}"))
    for n in range(2):
        project_rows(pe, B, U, ps, ring, [f"out.{n}.{t}" for t in range(TT)], [f"out.{n}.{i}" for i in range(2)], m.yT)
    turn_rows(pe, B, [f"n2.{i}" for i in range(4)], ps, m.xn, ident, F, "n2")
    wait_columns(pe, B, [f"n2.{i}" for i in range(4)])
    route_tensor(pe, m, ps, B, F)


def causal_scores(pe, B, ps, job, keys, queries):
    B.claim(pe, job)
    bank = ps[B.bank(job)]
    pe.matmul(bank[:, 0:T], keys[:, 0:P], queries, start=True, stop=True)
    pe.matmul(bank[:, T:T + P], keys[:, P:T], queries[:, P:T], start=True, stop=True).then_inc(B.full(job), 1)


def spread_rows(pe, B, ps, job, rows, ident, n, first):
    B.claim(pe, job)
    for k in range(2):
        mm = pe.matmul(ps[B.bank(job)][:, k * T:(k + 1) * T], ident[0:n, first + k:first + k + 1].to_broadcast([n, P]),
                       rows[0:n, :], start=True, stop=True)
    mm.then_inc(B.full(job), 1)



def route_tensor(pe, m, ps, B, F):
    wroute = m.p["wroute"].rearrange("p (k n) -> p k n", k=KT)
    B.claim(pe, "route")
    for t in range(TT):
        for k in range(KT):
            mm = pe.matmul(ps[B.bank("route")][:, t * 36:(t + 1) * 36], m.hT[:, k, t * P:(t + 1) * P], wroute[:, k, :],
                           start=k == 0, stop=k == KT - 1)
    mm.then_inc(B.full("route"), 1)
    pe.wait_ge(*F.at("chosen"))
    B.claim(pe, "rank")
    bank, chosen, before, ones = ps[B.bank("rank")], m.r.chosen, m.c["before"], m.c["ones"][:, 0:P]
    pe.matmul(bank[:, 0:32], before, chosen[:, 0, :], start=True, stop=True)
    pe.matmul(bank[:, 32:64], ones, chosen[:, 0, :], start=True, stop=False)
    pe.matmul(bank[:, 32:64], before, chosen[:, 1, :], start=False, stop=True)
    pe.matmul(bank[:, 64:96], ones, chosen[:, 0, :], start=True, stop=False)
    pe.matmul(bank[:, 64:96], ones, chosen[:, 1, :], start=False, stop=True).then_inc(B.full("rank"), 1)


def first_of(dve, step, values, best, prior, out):
    n = values.shape[2]
    step(dve.tensor_tensor(out, values, bc(best, [P, TT, n]), ALU.is_equal))
    step(dve.tensor_tensor(out, out, prior.unsqueeze(1).to_broadcast([P, TT, n]), ALU.mult))
    step(dve.tensor_reduce(best, out, AX.X, ALU.max))
    step(dve.tensor_tensor(out, out, bc(best, [P, TT, n]), ALU.is_equal))


def route_vector(dve, step, m, ps, B, F):
    r = m.r
    dve.wait_ge(*B.filled("route"))
    bank = ps[B.bank("route")][:, 0:72].rearrange("p (t n) -> p t n", t=TT)
    dve.tensor_tensor(r.lg, bank, m.p["broute"].unsqueeze(1).to_broadcast([P, TT, 36]),
                      ALU.add).then_inc(B.free("route"), 1)
    dve.wait_ge(*B.drained("route"))
    step(dve.tensor_reduce(r.best, r.lg[:, :, 0:4], AX.X, ALU.max))
    dve.tensor_scalar(r.nmg, r.best, -1.0, None, ALU.mult).then_inc(F["lg_max"], 1)
    first_of(dve, step, r.lg[:, :, 0:4], r.best, m.c["prior4"], r.group)
    for t in range(TT):
        step(dve.tensor_tensor(r.by_group[:, t], r.lg[:, t, 4:36].rearrange("p (g j) -> p g j", g=GROUPS),
                               bc(r.group[:, t, :], [P, GROUPS, PER_GROUP]), ALU.mult))
        step(dve.tensor_reduce(r.le[:, t, :], r.by_group[:, t].rearrange("p g j -> p j g"), AX.X, ALU.add))
    step(dve.tensor_reduce(r.best, r.le, AX.X, ALU.max))
    step(dve.tensor_scalar(r.e2, r.best, -1.0, None, ALU.mult))
    first_of(dve, step, r.le, r.best, m.c["prior8"], r.hot1)
    step(dve.scalar_tensor_tensor(out=r.le, in0=r.hot1, scalar=NEG, in1=r.le, op0=ALU.mult, op1=ALU.add))
    step(dve.tensor_reduce(r.best, r.le, AX.X, ALU.max))
    dve.tensor_tensor(r.e2, r.e2, r.best, ALU.add).then_inc(F["le_diff"], 1)
    first_of(dve, step, r.le, r.best, m.c["prior8"], r.hot2)
    step(dve.tensor_tensor(r.le, r.hot1, r.hot2, ALU.add))
    for t in range(TT):
        ins = dve.tensor_tensor(r.chosen[:, t, :].rearrange("p (g j) -> p g j", g=GROUPS),
                                bc(r.group[:, t, :], [P, GROUPS, PER_GROUP]),
                                r.le[:, t, :].unsqueeze(1).to_broadcast([P, GROUPS, PER_GROUP]), ALU.mult)
    ins.then_inc(F["chosen"], 1)
    dve.wait_ge(*F.at("lg_exp", 2))
    dve.wait_ge(*F.at("le_exp"))
    step(dve.tensor_scalar(r.w1, r.e2, 1.0, None, ALU.add))
    step(dve.tensor_tensor(r.sg, r.sg, r.w1, ALU.mult))
    step(dve.reciprocal(r.w1, r.sg))
    step(dve.tensor_tensor(r.w2, r.e2, r.w1, ALU.mult))
    step(dve.tensor_tensor(r.hot1, r.hot1, bc(r.w1, [P, TT, PER_GROUP]), ALU.mult))
    step(dve.tensor_tensor(r.hot2, r.hot2, bc(r.w2, [P, TT, PER_GROUP]), ALU.mult))
    step(dve.tensor_tensor(r.hot1, r.hot1, r.hot2, ALU.add))
    step(dve.memset(r.gates[:, :, PASSES * EXPERTS:], 0.0))
    step(dve.memset(r.ranks[:, :, PASSES * EXPERTS:], -1.0))
    for t in range(TT):
        for q in range(PASSES):
            dve.tensor_tensor(r.gates[:, t, q * EXPERTS:(q + 1) * EXPERTS].rearrange("p (g j) -> p g j", g=GROUPS),
                              bc(r.group[:, t, :], [P, GROUPS, PER_GROUP]),
                              r.hot1[:, t, :].unsqueeze(1).to_broadcast([P, GROUPS, PER_GROUP]), ALU.mult)
    dve.wait_ge(*B.filled("rank"))
    bank = ps[B.bank("rank")]
    step(dve.scalar_tensor_tensor(out=r.rank, in0=bank[:, 0:64].rearrange("p (t e) -> p t e", t=TT), scalar=1.0,
                                  in1=r.chosen, op0=ALU.add, op1=ALU.mult))
    dve.tensor_reduce(r.most, bank[:, 64:96], AX.X, ALU.max).then_inc(B.free("rank"), 1)
    dve.wait_ge(*B.drained("rank"))
    for q in range(PASSES):
        step(dve.tensor_scalar(r.ranks[:, :, q * EXPERTS:(q + 1) * EXPERTS], r.rank, -1.0 - q * CAP, None, ALU.add))
    step(dve.tensor_scalar(r.passes[:, 0:1], r.most, float(CAP), 1.0, ALU.is_gt, ALU.add))
    for q in range(2, PASSES):
        step(dve.tensor_scalar(r.passes[:, 1:2], r.most, float(q * CAP), None, ALU.is_gt))
        step(dve.tensor_tensor(r.passes[:, 0:1], r.passes[:, 0:1], r.passes[:, 1:2], ALU.add))
    step(dve.tensor_copy(r.turns_i[:, 0:1], r.passes[:, 0:1]))
    step(dve.tensor_scalar(r.passes[:, 1:2], r.passes[:, 0:1], float(PAIRS), None, ALU.mult))
    dve.tensor_copy(r.turns_i[:, 1:2], r.passes[:, 1:2]).then_inc(F["passes"], 1)


GATE, UP, GATHER, TURN, SUM, DOWN = 0, 1, 2, 4, 5, 6
LOADS = 3 * 2 * 2
GROUPS_USED = LOADS // 2


def moe_select(dve, m, out, turn):
    cols = m.r.ranks[:, :, bass.ds(turn * 2, 2)]
    o = out.rearrange("p t (e s) -> p t e s", e=2)
    for t in range(TT):
        ins = dve.tensor_tensor(o[:, t], m.c["slot"].rearrange("p (e s) -> p e s", e=2),
                                bc(cols[:, t, :], [P, 2, CAP]), ALU.is_equal)
    return ins


AHEAD = {"vector": ("hidden", "added"), "scalar": ("rows",), "tensor": ("turned", "hid_turned", "summed")}


def since(n):
    return n + 1


def raise_ahead(engine, M, name):
    for n in AHEAD[name]:
        engine.sem_inc(M[n], 1)


def moe_vector(dve, m, ps, M):
    r = m.r
    raise_ahead(dve, M, "vector")
    turns = dve.value_load(r.turns_i[0:1, 1:2], min_val=PAIRS, max_val=PAIRS * PASSES)
    moe_select(dve, m, m.sel, 0).then_inc(M["sel"], 1)
    for g in range(2):
        dve.wait_ge(M["gathered"], g + 1)
        gather_columns(dve, m, ps, g).then_inc(M["columns"], 1)
    with dve.Fori(0, turns) as i:
        dve.wait_ge(M["gathered"], i * 2 + 2)
        moe_select(dve, m, m.sel, i + 1).then_inc(M["sel"], 1)
        dve.wait_ge(M["turned"], since(i))
        moe_select(dve, m, m.selg, i).then_inc(M["selg1"], 1)
        dve.wait_ge(M["selg1"], i + 1)
        for t in range(TT):
            o = m.selg[:, t].rearrange("p (e s) -> p e s", e=2)
            ins = dve.tensor_tensor(o, o, bc(r.gates[:, t, bass.ds(i * 2, 2)], [P, 2, CAP]), ALU.mult)
        ins.then_inc(M["selg"], 1)
        dve.wait_ge(M["gate_exp"], i + 1)
        dve.tensor_scalar(m.eg, m.eg, 1.0, None, ALU.add).then_inc(M["silu"], 1)
        dve.wait_ge(M["silu"], i * 3 + 1)
        dve.reciprocal(m.eg, m.eg).then_inc(M["silu"], 1)
        dve.wait_ge(M["silu"], i * 3 + 2)
        dve.tensor_tensor(m.eg, m.eg, ps[GATE][:], ALU.mult).then_inc(M["silu"], 1)
        dve.wait_ge(M["silu"], i * 3 + 3)
        dve.wait_ge(M["used"], (i + 1) * GROUPS_USED + 4)
        dve.wait_ge(M["hid_turned"], since(i))
        dve.tensor_tensor(m.hid, m.eg, ps[UP][:], ALU.mult).then_inc(M["hidden"], 1)
        for g in range(2):
            dve.wait_ge(M["gathered"], i * 2 + 3 + g)
            gather_columns(dve, m, ps, g).then_inc(M["columns"], 1)
        for q in range(4):
            t, n = q // 2, q % 2
            dve.wait_ge(M["summed"], since(i * 4 + q + 1))
            xs = m.x[:, t, n * 512:(n + 1) * 512]
            dve.tensor_tensor(xs, xs, ps[(SUM, TURN)[q % 2]][:], ALU.add).then_inc(M["added"], 1)


def gather_columns(dve, m, ps, g):
    return dve.tensor_tensor(m.hc[:, 4 * g:4 * g + 4, :], split(ps[GATHER + g][:], 4),
                             bc(m.gcols[:, 4 * g:4 * g + 4], [P, 4, P]), ALU.mult)


def moe_scalar(act, m, ps, M):
    raise_ahead(act, M, "scalar")
    turns = act.value_load(m.r.turns_i[0:1, 1:2], min_val=PAIRS, max_val=PAIRS * PASSES)
    with act.Fori(0, turns) as i:
        act.wait_ge(M["used"], (i + 1) * GROUPS_USED + 2)
        act.wait_ge(M["hidden"], since(i))
        act.activation(m.eg, ps[GATE][:], ACT.Exp, scale=-1.0).then_inc(M["gate_exp"], 1)
        act.wait_ge(M["turned"], since(i + 1))
        act.wait_ge(M["summed"], since(i * 4))
        act.activation(m.selgT, ps[TURN][:, 0:T], ACT.Copy).then_inc(M["selgT"], 1)
        act.wait_ge(M["hid_turned"], since(i + 1))
        act.activation(m.hidT, ps[TURN][:], ACT.Copy).then_inc(M["hidT"], 1)
        act.wait_ge(M["used"], (i + 1) * GROUPS_USED + 6)
        for n in range(2):
            act.activation(m.ym[:, n * 512:(n + 1) * 512], ps[DOWN + n][:], ACT.Copy).then_inc(M["rows"], 1)


def moe_gather(pe, m, ps, M):
    for g in range(2):
        for k in range(4):
            kk = 4 * g + k
            for t in range(TT):
                mm = pe.matmul(ps[GATHER + g][:, k * P:(k + 1) * P], m.xn[:, t, kk * P:(kk + 1) * P], m.sel[:, t, :],
                               start=t == 0, stop=t == TT - 1)
        mm.then_inc(M["gathered"], 1)


def moe_tensor(pe, m, ps, M, landed):
    ident = m.c["ident"]
    raise_ahead(pe, M, "tensor")
    turns = pe.value_load(m.r.turns_i[0:1, 1:2], min_val=PAIRS, max_val=PAIRS * PASSES)
    pe.wait_ge(M["sel"], 1)
    moe_gather(pe, m, ps, M)

    def unit(i, u):
        pe.wait_ge(landed[u // 2], (i + 1) * 32)
        return m.expert_slots[u]

    with pe.Fori(0, turns) as i:
        pe.wait_ge(M["columns"], i * 2 + 2)
        pe.wait_ge(M["hidden"], since(i))
        for w, bank in ((0, GATE), (1, UP)):
            for h in range(2):
                both = [unit(i, w * 4 + h * 2 + e).rearrange("p (k n) -> p k n", k=4) for e in range(2)]
                for k in range(4):
                    for e in range(2):
                        mm = pe.matmul(ps[bank][e * 64:e * 64 + 64, :], m.hc[:, h * 4 + k, e * 64:e * 64 + 64],
                                       both[e][:, k, :], start=h + k == 0, stop=h * 4 + k == 7)
                mm.then_inc(M["used"], 1)
        pe.wait_ge(M["selg"], i + 1)
        pe.wait_ge(M["added"], since(i * 4))
        for t in range(TT):
            mm = pe.transpose(ps[TURN][:, t * P:(t + 1) * P], m.selg[:, t, :], ident)
        mm.then_inc(M["turned"], 1)
        pe.wait_ge(M["sel"], i + 2)
        moe_gather(pe, m, ps, M)
        pe.wait_ge(M["hidden"], since(i + 1))
        pe.wait_ge(M["selgT"], i + 1)
        for f in range(4):
            mm = pe.transpose(ps[TURN][:, f * P:(f + 1) * P], m.hid[:, f * P:(f + 1) * P], ident)
        mm.then_inc(M["hid_turned"], 1)
        pe.wait_ge(M["hidT"], i + 1)
        pe.wait_ge(M["rows"], since(i * 2))
        for h in range(2):
            both = [unit(i, 8 + h * 2 + e).rearrange("p (f n) -> p f n", f=2) for e in range(2)]
            for f in range(2):
                ff = h * 2 + f
                for n in range(2):
                    for e in range(2):
                        mm = pe.matmul(ps[DOWN + n][e * 64:e * 64 + 64, :],
                                       m.hidT[:, ff * P + e * 64:ff * P + e * 64 + 64],
                                       both[e][:, f, n * 512:(n + 1) * 512], start=ff == 0, stop=ff == 3)
            mm.then_inc(M["used"], 1)
        pe.wait_ge(M["rows"], since(i * 2 + 2))
        for q in range(4):
            t, n = q // 2, q % 2
            if q >= 2:
                pe.wait_ge(M["added"], since(i * 4 + q - 1))
            pe.matmul(ps[(SUM, TURN)[q % 2]][:], m.selgT[:, t * P:(t + 1) * P], m.ym[:, n * 512:(n + 1) * 512],
                      start=True, stop=True).then_inc(M["summed"], 1)


def moe_loads(sp, m, M, landed, experts, passes_known):
    sp.sem_inc(M["used"], GROUPS_USED)

    def load(u, pair):
        sp.dma_start(m.expert_slots[u], experts[pair, u]).then_inc(landed[u // 2], 16)

    for u in range(LOADS):
        load(u, 0)
    sp.wait_ge(*passes_known)
    turns = sp.value_load(m.r.turns_i[0:1, 1:2], min_val=PAIRS, max_val=PAIRS * PASSES)
    with sp.Fori(1, turns) as i:
        pair = i % PAIRS
        for u in range(LOADS):
            sp.wait_ge(M["used"], i * GROUPS_USED + (u // 2 + 1))
            load(u, bass.ds(pair, 1))
    return turns



BEFORE = {"f1": "f2", "mx": "f1", "f2": "mx"}



def passes_of(stationary, moving):
    return ((stationary[0], moving[0]), (stationary[0], moving[1]), (stationary[1], moving[0]))


def sofar(f, n):
    return n if f == "f2" else 0


def unit_hi(act, m, U, F, names, j, his):
    if j >= HI_BUFFERS:
        act.wait_ge(*U.given_back(names[j - HI_BUFFERS]))
    act.wait_ge(*U.landed(names[j]))
    act.activation(his[j % HI_BUFFERS], m.ring[U.slot(names[j])], ACT.Copy).then_inc(F["unit_hi"], 1)


def unit_lo(dve, m, U, F, f, names, j, his):
    slot = U.slot(names[j])
    dve.wait_ge(*F.at("unit_hi", SPLIT_BEFORE[f] + j + 1))
    dve.tensor_tensor(m.ring_r[slot], m.ring[slot], his[j % HI_BUFFERS].bitcast(F32), ALU.subtract).then_inc(
        F["unit_lo"], 1)


def unit_parts(pe, m, U, F, f, names, j, his, k):
    pe.wait_ge(*F.at("unit_lo", SPLIT_BEFORE[f] + j + 1))
    return [v.rearrange("p (k n) -> p k n", k=k) for v in (his[j % HI_BUFFERS], m.ring_r[U.slot(names[j])])]


def split_columns(pe, B, ps, job, parts, moving, cols=None):
    hi, lo = parts
    for c in range(2):
        for k in range(KT):
            if cols and c == 0 and k % 2 == 0:
                pe.wait_ge(*cols[k // 2])
            for n, (w, x) in enumerate(passes_of([w[:, k, c * P:(c + 1) * P] for w in (hi, lo)],
                                                 [x[:, k, :] for x in moving])):
                mm = pe.matmul(ps[B.bank(job)][:, c * T:(c + 1) * T], w, x, start=k + n == 0,
                               stop=k == KT - 1 and n == 2)
    mm.then_inc(B.full(job), 1)


def ffn_unit_names(f):
    return [n for n, _ in ffn_units(f)]


def ffn_tensor(pe, m, ps, B, U, F, f):
    names = [f"{f}.n.{i}" for i in range(4)]
    units = ffn_unit_names(f)
    turn_rows(pe, B, names, ps, m.xn, m.c["ident"], F, f)

    for i in range(FT):
        job = f"{f}.in.{i}"
        B.claim(pe, job)
        parts = unit_parts(pe, m, U, F, f, units, i, m.whi_r, KT)
        split_columns(pe, B, ps, job, parts, (m.hT_r, m.hTlo_r), [B.drained(n) for n in names] if i == 0 else None)
    for i in range(FT // 2):
        hi, lo = unit_parts(pe, m, U, F, f, units, FT + i, m.whi_r, 2)
        for k in range(2):
            kk = 2 * i + k
            pe.wait_ge(*F.at("ffn_hid", sofar(f, FT) + kk + 1))
            for n in range(2):
                for t in range(TT):
                    job = f"{f}.out.{n}.{t}"
                    if kk == 0:
                        B.claim(pe, job)
                    turns = passes_of([x[:, kk, t * P:(t + 1) * P] for x in (m.hid_r, m.hidlo_r)],
                                      [w[:, k, n * 512:(n + 1) * 512] for w in (hi, lo)])
                    for q, (x, w) in enumerate(turns):
                        mm = pe.matmul(ps[B.bank(job)][:], x, w, start=kk + q == 0, stop=kk == FT - 1 and q == 2)
                    if kk == FT - 1:
                        mm.then_inc(B.full(job), 1)
        if i < FT // 2 - 1:
            mm.then_inc(U.parts_sem, 1)


def ffn_scalar(act, step, m, ps, B, U, F, f, gain):
    units = ffn_unit_names(f)
    unit_hi(act, m, U, F, units, 0, m.whi_r)
    row_squares(act, m, F, f)
    for j in range(1, AHEAD_UNITS):
        unit_hi(act, m, U, F, units, j, m.whi_r)
    for i in range(4):
        job = f"{f}.n.{i}"
        act.wait_ge(*B.filled(job))
        for k in range(2):
            ins = act.activation(m.hT_r[:, 2 * i + k, :], ps[B.bank(job)][:, k * T:(k + 1) * T], ACT.Copy,
                                 scale=gain[:, 2 * i + k:2 * i + k + 1])
        ins.then_inc(F[f"{f}.cols"], 1)
    for i in range(FT):
        if i + AHEAD_UNITS < len(units):
            unit_hi(act, m, U, F, units, i + AHEAD_UNITS, m.whi_r)
        job, e = f"{f}.in.{i}", m.fe[i % 2]
        act.wait_ge(*B.filled(job))
        if i >= 2:
            act.wait_ge(*F.at("ffn_hid", sofar(f, FT) + i - 1))
        step(act.activation(e, ps[B.bank(job)][:, 0:T], ACT.Exp, scale=-1.0))
        step(act.activation(e, e, ACT.Ln, bias=1.0))
        act.activation(e, e, ACT.Exp, scale=-1.0).then_inc(F["ffn_exp"], 1)
    for j in range(FT + AHEAD_UNITS, len(units)):
        unit_hi(act, m, U, F, units, j, m.whi_r)
    post_scalar(act, m, ps, B, F, f)


def row_squares(act, m, F, f):
    for t in range(TT):
        act.wait_ge(*F.at(BEFORE[f] + ".x", t + 1 if f != "f1" else t - 1))
        act.activation(m.hrows[:, t, :], m.x[:, t, :], ACT.Square, scale=D ** -0.5,
                       accum_out=m.ss[:, t:t + 1]).then_inc(F[f"{f}.ss"], 1)


def post_scalar(act, m, ps, B, F, f):
    for n in range(2):
        for t in range(TT):
            job = f"{f}.out.{n}.{t}"
            act.wait_ge(*B.filled(job))
            act.activation(m.hrows[:, t, n * 512:(n + 1) * 512], ps[B.bank(job)][:], ACT.Square, scale=D ** -0.5,
                           accum_out=m.halves[:, n, t:t + 1]).then_inc(F[f"{f}.pss"], 1)
    if f == "f2":
        act.sem_inc(F["ring_free"], 1)


def ffn_vector(dve, step, m, ps, B, U, F, f, gain, post, post_landed=None):
    units = ffn_unit_names(f)
    unit_lo(dve, m, U, F, f, units, 0, m.whi_r)
    scale_rows(dve, m, F, f)
    for i in range(4):
        job = f"{f}.n.{i}"
        dve.wait_ge(*F.at(f"{f}.cols", i + 1))
        for k in range(2):
            kk = 2 * i + k
            ins = dve.scalar_tensor_tensor(out=m.hTlo_r[:, kk, :], in0=ps[B.bank(job)][:, k * T:(k + 1) * T],
                                           scalar=gain[:, kk:kk + 1], in1=m.hT_r[:, kk, :].bitcast(F32), op0=ALU.mult,
                                           op1=ALU.subtract)
        ins.then_inc(B.free(job), 1)
    unit_lo(dve, m, U, F, f, units, 1, m.whi_r)
    for i in range(FT):
        unit_lo(dve, m, U, F, f, units, i + AHEAD_UNITS, m.whi_r)
        job = f"{f}.in.{i}"
        bank, e = ps[B.bank(job)], m.fe[i % 2]
        dve.wait_ge(*F.at("ffn_exp", sofar(f, FT) + i + 1))
        step(dve.tensor_tensor(e, e, bank[:, 0:T], ALU.mult))
        dve.tensor_tensor(e, e, bank[:, T:2 * T], ALU.mult).then_inc(B.free(job), 1)
        dve.wait_ge(*B.drained(job))
        step(dve.tensor_copy(m.hid_r[:, i, :], e))
        dve.tensor_tensor(m.hidlo_r[:, i, :], e, m.hid_r[:, i, :].bitcast(F32), ALU.subtract).then_inc(F["ffn_hid"], 1)
    for j in range(FT + AHEAD_UNITS, len(units)):
        unit_lo(dve, m, U, F, f, units, j, m.whi_r)
    if post_landed is not None:
        dve.wait_ge(*post_landed)
    post_vector(dve, m, ps, B, F, f, post, 0.5)


def scale_rows(dve, m, F, f):
    dve.wait_ge(*F.at(f"{f}.rstd"))
    for t in range(TT):
        dve.tensor_scalar(m.xn[:, t, :], m.x[:, t, :], m.ss[:, t:t + 1], None, ALU.mult).then_inc(F[f"{f}.xn"], 1)


def post_vector(dve, m, ps, B, F, f, post, weight):
    for n in range(2):
        for t in range(TT):
            job = f"{f}.out.{n}.{t}"
            c = slice(n * 512, (n + 1) * 512)
            dve.wait_ge(*F.at(f"{f}.pss", 2 * n + t + 1))
            dve.scalar_tensor_tensor(out=m.xn[:, t, c], in0=ps[B.bank(job)][:], scalar=weight, in1=post[:, c],
                                     op0=ALU.mult, op1=ALU.mult).then_inc(B.free(job), 1)
    for t in range(TT):
        for n in range(2):
            dve.wait_ge(*B.drained(f"{f}.out.{n}.{t}"))
    dve.wait_ge(*F.at(f"{f}.prstd"))
    for t in range(TT):
        dve.scalar_tensor_tensor(out=m.x[:, t, :], in0=m.xn[:, t, :], scalar=m.pr[:, t:t + 1], in1=m.x[:, t, :],
                                 op0=ALU.mult, op1=ALU.add).then_inc(F[f"{f}.x"], 1)
    dve.wait_ge(*F.at(f"{f}.x", 2))


def pre_pool(pool, step, m, F, f):
    pool.wait_ge(*F.at(f"{f}.ss", 2))
    root_of_mean(pool, step, m.ss, m.c["eps"][:, 0:2], m.half[:, 0:2], F[f"{f}.rstd"])


def post_pool(pool, step, m, F, f):
    pool.wait_ge(*F.at(f"{f}.pss", 4))
    step(pool.tensor_tensor(m.pr, m.halves[:, 0, :], m.halves[:, 1, :], ALU.add))
    root_of_mean(pool, step, m.pr, m.c["eps"][:, 0:2], m.half[:, 0:2], F[f"{f}.prstd"])


def layer_pool(pool, m, B, F, step, load_next):
    pre_pool(pool, step, m, F, "f1")
    post_pool(pool, step, m, F, "f1")
    pre_pool(pool, step, m, F, "mx")
    pool.wait_ge(*F.at("o_var"))
    root_of_mean(pool, step, m.ov, m.c["eps"], m.half[:, 0:8], F["o_rstd"])
    post_pool(pool, step, m, F, "mx")
    pre_pool(pool, step, m, F, "f2")
    pool.wait_ge(*F.at("f2.cols", 4))
    pool.wait_ge(*B.drained("f2.n.3"))
    load_next()
    post_pool(pool, step, m, F, "f2")


CONV_PARTS = ((0, 8), (8, CONV_T))


def mix_tensor(pe, m, ps, B, U, F):
    ident, ring = m.c["ident"], m.ring
    names = [f"mx.n.{i}" for i in range(4)]
    turn_rows(pe, B, names, ps, m.xn, ident, F, "mx")
    def split_rows(jobs, f, units, j, his, held, ready):
        for u in range(2):
            hi, lo = unit_parts(pe, m, U, F, f, units, j + u, his, KT // 2)
            for t in range(TT):
                if u == 0:
                    B.claim(pe, jobs[t])
                for k in range(KT // 2):
                    kk = u * (KT // 2) + k
                    if ready and t == 0 and kk % 2 == 0:
                        pe.wait_ge(*F.at(ready, kk // 2 + 1))
                    for n, (x, w) in enumerate(passes_of([x[:, kk, t * P:(t + 1) * P] for x in held],
                                                         [w[:, k, :] for w in (hi, lo)])):
                        mm = pe.matmul(ps[B.bank(jobs[t])][:], x, w, start=kk + n == 0, stop=kk == KT - 1 and n == 2)
                if u == 1:
                    mm.then_inc(B.full(jobs[t]), 1)
                elif t == TT - 1:
                    mm.then_inc(U.parts_sem, 1)

    for a, name in enumerate(("rq", "rk", "rv.0", "rv.1", "rg.0", "rg.1")):
        split_rows([f"{name}.{t}" for t in range(TT)], "mx", MIX_SPLIT, 2 * a, m.mhi_r, (m.mh_r, m.mhlo_r),
                   "mx.cols" if a == 0 else None)
    for i in range(6):
        job = f"xbc.{i}"
        B.claim(pe, job)
        split_columns(pe, B, ps, job, unit_parts(pe, m, U, F, "mx", MIX_SPLIT, 12 + i, m.mhi_r, KT), (m.mh_r, m.mhlo_r))
    pe.wait_ge(*F.at("rope", 4))
    for n, name in enumerate(("rqT", "rkT")):
        for i in range(2):
            job = f"{name}.{i}"
            B.claim(pe, job)
            for k in range(2):
                h = 2 * i + k
                for t in range(TT):
                    mm = pe.transpose(ps[B.bank(job)][:, k * T + t * P:k * T + t * P + P],
                                      m.rope[:, n, t, h * P:(h + 1) * P], ident)
            mm.then_inc(B.full(job), 1)
    B.claim(pe, "dt")
    wdt = m.lp["wdt"].rearrange("p (k n) -> p k n", k=KT)
    for k in range(KT):
        mm = pe.matmul(ps[B.bank("dt")][0:16, 0:T], wdt[:, k, :], m.hT[:, k, :], start=k == 0, stop=k == KT - 1)
    mm.then_inc(B.full("dt"), 1)
    for i in range(4):
        project_columns(pe, B, U, ps, ring, f"z.{i}", f"z.{i}", m.hT)
    for h in range(RET_H):
        if h % 2 == 0:
            pe.wait_ge(*B.drained(f"rqT.{h // 2}"))
            pe.wait_ge(*B.drained(f"rkT.{h // 2}"))
        causal_scores(pe, B, ps, f"rs.{h}", m.rT[:, 1, h, :], m.rT[:, 0, h, :])
    pe.wait_ge(*F.at("dt_rows", 2))
    B.claim(pe, "dtcol")
    for half, row in enumerate((m.drow[0], m.drow[1])):
        for t in range(TT):
            o = (half * 2 + t) * 16
            mm = pe.matmul(ps[B.bank("dtcol")][:, o:o + 16], row[0:16, t * P:(t + 1) * P], ident[0:16, 0:16],
                           start=True, stop=True)
    mm.then_inc(B.full("dtcol"), 1)
    pe.wait_ge(*F.at("xc", len(CONV_PARTS)))
    for g in range(SSD_G):
        causal_scores(pe, B, ps, f"cb.{g}", m.xc[:, 8 + g, :], m.xc[:, 10 + g, :])
    for i in range(4):
        job = f"xst.{i}"
        B.claim(pe, job)
        for k in range(4):
            mm = pe.transpose(ps[B.bank(job)][:, k * P:(k + 1) * P],
                              m.xc[:, 4 * (i % 2) + k, (i // 2) * P:(i // 2 + 1) * P], ident)
        mm.then_inc(B.full(job), 1)
    for h in range(RET_H):
        pe.wait_ge(*B.drained(f"rs.{h}"))
    for n in range(2):
        for t in range(TT):
            pe.wait_ge(*B.drained(f"rv.{n}.{t}"))
    for t in range(TT):
        for i in range(2):
            job = f"ro.{t}.{i}"
            B.claim(pe, job)
            for k in range(2):
                h = 2 * i + k
                for s in range(t + 1):
                    mm = pe.matmul(ps[B.bank(job)][:, k * T:(k + 1) * T], m.rw[:, h, (t + s) * P:(t + s + 1) * P],
                                   m.rv[:, s, h * T:(h + 1) * T], start=s == 0, stop=s == t)
            mm.then_inc(B.full(job), 1)

    def spread(i):
        spread_rows(pe, B, ps, f"sbc.{i}", m.drow[1], ident, 16, 2 * i)

    def ssd_out(i):
        job = f"sy.{i}"
        B.claim(pe, job)
        pe.wait_ge(*F.at("sw", 2 * i + 2))
        for c in range(2):
            for s in range(2):
                for e in range(2):
                    h = 4 * i + 2 * c + e
                    lo, n = (0, T) if s == 0 else (P, P)
                    mm = pe.matmul(ps[B.bank(job)][e * 64:e * 64 + 64, c * T + lo:c * T + lo + n],
                                   m.xdt[:, s, h * 64:(h + 1) * 64],
                                   m.sw[:, h % 8, s * T:s * T + n], start=s == 0, stop=s == 1)
        mm.then_inc(B.full(job), 1)

    for i in range(4):
        spread(i)
    for i in range(3):
        project_columns(pe, B, U, ps, ring, f"aq.{i}", f"aq.{i}", m.hT)
    for i in range(4):
        pe.wait_ge(*B.drained(f"xst.{i}"))
    ssd_out(0)
    ssd_out(1)
    for i in range(4, 8):
        spread(i)
    B.claim(pe, "akv")
    pe.wait_ge(*U.landed("akv"))
    w = ring[U.slot("akv")].rearrange("p (k n) -> p k n", k=KT)
    for k in range(KT):
        pe.matmul(ps[B.bank("akv")][:, 0:T], w[:, k, 0:P], m.hT[:, k, :], start=k == 0, stop=k == KT - 1)
    for t in range(TT):
        for k in range(KT):
            mm = pe.matmul(ps[B.bank("akv")][:, T + t * P:T + (t + 1) * P], m.hT[:, k, t * P:(t + 1) * P], w[:, k, P:T],
                           start=k == 0, stop=k == KT - 1)
    mm.then_inc(B.full("akv"), 1)
    project_columns(pe, B, U, ps, ring, "aq.3", "aq.3", m.hT)
    pe.wait_ge(*F.at("ret_y"))
    for i in range(4):
        job = f"rT.{i}"
        B.claim(pe, job)
        for k in range(2):
            for t in range(TT):
                mm = pe.transpose(ps[B.bank(job)][:, k * T + t * P:k * T + t * P + P],
                                  m.ro[:, t, (2 * i + k) * P:(2 * i + k + 1) * P], ident)
        mm.then_inc(B.full(job), 1)
    ssd_out(2)
    ssd_out(3)
    pe.wait_ge(*F.at("ssd_sq"))
    B.claim(pe, "ssum")
    for k in range(KT):
        mm = pe.matmul(ps[B.bank("ssum")][:, 0:T], m.c["ones"][:, 0:P], m.ysum[:, k, :], start=k == 0, stop=k == KT - 1)
    mm.then_inc(B.full("ssum"), 1)
    pe.wait_ge(*B.drained("akv"))
    for i in range(4):
        pe.wait_ge(*B.drained(f"aq.{i}"))
    for kv in range(2):
        for g in range(2):
            job = f"as.0.{kv}.{g}"
            B.claim(pe, job)
            for k in range(4):
                mm = pe.matmul(ps[B.bank(job)][:, k * P:(k + 1) * P], m.aq[kv * 64:kv * 64 + 64, 4 * g + k, 0:P],
                               m.akv[kv * 64:kv * 64 + 64, 0:P], start=True, stop=True)
            mm.then_inc(B.full(job), 1)
    for kv in range(2):
        for g in range(4):
            job = f"as.1.{kv}.{g}"
            B.claim(pe, job)
            for k in range(2):
                mm = pe.matmul(ps[B.bank(job)][:, k * T:(k + 1) * T], m.aq[kv * 64:kv * 64 + 64, 2 * g + k, P:T],
                               m.akv[kv * 64:kv * 64 + 64, 0:T], start=True, stop=True)
            mm.then_inc(B.full(job), 1)

    def branch(b):
        if b == 0:
            for i in range(4):
                project_columns(pe, B, U, ps, ring, f"g.0.{i}", f"g.0.{i}", m.hT)
            pe.wait_ge(*F.at("ssd_y", 8))
            for i in range(4):
                project_columns(pe, B, U, ps, ring, f"b.0.{i}", f"b.0.{i}", m.zT)
            return
        for n, (name, moving) in enumerate((("g", (m.mh_r, m.ghlo_r)), ("b", (m.yhi_r[b - 1], m.ylo_r[b - 1])))):
            pe.wait_ge(*F.at("end_lo", (1, b + 1)[n]))
            for i in range(4):
                job = f"{name}.{b}.{i}"
                B.claim(pe, job)
                parts = unit_parts(pe, m, U, F, "end", END_SPLIT, (b - 1) * 8 + n * 4 + i, m.ehi_r, KT)
                split_columns(pe, B, ps, job, parts, moving)

    def attend(t):
        pe.wait_ge(*F.at("ap", t + 1))
        for kv in range(2):
            for j in range(2):
                for s in range(t + 1):
                    job = f"ap.0.{kv}.{j}" if t == 0 else f"ap.1.{kv}.{j}.{s}"
                    B.claim(pe, job)
                    for k in range(4):
                        mm = pe.transpose(ps[B.bank(job)][:, k * P:(k + 1) * P],
                                          m.al[t][:, kv * 8 + 4 * j + k, s * P:(s + 1) * P], ident)
                    mm.then_inc(B.full(job), 1)
        for j in range(2):
            job = f"ao.{t}.{j}"
            B.claim(pe, job)
            for s in range(t + 1):
                for kv in range(2):
                    pe.wait_ge(*B.drained(f"ap.0.{kv}.{j}" if t == 0 else f"ap.1.{kv}.{j}.{s}"))
                    mm = pe.matmul(ps[B.bank(job)][kv * 64:kv * 64 + 64, :],
                                   m.akv[:, T + s * P + kv * 64:T + s * P + kv * 64 + 64],
                                   m.pT[:, ((kv * 2 + j) * (t + 1) + s) * 512:((kv * 2 + j) * (t + 1) + s + 1) * 512],
                                   start=s == 0, stop=s == t)
            mm.then_inc(B.full(job), 1)

    branch(0)
    attend(0)
    attend(1)
    branch(1)
    branch(2)
    for n in range(2):
        split_rows([f"mx.out.{n}.{t}" for t in range(TT)], "end", END_SPLIT, 16 + 2 * n, m.ehi_r,
                   (m.yhi_r[0], m.sumlo_r), "sum_lo" if n == 0 else None)


def mix_scalar(act, step, m, ps, B, U, F):
    lp = m.lp
    def unit(j):
        if j < len(MIX_SPLIT):
            unit_hi(act, m, U, F, MIX_SPLIT, j, m.mhi_r)

    unit(0)
    row_squares(act, m, F, "mx")
    for j in range(1, AHEAD_UNITS):
        unit(j)
    for i in range(4):
        job = f"mx.n.{i}"
        act.wait_ge(*B.filled(job))
        if i == 2:
            act.wait_ge(*B.filled("mx.n.3"))
        for k in range(2):
            ins = act.activation(m.mh_r[:, 2 * i + k, :], ps[B.bank(job)][:, k * T:(k + 1) * T], ACT.Copy,
                                 scale=lp["gmix"][:, 2 * i + k:2 * i + k + 1])
        ins.then_inc(F["mx.hi"], 1)
    for j in range(2, 6):
        unit(j)
    for n in range(2):
        for t in range(TT):
            job = f"rv.{n}.{t}"
            if t == 0:
                unit(6 + 2 * n)
                unit(7 + 2 * n)
            act.wait_ge(*B.filled(job))
            act.activation(m.rv[:, t, n * 512:(n + 1) * 512], ps[B.bank(job)][:], ACT.Copy).then_inc(B.free(job), 1)
    for n in range(2):
        for t in range(TT):
            job = f"rg.{n}.{t}"
            if t == 0:
                unit(10 + 2 * n)
                unit(11 + 2 * n)
            act.wait_ge(*B.filled(job))
            ins = act.activation(m.rg[:, t, n * 512:(n + 1) * 512], ps[B.bank(job)][:], ACT.Exp, scale=-1.0)
    step(ins)
    for i in range(6):
        job = f"xbc.{i}"
        unit(14 + i)
        act.wait_ge(*B.filled(job))
        act.activation(m.xpad[:, 2 * i:2 * i + 2, 3:], split(ps[B.bank(job)][:], 2), ACT.Copy).then_inc(B.free(job), 1)
        if i == 0:
            step(act.activation(m.rg, m.rg, ACT.Ln, bias=1.0))
        elif i == 1:
            act.activation(m.rg, m.rg, ACT.Exp, scale=-1.0).then_inc(F["rg_sig"], 1)
    for name, n in (("rqT", 0), ("rkT", 1)):
        for i in range(2):
            job = f"{name}.{i}"
            act.wait_ge(*B.filled(job))
            act.activation(m.rT[:, n, 2 * i:2 * i + 2, :], split(ps[B.bank(job)][:], 2),
                           ACT.Copy).then_inc(B.free(job), 1)
    for i, (lo, hi) in enumerate(CONV_PARTS):
        act.wait_ge(*F.at("conv", hi))
        if i:
            act.wait_ge(*F.at("xc", i))
        e = m.ce[:, 0:hi - lo, :]
        step(act.activation(e, m.xc[:, lo:hi, :], ACT.Exp, scale=-1.0))
        sigmoid_tail(act, step, e, F["conv_sig"])
    act.activation(m.acol[0:16, 0:1], lp["alog"][0:16, :], ACT.Exp).then_inc(F["a"], 1)
    act.wait_ge(*F.at("abs_dt"))
    step(act.activation(m.drow[2][0:16, :], m.drow[2][0:16, :], ACT.Exp, scale=-1.0))
    act.activation(m.drow[2][0:16, :], m.drow[2][0:16, :], ACT.Ln, bias=1.0).then_inc(F["dt_ln"], 1)
    for i in range(4):
        job = f"z.{i}"
        act.wait_ge(*B.filled(job))
        ins = act.activation(m.zT[:, 2 * i:2 * i + 2, :], split(ps[B.bank(job)][:], 2), ACT.Exp, scale=-1.0)
        if i % 2:
            step(ins)
            sigmoid_tail(act, step, m.zT[:, 2 * i - 2:2 * i + 2, :], F["z_sig"])
    for g in range(SSD_G):
        job = f"cb.{g}"
        act.wait_ge(*B.filled(job))
        act.activation(m.cb[:, g, :], ps[B.bank(job)][:, 0:3 * P], ACT.Copy).then_inc(B.free(job), 1)
    for t in range(TT):
        for i in range(2):
            job = f"ro.{t}.{i}"
            act.wait_ge(*B.filled(job))
            act.activation(m.ro[:, t, i * 512:(i + 1) * 512], ps[B.bank(job)][:], ACT.Copy).then_inc(B.free(job), 1)
    act.wait_ge(*B.drained("dtcol"))

    def decay(i):
        act.wait_ge(*B.drained(f"sbc.{i}"))
        for k in range(2):
            h = 2 * i + k
            for s, lo, hi in ((0, 0, T), (1, T, T + P)):
                e = m.sw[:, h % 8, lo:hi]
                act.activation(e, e, ACT.Exp, bias=m.dcol[:, 32 + s * 16 + h:33 + s * 16 + h]).then_inc(F["decay"], 1)

    for i in range(4):
        decay(i)

    def queries(i):
        job = f"aq.{i}"
        act.wait_ge(*B.filled(job))
        act.activation(m.aq[:, 2 * i:2 * i + 2, :], split(ps[B.bank(job)][:], 2), ACT.Copy).then_inc(B.free(job), 1)

    for i in range(3):
        queries(i)
    act.wait_ge(*F.at("o_centred"))
    act.activation(m.osq, m.ro, ACT.Square, scale=T ** -0.5).then_inc(F["o_sq"], 1)
    for i in range(4, 8):
        decay(i)
    act.wait_ge(*B.filled("akv"))
    act.activation(m.akv, ps[B.bank("akv")][:], ACT.Copy).then_inc(B.free("akv"), 1)
    queries(3)
    act.wait_ge(*F.at("ssd_gated", 4))
    act.activation(m.ysum, m.zT, ACT.Square).then_inc(F["ssd_sq"], 1)
    act.wait_ge(*B.drained("ssum"))
    step(act.activation(m.srs, m.srs, ACT.Ln))
    act.activation(m.srs, m.srs, ACT.Exp, scale=-0.5).then_inc(F["ssd_rs"], 1)
    for t in range(TT):
        act.wait_ge(*F.at("a_max", t + 1))
        for h in range(ATT_H):
            s = m.al[t][:, h, :]
            act.activation(s, s, ACT.Exp, bias=m.amax[:, t * 16 + h:t * 16 + h + 1],
                           accum_out=m.asum[:, t * 16 + h:t * 16 + h + 1]).then_inc(F["a_exp"], 1)
        act.wait_ge(*F.at("a_sink", t + 1))
        c = slice(t * 16, t * 16 + 16)
        act.activation(m.asink[:, c], m.asink[:, c], ACT.Exp).then_inc(F["a_sink_exp"], 1)

    def gate(b, i):
        job = f"g.{b}.{i}"
        act.wait_ge(*B.filled(job))
        if b == 1:
            act.wait_ge(*B.drained(f"b.0.{i}"))
        elif b == 2:
            act.wait_ge(*F.at("ysum", i + 1))
        for k in range(2):
            n = b * KT + 2 * i + k
            ins = act.activation(m.sg[:, 2 * i + k, :], ps[B.bank(job)][:, k * T:(k + 1) * T], ACT.Exp,
                                 bias=m.nbg[:, n:n + 1], scale=-1.0)
        ins.then_inc(B.free(job), 1)

    def end_unit(j):
        if j < len(END_SPLIT):
            unit_hi(act, m, U, F, END_SPLIT, j, m.ehi_r)

    for i in range(4):
        gate(0, i)
    for i in range(4):
        act.wait_ge(*B.drained(f"g.0.{i}"))
    sigmoid_tail(act, step, m.sg, F["gate_sig"])
    for t in range(TT):
        for kv in range(2):
            for j in range(2):
                for s in range(t + 1):
                    if (j + s) % 2:
                        turned_probs(act, m, ps, B, F, t, kv, j, s)
        if t == 0:
            act.wait_ge(*B.filled("ap.0.1.1"))
            act.activation(m.mh_r, m.hT, ACT.Copy).then_inc(F["end_hi"], 1)
            end_unit(0)
    act.wait_ge(*B.filled("ap.1.1.1.1"))
    end_unit(1)
    for b in (1, 2):
        u = (b - 1) * 8 + AHEAD_UNITS
        for i in range(4):
            end_unit(u + i)
            if b == 1 and i < 2:
                for k in range(2):
                    act.wait_ge(*B.filled(f"ao.1.{k}"))
                    act.wait_ge(*B.drained(f"ao.1.{k}"))
                act.activation(m.yhi_r[i], (m.yret, m.yatt)[i], ACT.Copy).then_inc(F["end_hi"], 1)
            gate(b, i)
        for i in range(4):
            act.wait_ge(*B.drained(f"g.{b}.{i}"))
        end_unit(u + 4)
        step(act.activation(m.sg, m.sg, ACT.Ln, bias=1.0))
        end_unit(u + 5)
        act.activation(m.sg, m.sg, ACT.Exp, scale=-1.0).then_inc(F["gate_sig"], 1)
        end_unit(u + 6)
        end_unit(u + 7)
    for j in range(16 + AHEAD_UNITS, len(END_SPLIT)):
        end_unit(j)
    post_scalar(act, m, ps, B, F, "mx")


def turned_probs(eng, m, ps, B, F, t, kv, j, s):
    job = f"ap.0.{kv}.{j}" if t == 0 else f"ap.1.{kv}.{j}.{s}"
    eng.wait_ge(*B.filled(job))
    if t:
        for k in range(2):
            eng.wait_ge(*B.filled(f"ao.0.{k}"))
    n = (kv * 2 + j) * (t + 1) + s
    dst = m.pT[:, n * 512:(n + 1) * 512]
    if (j + s) % 2:
        eng.activation(dst, ps[B.bank(job)][:], ACT.Copy).then_inc(B.free(job), 1)
    else:
        eng.tensor_copy(dst, ps[B.bank(job)][:]).then_inc(B.free(job), 1)


def mix_vector(dve, step, m, ps, B, U, F):
    lp = m.lp
    def unit(j):
        if j < len(MIX_SPLIT):
            unit_lo(dve, m, U, F, "mx", MIX_SPLIT, j, m.mhi_r)

    unit(0)
    scale_rows(dve, m, F, "mx")
    for i in range(4):
        job, c = f"mx.n.{i}", slice(2 * i, 2 * i + 2)
        dve.wait_ge(*F.at("mx.hi", i + 1))
        dve.tensor_tensor(m.hT[:, c, :], split(ps[B.bank(job)][:], 2), bc(lp["gmix"][:, c], [P, 2, T]),
                          ALU.mult).then_inc(B.free(job), 1)
        dve.wait_ge(*B.drained(job))
        dve.tensor_tensor(m.mhlo_r[:, c, :], m.hT[:, c, :], m.mh_r[:, c, :].bitcast(F32),
                          ALU.subtract).then_inc(F["mx.cols"], 1)
    unit(1)
    step(dve.tensor_scalar(m.nbg, lp["bgate"], -1.0, None, ALU.mult))
    for n, r in enumerate(("rq", "rk")):
        for t in range(TT):
            job = f"{r}.{t}"
            unit(2 + 2 * n + t)
            dve.wait_ge(*B.filled(job))
            x = ps[B.bank(job)][:].rearrange("p (h c d) -> p h c d", h=RET_H, c=2)
            o = m.rope[:, n, t, :].rearrange("p (h c d) -> p h c d", h=RET_H, c=2)
            cos = m.s["cos"][:, t * 64:(t + 1) * 64].unsqueeze(1).to_broadcast([P, RET_H, 64])
            sin = m.s["sin"][:, t * 64:(t + 1) * 64].unsqueeze(1).to_broadcast([P, RET_H, 64])
            t0, t1 = m.rtmp[0], m.rtmp[1]
            dve.tensor_tensor(o[:, :, 0, :], x[:, :, 0, :], cos, ALU.mult)
            dve.tensor_tensor(o[:, :, 1, :], x[:, :, 1, :], cos, ALU.mult)
            dve.tensor_tensor(t0, x[:, :, 1, :], sin, ALU.mult)
            dve.tensor_tensor(t1, x[:, :, 0, :], sin, ALU.mult).then_inc(B.free(job), 1)
            dve.wait_ge(*B.drained(job))
            dve.tensor_tensor(o[:, :, 0, :], o[:, :, 0, :], t0, ALU.subtract)
            dve.tensor_tensor(o[:, :, 1, :], o[:, :, 1, :], t1, ALU.add).then_inc(F["rope"], 1)
            dve.wait_ge(*F.at("rope", 2 * n + t + 1))
    for j in range(6, 16):
        unit(j)
    dve.wait_ge(*F.at("rg_sig"))
    for n in range(2):
        for t in range(TT):
            job = f"rg.{n}.{t}"
            e = m.rg[:, t, n * 512:(n + 1) * 512]
            dve.tensor_tensor(e, e, ps[B.bank(job)][:], ALU.mult).then_inc(B.free(job), 1)
    step(dve.memset(m.xpad[:, :, 0:3], 0.0))
    for i in range(CONV_T):
        if i % 2 == 0:
            unit(16 + i // 2)
            dve.wait_ge(*B.drained(f"xbc.{i // 2}"))
        causal_conv(dve, step, m.xc[:, i, :], m.xpad[:, i, :], lp["convw"][:, 4 * i:4 * i + 4],
                    lp["convb"][:, i:i + 1], F["conv"])
    dt, cs, r2, r3 = m.drow
    dve.wait_ge(*B.filled("dt"))
    dve.tensor_scalar(r3[0:16, :], ps[B.bank("dt")][0:16, 0:T], lp["dtbias"][0:16, :], None,
                      ALU.add).then_inc(B.free("dt"), 1)
    dve.wait_ge(*B.drained("dt"))
    magnitude(dve, r2[0:16, :], r3[0:16, :]).then_inc(F["abs_dt"], 1)
    step(dve.tensor_scalar(r3[0:16, :], r3[0:16, :], 0.0, None, ALU.max))
    for i, (lo, hi) in enumerate(CONV_PARTS):
        dve.wait_ge(*F.at("conv_sig", i + 1))
        dve.tensor_tensor(m.xc[:, lo:hi, :], m.xc[:, lo:hi, :], m.ce[:, 0:hi - lo, :], ALU.mult).then_inc(F["xc"], 1)
    dve.wait_ge(*F.at("dt_ln"))
    dve.tensor_tensor(dt[0:16, :], r3[0:16, :], r2[0:16, :], ALU.add).then_inc(F["dt_rows"], 1)
    dve.wait_ge(*F.at("dt_rows"))
    dve.wait_ge(*F.at("a"))
    step(dve.tensor_scalar(r3[0:16, :], dt[0:16, :], m.acol[0:16, 0:1], -1.0, ALU.mult, ALU.mult))
    dve.tensor_tensor_scan(cs[0:16, :], m.c["ones"][0:16, :], r3[0:16, :], 0.0, ALU.mult,
                           ALU.add).then_inc(F["dt_rows"], 1)
    for i in range(4):
        job = f"z.{i}"
        dve.wait_ge(*F.at("z_sig", i // 2 + 1))
        e = m.zT[:, 2 * i:2 * i + 2, :]
        dve.tensor_tensor(e, e, split(ps[B.bank(job)][:], 2), ALU.mult).then_inc(B.free(job), 1)
    for h in range(RET_H):
        job = f"rs.{h}"
        dve.wait_ge(*B.filled(job))
        dve.scalar_tensor_tensor(out=m.rw[:, h, :], in0=ps[B.bank(job)][:, 0:3 * P], scalar=P ** -0.5,
                                 in1=split(m.s["decay"], RET_H)[:, h, :], op0=ALU.mult,
                                 op1=ALU.mult).then_inc(B.free(job), 1)
    dve.wait_ge(*B.filled("dtcol"))
    dve.tensor_copy(m.dcol[:, 0:32], ps[B.bank("dtcol")][:, 0:32])
    dve.tensor_scalar(m.dcol[:, 32:64], ps[B.bank("dtcol")][:, 32:64], -1.0, None,
                      ALU.mult).then_inc(B.free("dtcol"), 1)
    dve.wait_ge(*B.drained("dtcol"))
    for i in range(4):
        job, t, g = f"xst.{i}", i // 2, i % 2
        dve.wait_ge(*B.filled(job))
        dve.tensor_tensor(m.xdt[:, t, g * 512:(g + 1) * 512].rearrange("p (h d) -> p h d", h=8),
                          split(ps[B.bank(job)][:], 8), bc(m.dcol[:, t * 16 + g * 8:t * 16 + g * 8 + 8], [P, 8, 64]),
                          ALU.mult).then_inc(B.free(job), 1)

    def spread(i):
        job = f"sbc.{i}"
        dve.wait_ge(*B.filled(job))
        if i >= 4:
            dve.wait_ge(*B.filled(f"sy.{(i - 4) // 2}"))
        spread_and_mask(dve, split(ps[B.bank(job)][:], 2), m.sw[:, 2 * i % 8:2 * i % 8 + 2, :], m.c["mask"],
                        B.free(job))

    def weights(i):
        dve.wait_ge(*F.at("decay", 4 * i + 4))
        w = m.sw[:, 2 * i % 8:2 * i % 8 + 2, :]
        dve.tensor_tensor(w, w, m.cb[:, i // 4, :].unsqueeze(1).to_broadcast([P, 2, 3 * P]),
                          ALU.mult).then_inc(F["sw"], 1)

    def gated(i):
        job = f"sy.{i}"
        dve.wait_ge(*B.filled(job))
        for c in range(2):
            k = 2 * i + c
            ins = dve.scalar_tensor_tensor(out=m.xc[:, k, :], in0=m.xc[:, k, :], scalar=lp["dskip"][:, k:k + 1],
                                           in1=ps[B.bank(job)][:, c * T:(c + 1) * T], op0=ALU.mult, op1=ALU.add)
        ins.then_inc(B.free(job), 1)
        dve.wait_ge(*B.drained(job))
        z = m.zT[:, 2 * i:2 * i + 2, :]
        dve.tensor_tensor(z, z, m.xc[:, 2 * i:2 * i + 2, :], ALU.mult).then_inc(F["ssd_gated"], 1)

    for i in range(4):
        spread(i)
    for g in range(SSD_G):
        dve.wait_ge(*B.drained(f"cb.{g}"))
    for i in range(4):
        weights(i)
    for t in range(TT):
        for i in range(2):
            dve.wait_ge(*B.drained(f"ro.{t}.{i}"))
    centre(dve, step, m.roh, m.ov, T, F["o_centred"])
    gated(0)
    gated(1)
    for i in range(4, 8):
        spread(i)
    dve.wait_ge(*F.at("o_sq"))
    dve.tensor_reduce(m.ov, m.osqh, AX.X, ALU.add).then_inc(F["o_var"], 1)
    for i in range(4, 8):
        weights(i)
    dve.wait_ge(*F.at("o_rstd"))
    step(dve.tensor_tensor(m.roh, m.roh, bc(m.ov, [P, 8, T]), ALU.mult))
    dve.tensor_tensor(m.ro, m.ro, m.rg, ALU.mult).then_inc(F["ret_y"], 1)
    for i in range(4):
        job = f"rT.{i}"
        dve.wait_ge(*B.filled(job))
        dve.tensor_tensor(m.yret[:, 2 * i:2 * i + 2, :], split(ps[B.bank(job)][:], 2),
                          bc(lp["gret"][:, 2 * i:2 * i + 2], [P, 2, T]), ALU.mult).then_inc(B.free(job), 1)
    gated(2)
    gated(3)
    dve.wait_ge(*F.at("ssd_gated", 4))
    dve.wait_ge(*B.filled("ssum"))
    dve.tensor_scalar(m.srs, ps[B.bank("ssum")][:, 0:T], 1.0 / D, EPS, ALU.mult, ALU.add).then_inc(B.free("ssum"), 1)
    abias = m.s["bias"].rearrange("p (h k) -> p h k", h=ATT_H)
    for t in range(TT):
        per = 4 if t == 0 else 2
        for kv in range(2):
            for g in range(8 // per):
                job = f"as.{t}.{kv}.{g}"
                h = kv * 8 + g * per
                dst = m.al[t][:, h:h + per, :]
                dve.wait_ge(*B.filled(job))
                dve.scalar_tensor_tensor(out=dst, in0=split(ps[B.bank(job)][:], per), scalar=ATT_D ** -0.5,
                                         in1=abias[:, h:h + per, (1 - t) * P:], op0=ALU.mult,
                                         op1=ALU.add).then_inc(B.free(job), 1)
                dve.wait_ge(*B.drained(job))
                step(dve.tensor_reduce(m.amax[:, t * 16 + h:t * 16 + h + per], dst, AX.X, ALU.max))
        c = slice(t * 16, t * 16 + 16)
        step(dve.tensor_tensor(m.amax[:, c], m.amax[:, c], lp["sinks"], ALU.max))
        dve.tensor_scalar(m.amax[:, c], m.amax[:, c], -1.0, None, ALU.mult).then_inc(F["a_max"], 1)
        dve.wait_ge(*F.at("a_max", t + 1))
        dve.tensor_tensor(m.asink[:, c], m.amax[:, c], lp["sinks"], ALU.add).then_inc(F["a_sink"], 1)
    dve.wait_ge(*F.at("ssd_rs"))
    for k in range(KT):
        dve.scalar_tensor_tensor(out=m.zT[:, k, :], in0=m.zT[:, k, :], scalar=lp["gssd"][:, k:k + 1], in1=m.srs,
                                 op0=ALU.mult, op1=ALU.mult).then_inc(F["ssd_y"], 1)

    def probabilities(t):
        c = slice(t * 16, t * 16 + 16)
        dve.wait_ge(*F.at("a_exp", 16 * (t + 1)))
        dve.wait_ge(*F.at("a_sink_exp", t + 1))
        step(dve.tensor_tensor(m.asum[:, c], m.asum[:, c], m.asink[:, c], ALU.add))
        step(dve.reciprocal(m.asum[:, c], m.asum[:, c]))
        dve.tensor_tensor(m.al[t], m.al[t], bc(m.asum[:, c], [P, ATT_H, (t + 1) * P]), ALU.mult).then_inc(F["ap"], 1)

    def branch(b, i):
        job = f"b.{b}.{i}"
        dve.wait_ge(*F.at("gate_sig", b + 1))
        dve.wait_ge(*B.filled(job))
        s, y = m.sg[:, 2 * i:2 * i + 2, :], m.ysum[:, 2 * i:2 * i + 2, :]
        bank = split(ps[B.bank(job)][:], 2)
        if b == 0:
            dve.tensor_tensor(y, bank, s, ALU.mult).then_inc(B.free(job), 1)
            dve.wait_ge(*B.drained(job))
        else:
            dve.tensor_tensor(s, bank, s, ALU.mult).then_inc(B.free(job), 1)
            dve.wait_ge(*B.drained(job))
            dve.tensor_tensor(y, y, s, ALU.add).then_inc(F["ysum"], 1)

    def end_unit(j):
        if j < len(END_SPLIT):
            unit_lo(dve, m, U, F, "end", END_SPLIT, j, m.ehi_r)

    def low(n, out, whole, hi):
        dve.wait_ge(*F.at("end_hi", n))
        dve.tensor_tensor(out, whole, hi.bitcast(F32), ALU.subtract).then_inc(F["end_lo"], 1)

    probabilities(0)
    probabilities(1)
    for i in range(4):
        branch(0, i)
    for t in range(TT):
        for kv in range(2):
            for j in range(2):
                for s in range(t + 1):
                    if (j + s) % 2 == 0:
                        turned_probs(dve, m, ps, B, F, t, kv, j, s)
        for j in range(2):
            job = f"ao.{t}.{j}"
            dve.wait_ge(*B.filled(job))
            dve.tensor_copy(m.yatt[:, 4 * j:4 * j + 4, t * P:(t + 1) * P],
                            split(ps[B.bank(job)][:], 4)).then_inc(B.free(job), 1)
        if t == 0:
            low(1, m.ghlo_r, m.hT, m.mh_r)
            end_unit(0)
    end_unit(1)
    for b in (1, 2):
        u = (b - 1) * 8 + AHEAD_UNITS
        for i in range(4):
            end_unit(u + i)
            if b == 1 and i < 2:
                low(2 + i, m.ylo_r[i], (m.yret, m.yatt)[i], m.yhi_r[i])
        for i in range(4):
            end_unit(u + 4 + i)
            branch(b, i)
            if b == 2:
                c = slice(2 * i, 2 * i + 2)
                dve.wait_ge(*F.at("ysum", 4 + i + 1))
                dve.tensor_copy(m.yhi_r[0][:, c, :], m.ysum[:, c, :]).then_inc(F["sum_hi"], 1)
                dve.wait_ge(*F.at("sum_hi", i + 1))
                dve.tensor_tensor(m.sumlo_r[:, c, :], m.ysum[:, c, :], m.yhi_r[0][:, c, :].bitcast(F32),
                                  ALU.subtract).then_inc(F["sum_lo"], 1)
    for j in range(16 + AHEAD_UNITS, len(END_SPLIT)):
        end_unit(j)
    post_vector(dve, m, ps, B, F, "mx", m.post[:, D:2 * D], 1.0)



LAYER_PER = {f"{f}.{n}": k for f in ("f1", "mx", "f2") for n, k in (("ss", 2), ("xn", 2), ("pss", 4), ("x", 2))}
LAYER_PER.update({
             "rope": 4, "conv": CONV_T, "conv_sig": 2, "z_sig": 2, "xc": 2, "gate_sig": 3, "dt_rows": 2, "decay": 32,
             "sw": 8, "ssd_gated": 4,
             "a_max": 2, "a_sink": 2, "a_sink_exp": 2, "a_exp": 32, "ap": 2, "ssd_y": 8, "ysum": 8})
LAYER_PER.update({"unit_hi": SPLITS, "unit_lo": SPLITS, "mx.hi": 4, "mx.cols": 4, "end_hi": 3, "end_lo": 3,
                  "sum_hi": 4, "sum_lo": 4, "ffn_hid": 2 * FT, "ffn_exp": 2 * FT,
                  "f1.cols": 4, "f2.cols": 4})
LAYER_BEFORE = {"f2.pss": 2, "f2.prstd": 1, "f2.x": 2, "ring_free": 1}
DVE_STEPS, ACT_STEPS, POOL_STEPS = 149, 103, 10


def lay_out(sb, both):
    m = type("Views", (), {})()
    m.x = sb("x", [P, TT, D], F32)[:]
    m.half = sb("minus_half", [P, T], F32)[:]
    m.ss = sb("sums", [P, TT], F32)[:]
    m.pr = sb("post_roots", [P, TT], F32)[:]
    m.halves = split(sb("half_sums", [P, 2 * TT], F32)[:], 2)
    at, n = offsets(CONST)
    m.const = sb("const", [P, n], F32)
    m.c = {k: m.const[:, o:o + w] for k, (o, w) in at.items()}

    second, n_second = offsets(SECOND)
    layer, n_layer = offsets(LAYER)
    kept = n_second + n_layer + 3 * D
    total = 33684
    m.turns = sb("turns", [P, 2], I32)[:]
    with both(F32) as sb_f32:
        m.xn = split(sb_f32("rows", TT * D), TT)
        hT, ring, area = sb_f32("columns", KT * T), sb_f32("ring", SLOTS * UNIT), sb_f32("work", total)
    with both(F32R) as sb_f32r:
        m.mh_r = split(sb_f32r("rows_parts", TT * D), KT)
        hT_r, ring_r, area_r = (sb_f32r("columns_parts", KT * T), sb_f32r("ring_parts", SLOTS * UNIT),
                                sb_f32r("work_parts", 2 * FT * T + KT * T + HI_BUFFERS * UNIT + T * 2))
    m.hT, m.hrows, m.hT_r = split(hT, KT), split(hT, TT), split(hT_r, KT)
    m.ring, m.ring_r = ([v[:, s * UNIT:(s + 1) * UNIT] for s in range(SLOTS)] for v in (ring, ring_r))

    S = Memory(area)
    S.at = total - kept
    m.second_area = S.take(n_second)
    m.s = {k: m.second_area[:, o:o + w] for k, (o, w) in second.items()}
    m.layer_area = S.take(n_layer)
    m.lp = {k: m.layer_area[:, o:o + w] for k, (o, w) in layer.items()}
    m.post, m.post2 = S.take(2 * D), S.take(D)
    m.normf = area[:, total - kept - D:total - kept]

    W = Memory(area)
    first, n_first = offsets(FIRST)
    m.first_area = W.take(n_first)
    m.p = {k: m.first_area[:, o:o + w] for k, (o, w) in first.items()}
    m.gcols = m.p["g2"]
    r = m.r = type("Routing", (), {})()

    def t2(n):
        return split(W.take(TT * n), TT)
    r.lg, r.eg, r.group, r.le, r.hot1, r.hot2 = t2(36), t2(4), t2(4), t2(8), t2(8), t2(8)
    r.by_group = W.take(TT * 32).rearrange("p (t g j) -> p t g j", t=TT, g=GROUPS)
    r.chosen, r.rank = t2(32), t2(32)
    r.gates, r.ranks = t2(PASSES * EXPERTS + 2), t2(PASSES * EXPERTS + 2)
    r.best, r.nmg, r.sg, r.e2, r.w1, r.w2, r.passes = [W.take(2) for _ in range(7)]
    r.most = W.take(1)
    r.turns_i = m.turns
    m.sel, m.selg, m.selgT = t2(2 * CAP), t2(2 * CAP), W.take(T)
    m.hc = split(W.take(KT * P), KT)
    m.eg, m.hid, m.hidT, m.ym = W.take(FE), W.take(FE), W.take(4 * P), W.take(D)
    mixers_at = W.at
    m.expert_slots = m.ring + [W.take(UNIT) for _ in range(SLOTS, LOADS)]
    assert W.at <= total - kept - D
    W.at = mixers_at
    m.cpad = split(W.take(4 * (T + 3)), 4)
    m.cv, m.ec, m.ez = [split(W.take(4 * T), 4) for _ in range(3)]
    m.cols = {n: split(W.take(4 * T), 4) for n in ("v", "qd", "kd", "vd")}
    m.vtok, m.vdtok = t2(4 * P), t2(4 * P)
    m.dp = [W.take(2 * H1 * (t + 1) * P).rearrange("p (c h k) -> p c h k", c=2, h=H1) for t in range(TT)]
    m.mq, m.mk = split(W.take(4 * T), 4), split(W.take(4 * T), 4)
    m.frow = [W.take(T) for _ in range(6)]
    m.me = split(W.take(H1 * 3 * P), H1)
    m.gcol, m.em = W.take(16), W.take(8)
    m.daT = split(W.take(3 * 4 * P), 3)
    m.hm = split(W.take(8 * P), 8)
    m.hsq = m.ec.rearrange("p a b -> p (a b)").rearrange("p (n d) -> p n d", n=8)
    yd = W.take(8 * P)
    m.yd, m.ydh = split(yd, TT), split(yd, 8)
    m.yT = split(W.take(KT * T), KT)
    m.dmax, m.dsum, m.den, m.hv, m.dv, m.lam, m.lamj = [W.take(n) for n in (16, 16, 8, 8, 8, 5, 128)]
    assert W.at <= total, W.at

    W = Memory(area)
    R = Memory(area_r)
    m.hid_r, m.hidlo_r, m.hTlo_r = split(R.take(FT * T), FT), split(R.take(FT * T), FT), split(R.take(KT * T), KT)
    m.whi_r = [R.take(UNIT) for _ in range(HI_BUFFERS)]
    W.at = R.at
    m.fe = [W.take(T) for _ in range(2)]
    W = Memory(area)
    R = Memory(area_r)
    m.mhi_r, m.mhlo_r = [R.take(UNIT) for _ in range(HI_BUFFERS)], split(R.take(KT * T), KT)
    m.ghlo_r, m.sumlo_r = (split(area_r[:, i * UNIT:(i + 1) * UNIT], KT) for i in (1, 2))
    m.ylo_r = [split(area_r[:, i * UNIT:(i + 1) * UNIT], KT) for i in (0, 3)]
    m.ehi_r = [area_r[:, i * UNIT:(i + 1) * UNIT] for i in (6, 4, 5)]
    rt, zT, xdt, ya = [W.take(KT * T) for _ in range(4)]
    al = W.take(ATT_H * 2 * P)
    m.rope = al[:, 0:2048].rearrange("p (n t c) -> p n t c", n=2, t=TT)
    m.ro = split(al[:, 0:2048], TT)
    m.roh = split(al[:, 0:2048], 8)
    m.rg = split(al[:, 2048:4096], TT)
    m.al = [m.xn.rearrange("p t d -> p (t d)").rearrange("p (h k) -> p h k", h=ATT_H), split(al, ATT_H)]
    m.osq = m.xn
    m.osqh = m.xn.rearrange("p t d -> p (t d)").rearrange("p (n d) -> p n d", n=8)
    m.rT = rt.rearrange("p (n h t) -> p n h t", n=2, h=RET_H)
    m.yret = split(rt, KT)
    rv = W.take(TT * D)
    m.rv, m.aq = split(rv, TT), split(rv, KT)
    rw = W.take(RET_H * 3 * P)
    m.rw, m.akv = split(rw, RET_H), rw[:, 0:512]
    conv = W.take(CONV_T * (T + 3) + CONV_T * T)
    m.xpad = split(conv[:, 0:CONV_T * (T + 3)], CONV_T)
    m.sw = split(conv[:, 0:8 * 3 * P], 8)
    m.xc = split(conv[:, CONV_T * (T + 3):], CONV_T)
    m.pT = conv[:, 0:4096]
    turned_at = W.at - CONV_T * (2 * T + 3)
    m.yhi_r = [split(area_r[:, turned_at + i * UNIT:turned_at + (i + 1) * UNIT], KT) for i in range(2)]
    m.sg = split(conv[:, 4096:4096 + 2048], KT)
    m.zT = split(zT, KT)
    m.xdt, m.ysum = split(xdt, TT), split(xdt, KT)
    m.cb = split(W.take(2 * 3 * P), 2)
    m.drow = [W.take(T) for _ in range(4)]
    m.yatt = split(ya, KT)
    m.ce = split(ya, KT)
    m.rtmp = [split(rw[:, i * T:(i + 1) * T], RET_H) for i in range(2)]
    m.dcol, m.acol, m.nbg, m.ov, m.srs = W.take(64), W.take(1), W.take(24), W.take(8), W.take(T)
    m.amax, m.asum, m.asink = W.take(32), W.take(32), W.take(32)
    assert W.at <= total - kept, (W.at, total - kept)
    return m


def build(nc, x, const, first, second, layer, post, post2, normf, w_first, w_experts, w_layers, out):
    with ExitStack() as ctx:
        def sb(name, shape, dt):
            return ctx.enter_context(nc.sbuf_tensor(name, shape, dt))

        def sem(name):
            return ctx.enter_context(nc.semaphore(name))

        @contextmanager
        def both(dt):
            with ExitStack() as own:
                yield lambda name, n: own.enter_context(nc.sbuf_tensor(name, [P, n], dt))[:]

        m = lay_out(sb, both)
        ps = [ctx.enter_context(nc.psum_tensor(f"bank{b}", [P, 512], F32)) for b in range(BANKS)]
        full = [sem(f"bank{b}_full") for b in range(BANKS)]
        free = [sem(f"bank{b}_read") for b in range(BANKS)]
        landed = [sem(f"slot{s}_landed") for s in range(SLOTS)]
        parts = sem("unit_parts_read")

        F = Flags(sem, "a_", {})
        B1 = Banks(full, free, FIRST_JOBS, [0] * BANKS)
        U1 = Units(landed, parts, FIRST_UNITS, [0] * SLOTS, 0, B1)
        M = {n: sem(f"moe_{n}") for n in ("sel", "selg1", "selg", "gathered", "columns", "used", "gate_exp", "silu", "hidden",
                                          "turned", "selgT", "hid_turned", "hidT", "rows", "summed", "added")}
        flags = {}
        N = Flags(sem, "n_", {})
        first_layer = Flags(lambda n: flags[n] if n in flags else flags.setdefault(n, sem(n)), "b_", {})
        steps = {n: sem(f"{n}_step") for n in ("pool", "act", "dve")}
        stored = sem("stored")
        layer_loads, table_loads, post2_loads = sem("layer_loads"), sem("table_loads"), sem("post2_loads")
        experts_landed = [sem(f"expert_slots{u}_landed") for u in range(0, LOADS, 2)]

        def layer_parts(l):
            B = Banks(full, free, LAYER_JOBS, B1.after(), l)
            U = Units(landed, parts, LAYER_UNITS, *U1.after(), B, l)
            G = Flags(lambda n: flags[n] if n in flags else flags.setdefault(n, sem(n)), "b_", LAYER_PER, l, LAYER_BEFORE)
            return B, U, G

        raised = {}

        def close(G):
            for n, k in G.raised.items():
                raised[n] = raised.get(n, 0) + k

        block = ctx.enter_context(nc.Block())

        @block.sync
        def _(sp):
            sp.dma_start(m.x, x.rearrange("b (t p) d -> p (b t) d", p=P)).then_inc(F.sem("x_in"), 16)
            sp.dma_start(m.const[:], const).then_inc(F.sem("params"), 16)
            sp.dma_start(m.first_area, first).then_inc(F.sem("params"), 16)
            load_units(sp, U1, m.ring, lambda i: w_first[i])
            sp.wait_ge(*U1.given_back("out.1.1"))
            turns = moe_loads(sp, m, M, experts_landed, w_experts, F.at("passes"))
            sp.wait_ge(M["used"], turns * GROUPS_USED + SLOTS // 2)
            sp.sem_inc(first_layer["ring_free"], 1)
            with sp.Fori(0, LAYERS) as l:
                B, U, G = layer_parts(l)
                load_units(sp, U, m.ring, lambda i: w_layers[bass.ds(l, 1), i], G.at("ring_free", 0))
                close(G)
            G = layer_parts(LAYERS - 1)[2]
            sp.wait_ge(*G.at("f2.x", 2))
            sp.dma_start(out.rearrange("b (t p) d -> p (b t) d", p=P), m.x).then_inc(stored, 16)
            sp.wait_ge(stored, 16)

        @block.gpsimd
        def _(pool):
            first = Chain(pool, steps["pool"])
            first_pool(pool, first, m, B1, F)
            pool.wait_ge(*F.at("passes"))
            pool.dma_start(m.second_area, second).then_inc(table_loads, 16)
            pool.dma_start(m.normf, normf.to_broadcast([P, D])).then_inc(table_loads, 16)
            pool.dma_start(m.layer_area, layer[0]).then_inc(layer_loads, 16)
            pool.dma_start(m.post, post[0].to_broadcast([P, 2 * D])).then_inc(layer_loads, 16)
            pool.wait_ge(*first_layer.at("f2.pss", 2))
            root_of_mean(pool, first, m.ss, m.c["eps"][:, 0:2], m.half[:, 0:2], first_layer["f2.prstd"])
            pool.wait_ge(table_loads, 32)
            with pool.Fori(0, LAYERS) as l:
                B, U, G = layer_parts(l)
                pool.wait_ge(*G.at("f2.x", 0))
                pool.dma_start(m.post2, post2[bass.ds(l, 1)].squeeze(0).to_broadcast([P, D])).then_inc(post2_loads, 16)

                def load_next():
                    pool.dma_start(m.layer_area, layer[bass.ds(l + 1, 1)].squeeze(0)).then_inc(layer_loads, 16)
                    pool.dma_start(m.post, post[bass.ds(l + 1, 1)].squeeze(0).to_broadcast([P, 2 * D])).then_inc(layer_loads, 16)

                step = Chain(pool, steps["pool"], first.n, POOL_STEPS, l)
                layer_pool(pool, m, B, G, step, load_next)
                assert step.n == POOL_STEPS, step.n
                close(G)
            pool.wait_ge(layer_loads, (LAYERS + 1) * 32)

        @block.scalar
        def _(act):
            first = Chain(act, steps["act"])
            first_scalar(act, first, m, ps, B1, F)
            act.wait_ge(*F.at("passes"))
            moe_scalar(act, m, ps, M)
            act.wait_ge(*N.at("moe"))
            square_sums(act, m.x, m.xn, m.ss, lambda: first_layer["f2.pss"])
            with act.Fori(0, LAYERS) as l:
                B, U, G = layer_parts(l)
                step = Chain(act, steps["act"], first.n, ACT_STEPS, l)
                act.wait_ge(layer_loads, l * 32 + 32)
                ffn_scalar(act, step, m, ps, B, U, G, "f1", m.lp["gpre1"])
                mix_scalar(act, step, m, ps, B, U, G)
                ffn_scalar(act, step, m, ps, B, U, G, "f2", m.lp["gpre2"])
                assert step.n == ACT_STEPS, step.n
                close(G)

        @block.vector
        def _(dve):
            first = Chain(dve, steps["dve"])
            first_vector(dve, first, m, ps, B1, F)
            dve.wait_ge(*F.at("passes"))
            moe_vector(dve, m, ps, M)
            end = dve.value_load(m.r.turns_i[0:1, 1:2], min_val=PAIRS, max_val=PAIRS * PASSES)
            dve.wait_ge(M["added"], since(end * 4))
            dve.memset(m.r.best, 0.0).then_inc(N["moe"], 1)
            dve.wait_ge(*first_layer.at("f2.prstd"))
            dve.wait_ge(table_loads, 32)
            for t in range(TT):
                dve.scalar_tensor_tensor(out=m.x[:, t, :], in0=m.x[:, t, :], scalar=m.ss[:, t:t + 1],
                                         in1=m.normf, op0=ALU.mult, op1=ALU.mult).then_inc(first_layer["f2.x"], 1)
            with dve.Fori(0, LAYERS) as l:
                B, U, G = layer_parts(l)
                step = Chain(dve, steps["dve"], first.n, DVE_STEPS, l)
                dve.wait_ge(layer_loads, l * 32 + 32)
                ffn_vector(dve, step, m, ps, B, U, G, "f1", m.lp["gpre1"], m.post[:, 0:D])
                mix_vector(dve, step, m, ps, B, U, G)
                ffn_vector(dve, step, m, ps, B, U, G, "f2", m.lp["gpre2"], m.post2, (post2_loads, l * 16 + 16))
                assert step.n == DVE_STEPS, step.n
                close(G)

        @block.tensor
        def _(pe):
            first_tensor(pe, m, ps, B1, U1, F)
            pe.wait_ge(*F.at("passes"))
            moe_tensor(pe, m, ps, M, experts_landed)
            with pe.Fori(0, LAYERS) as l:
                B, U, G = layer_parts(l)
                pe.wait_ge(layer_loads, l * 32 + 32)
                ffn_tensor(pe, m, ps, B, U, G, "f1")
                mix_tensor(pe, m, ps, B, U, G)
                ffn_tensor(pe, m, ps, B, U, G, "f2")
                close(G)
        F.settle()
        N.settle()
        assert first_layer.raised == LAYER_BEFORE, first_layer.raised
        for n, k in raised.items():
            assert k == LAYER_PER.get(n, 1), (n, k)


def bucket(dist):
    exact, far = 16, 128
    d = np.maximum(dist, 1).astype(np.float32)
    large = exact + (np.log(d / np.float32(exact)) / np.float32(math.log(far / exact)) * 16).astype(np.int32)
    return np.where(dist < exact, dist, np.minimum(large, 31))


def cols(v):
    return np.ascontiguousarray(v).reshape(-1, P).T


def rows(v):
    return np.broadcast_to(np.ascontiguousarray(v).reshape(1, -1), (P, v.size))


def on_few(v):
    out = np.zeros((P, 1), v.dtype)
    out[:v.size, 0] = v.reshape(-1)
    return out


def pack(table, parts):
    for name, n in table:
        assert parts[name].shape == (P, n), (name, parts[name].shape)
    return np.concatenate([parts[name] for name, _ in table], axis=1)


def column_units(w, n=256):
    k = w.shape[0] // P
    return w.reshape(k, P, w.shape[1] // n, n).transpose(2, 1, 0, 3).reshape(-1, P, k * n)


def row_unit_pairs(w):
    return w.reshape(2, 4, P, w.shape[1] // 512, 512).transpose(3, 0, 2, 1, 4).reshape(-1, P, UNIT)


def deep_units(w):
    return w.reshape(-1, 2, P, D).transpose(0, 2, 1, 3).reshape(-1, P, UNIT)


def masked_bias(table, dist, keep):
    b = table[bucket(np.maximum(dist, 0))].transpose(0, 2, 1).copy()
    b[np.broadcast_to(~keep[:, None, :], b.shape)] = NEG
    return b.astype(np.float32)


def kernel(**inputs):
    import concourse.bacc as bacc
    from concourse.bass_utils import run_bass_kernel_spmd as run

    a = {k: np.asarray(v) for k, v in inputs.items()}
    q, k = np.arange(P), np.arange(T)
    arrays = {"x": a["x"]}

    ident = np.eye(P, dtype=np.float32)
    arrays["const"] = pack(CONST, {
        "ident": ident, "mask": np.where(q[:, None] <= q[None, :], 0, NEG).astype(np.float32),
        "ones": np.ones((P, T), np.float32), "before": (q[:, None] < q[None, :]).astype(np.float32),
        "slot": rows(np.tile(np.arange(CAP, dtype=np.float32), 2)),
        "eps": np.full((P, 8), EPS, np.float32),
        "prior4": rows(np.arange(4, 0, -1, dtype=np.float32)), "prior8": rows(np.arange(8, 0, -1, dtype=np.float32))})

    dist = k[:, None] - k[None, :]
    bias1 = masked_bias(a["rel_bias"], dist, dist >= 0)
    wr = np.concatenate([a["w_rg"][0], a["w_re"][0].reshape(D, EXPERTS)], axis=1)
    arrays["first"] = pack(FIRST, {
        "g1": cols(a["norm1_g"]), "g2": cols(a["norm2_g"]),
        "convw": a["conv_w"][0].reshape(4, 4, P).transpose(2, 1, 0).reshape(P, 16), "convb": cols(a["conv_b"]),
        "mnorm": cols(a["m_norm_g"]), "mskip": cols(a["m_skip"]),
        "wgate": a["w_mgate"][0].reshape(12, P, 8).transpose(1, 0, 2).reshape(P, 96),
        "bi": on_few(a["b_mgate"][0, :4]), "bf": on_few(a["b_mgate"][0, 4:]), "lam": rows(a["lambda_qk"]),
        "danorm": cols(a["da_norm_g"]), "wroute": wr.reshape(KT, P, 36).transpose(1, 0, 2).reshape(P, KT * 36),
        "broute": rows(np.concatenate([a["b_rg"].ravel(), a["b_re"].ravel()])),
        "wmq": a["w_mq"][0].transpose(1, 0, 2).reshape(P, 512), "wmk": a["w_mk"][0].transpose(1, 0, 2).reshape(P, 512),
        "bias": np.concatenate([bias1[:P, :, :P].reshape(P, -1), bias1[P:].reshape(P, -1)], axis=1)})

    log_g = np.log(1.0 - 2.0 ** (-5.0 - np.arange(RET_H)))
    lag = q[None, :] - q[:, None]
    blocks = [np.where(lag >= 0, np.exp(np.maximum(lag, 0) * g), 0) for g in log_g]
    decay = np.stack([np.concatenate([b, np.exp((lag + P) * g), b], axis=1) for b, g in zip(blocks, log_g)], axis=1)
    inv = (1.0 / (np.float32(10000.0) ** (np.arange(0, 128, 2, dtype=np.float32) / np.float32(128)))).astype(np.float32)
    ang = k.astype(np.float32)[:, None] * inv[None, :]
    band = q[:, None] + P - k[None, :]
    arrays["second"] = pack(SECOND, {
        "decay": decay.reshape(P, -1).astype(np.float32),
        "cos": np.cos(ang).reshape(TT, P, 64).transpose(1, 0, 2).reshape(P, -1).astype(np.float32),
        "sin": np.sin(ang).reshape(TT, P, 64).transpose(1, 0, 2).reshape(P, -1).astype(np.float32),
        "bias": masked_bias(a["rel_bias_2"], band, (band >= 0) & (band < P)).reshape(P, -1)})

    perm = np.arange(D).reshape(2, 8, ATT_D).transpose(1, 0, 2).ravel()
    layers, weights = [], []
    for l in range(LAYERS):
        layers.append(pack(LAYER, {
            "gpre1": cols(a["ffn1_pre_g_2"][l]), "gmix": cols(a["mix_pre_g_2"][l]), "gpre2": cols(a["ffn2_pre_g_2"][l]),
            "convw": a["conv_w_2"][l].reshape(4, CONV_T, P).transpose(2, 1, 0).reshape(P, -1),
            "convb": cols(a["conv_b_2"][l]),
            "wdt": a["w_in_2"][l][:, 2560:2576].reshape(KT, P, 16).transpose(1, 0, 2).reshape(P, -1),
            "gssd": cols(a["ssd_norm_g_2"][l]), "gret": cols(a["ret_gn_g_2"][l]), "bgate": cols(a["b_gate_2"][l]),
            "dtbias": on_few(a["dt_bias_2"][l]), "alog": on_few(a["a_log_2"][l]),
            "dskip": cols(np.repeat(a["d_skip_2"][l], 64)), "sinks": rows(a["attn_sinks_2"][l])}))
        w = a["w_in_2"][l]
        z, xbc, rq, rk, rv, rg, aq, akv, gate = (w[:, i:j] for i, j in (
            (0, 1024), (1024, 2560), (2576, 3088), (3088, 3600), (3600, 4624), (4624, 5648), (5648, 6672),
            (6672, 6928), (6928, 10000)))

        def gated(w_in):
            return column_units(w_in.reshape(D, 2, FT, P).transpose(0, 2, 1, 3).reshape(D, 2 * FF))

        branch = a["w_branch_2"][l]
        pairs = []
        for b in range(3):
            pairs += [column_units(gate[:, b * D:(b + 1) * D]), column_units(branch[b] if b < 2 else branch[b][perm])]
        weights.append(np.concatenate(
            [gated(a["w_ffn1_in_2"][l]), deep_units(a["w_ffn1_out_2"][l])]
            + [row_unit_pairs(v) for v in (rq, rk, rv, rg)]
            + [column_units(v) for v in (xbc, z, aq[:, perm[:768]], akv, aq[:, perm[768:]])] + pairs
            + [row_unit_pairs(a["w_out_2"][l]), gated(a["w_ffn2_in_2"][l]), deep_units(a["w_ffn2_out_2"][l])], axis=0))
    arrays["layer"] = np.stack(layers + layers[-1:])
    arrays["w_layers"] = np.stack(weights)
    gains = [np.concatenate([a["ffn1_post_g_2"][l], a["mix_post_g_2"][l]]) for l in range(LAYERS)]
    arrays["post"] = np.stack(gains + gains[-1:]).reshape(LAYERS + 1, 1, 2 * D)
    arrays["post2"] = a["ffn2_post_g_2"].reshape(LAYERS, 1, D)
    arrays["normf"] = a["normf_g"].reshape(1, D)

    c, v, z, qd, kd, vd = (a["w_in"][0][:, i * 512:(i + 1) * 512] for i in range(6))
    arrays["w_first"] = np.concatenate([column_units(w) for w in (c, v, qd, kd, vd, z)]
                                       + [row_unit_pairs(a["w_out"][0])], axis=0)
    up = [a[n][0].reshape(PAIRS, 2, 2, 4, P, FE).transpose(0, 2, 1, 4, 3, 5).reshape(PAIRS, 4, P, UNIT)
          for n in ("w_eg", "w_eu")]
    down = a["w_ed"][0].reshape(PAIRS, 2, 2, 2, P, D).transpose(0, 2, 1, 4, 3, 5).reshape(PAIRS, 4, P, UNIT)
    arrays["w_experts"] = np.concatenate(up + [down], axis=1)

    nc = bacc.Bacc("TRN2", target_bir_lowering=False, num_devices=1)
    order = ("x", "const", "first", "second", "layer", "post", "post2", "normf", "w_first", "w_experts", "w_layers")
    feed, args = {}, []
    for name in order:
        v = np.ascontiguousarray(arrays[name])
        feed[f"in_{name}"] = v
        args.append(nc.dram_tensor(f"in_{name}", v.shape, mybir.dt.from_np(v.dtype), kind="ExternalInput").ap())
    args.append(nc.dram_tensor("out", (1, T, D), F32, kind="ExternalOutput").ap())
    build(nc, *args)
    return run(nc, [feed], core_ids=[0]).results[0]["out"]
```
